# Optimizing a Trainium2 kernel written in Bass

```python
import jax, jax.numpy as jnp
from jax import lax
import numpy as np

D_MODEL = 1024
BATCH = 1
SEQ = 512
DEPTH = 2
DEC_BATCH = 8
DEC_SEQ = 4
PAST_LEN = 4096
PAGE_SIZE = 128

N_MIXERS = 2
N_POOL_LAYERS = (DEPTH + N_MIXERS - 1) // N_MIXERS
N_LRU_LAYERS = DEPTH // N_MIXERS
POOL_GROUPS = 4
POOL_WINDOWS = (2, 4, 8, 16)
POOL_GW = D_MODEL // POOL_GROUPS
POOL_BUF = max(POOL_WINDOWS) - 1
LRU_WIDTH = D_MODEL
LRU_BLOCKS = 4
LRU_BW = LRU_WIDTH // LRU_BLOCKS
CONV_WIDTH = 4
LRU_C = 8.0
N_EXPERTS = 16
N_EXPERT_GROUPS = 4
EXPERTS_PER_GROUP = N_EXPERTS // N_EXPERT_GROUPS
TOP_K = 2
D_FF = 512
EPS = 1e-6

kernel_name = "hybrid_pool_rglru_shared_router_moe_adaln_step"

def rmsnorm(x, g):
    x32 = x.astype(jnp.float32)
    y = x32 * lax.rsqrt(jnp.mean(x32 * x32, axis=-1, keepdims=True) + EPS)
    return (y * g.astype(jnp.float32)).astype(x.dtype)

def modulate(x, g, shift, scale):
    return rmsnorm(x, g) * (1 + scale[:, None, :]) + shift[:, None, :]

def pool_mixer(h, buf, start, w_pool, scale):
    B, S, D = h.shape
    xp = jnp.concatenate([buf.astype(h.dtype), h], axis=1)
    xp32 = xp.astype(jnp.float32)
    cs = jnp.concatenate([jnp.zeros((B, 1, D), jnp.float32), jnp.cumsum(xp32, axis=1)], axis=1)
    off = POOL_BUF
    pos = start + jnp.arange(S)
    end = cs[:, off + 1: off + 1 + S]
    parts = []
    for g, w in enumerate(POOL_WINDOWS):
        sl = slice(g * POOL_GW, (g + 1) * POOL_GW)
        begin = cs[:, off + 1 - w: off + 1 - w + S, sl]
        cnt = jnp.minimum(pos + 1, w).astype(jnp.float32)[None, :, None]
        parts.append((end[..., sl] - begin) / cnt)
    pooled = jnp.concatenate(parts, axis=-1) - xp32[:, off:]
    pooled = pooled.astype(h.dtype).reshape(B, S, POOL_GROUPS, POOL_GW)
    mixed = jnp.einsum('bsgc,gcd->bsgd', pooled, w_pool).reshape(B, S, D)
    new_buf = xp[:, -POOL_BUF:]
    return mixed * scale, new_buf

def _lin_comb(left, right):
    al, bl = left
    ar, br = right
    return (al * ar, ar * bl + br)

def recurrent_block(h, conv_buf, h0, start, w_x, b_x, w_y, b_y, cw, cb, w_a, b_a, w_i, b_i, lam, w_out, b_out):
    B, S, _ = h.shape
    xb = h @ w_x + b_x
    yb = jax.nn.gelu(h @ w_y + b_y)
    xp = jnp.concatenate([conv_buf.astype(xb.dtype), xb], axis=1)
    xc = xp[:, 0:S] * cw[0]
    for k in range(1, CONV_WIDTH):
        xc = xc + xp[:, k:k + S] * cw[k]
    xc = xc + cb
    new_conv = xp[:, -(CONV_WIDTH - 1):]
    xblk = xc.reshape(B, S, LRU_BLOCKS, LRU_BW)
    r = jax.nn.sigmoid((jnp.einsum('bsnc,ncd->bsnd', xblk, w_a).reshape(B, S, LRU_WIDTH) + b_a).astype(jnp.float32))
    i = jax.nn.sigmoid((jnp.einsum('bsnc,ncd->bsnd', xblk, w_i).reshape(B, S, LRU_WIDTH) + b_i).astype(jnp.float32))
    log_a = -LRU_C * r * jax.nn.softplus(-lam.astype(jnp.float32))
    a = jnp.exp(log_a)
    mult = jnp.sqrt(jnp.maximum(1.0 - jnp.exp(2.0 * log_a), 0.0))
    pos = start + jnp.arange(S)
    mult = jnp.where((pos == 0)[None, :, None], 1.0, mult)
    b = xc.astype(jnp.float32) * i * mult
    b = b.at[:, 0].add(a[:, 0] * h0.astype(jnp.float32))
    _, hs = lax.associative_scan(_lin_comb, (a, b), axis=1)
    y = (hs.astype(h.dtype) * yb) @ w_out + b_out
    return y, new_conv, hs[:, -1].astype(h.dtype)

def moe(h, router_w, router_b, w_gate, w_up, w_down):
    B, S, D = h.shape
    t = h.reshape(-1, D)
    logits = t.astype(jnp.float32) @ router_w.astype(jnp.float32)
    scores = jax.nn.softmax(logits, axis=-1)
    sel = scores + router_b.astype(jnp.float32)
    gscore = lax.top_k(sel.reshape(-1, N_EXPERT_GROUPS, EXPERTS_PER_GROUP), TOP_K)[0].sum(-1)
    best = jnp.argmax(gscore, axis=-1)
    expert_group = jnp.arange(N_EXPERTS) // EXPERTS_PER_GROUP
    masked = jnp.where(expert_group[None, :] == best[:, None], sel, -jnp.inf)
    _, idx = lax.top_k(masked, TOP_K)
    wts = jnp.take_along_axis(scores, idx, axis=-1)
    wts = wts / jnp.sum(wts, axis=-1, keepdims=True)
    gates = jnp.sum(jax.nn.one_hot(idx, N_EXPERTS, dtype=jnp.float32) * wts[..., None], axis=1)
    hg = jnp.einsum('td,edf->tef', t, w_gate)
    hu = jnp.einsum('td,edf->tef', t, w_up)
    hid = jax.nn.silu(hg) * hu * gates[..., None].astype(t.dtype)
    out = jnp.einsum('tef,efd->td', hid, w_down)
    return out.reshape(B, S, D)

def trunk(x, c, start, pool_bufs, conv_bufs, lru_hs, w_mod, b_mod, norm_g, pool_w, pool_scale,
          lru_w_x, lru_b_x, lru_w_y, lru_b_y, conv_w, conv_b, lru_w_a, lru_b_a, lru_w_i, lru_b_i,
          lru_lambda, lru_w_out, lru_b_out, router_w, router_b, moe_w_gate, moe_w_up, moe_w_down, final_g):
    new_pool, new_conv, new_h = [], [], []
    cs = jax.nn.silu(c)
    for i in range(DEPTH):
        mod = cs @ w_mod[i] + b_mod[i]
        sh1, sc1, g1, sh2, sc2, g2 = jnp.split(mod, 6, axis=-1)
        h = modulate(x, norm_g[i, 0], sh1, sc1)
        j = i // N_MIXERS
        if i % N_MIXERS == 0:
            mix, nb = pool_mixer(h, pool_bufs[j], start, pool_w[j], pool_scale[j])
            new_pool.append(nb)
        else:
            mix, nc, nh = recurrent_block(h, conv_bufs[j], lru_hs[j], start,
                                          lru_w_x[j], lru_b_x[j], lru_w_y[j], lru_b_y[j],
                                          conv_w[j], conv_b[j], lru_w_a[j], lru_b_a[j],
                                          lru_w_i[j], lru_b_i[j], lru_lambda[j],
                                          lru_w_out[j], lru_b_out[j])
            new_conv.append(nc)
            new_h.append(nh)
        x = x + g1[:, None, :] * mix
        h2 = modulate(x, norm_g[i, 1], sh2, sc2)
        x = x + g2[:, None, :] * moe(h2, router_w, router_b, moe_w_gate[i], moe_w_up[i], moe_w_down[i])
    y = rmsnorm(x, final_g)
    return y, jnp.stack(new_pool), jnp.stack(new_conv), jnp.stack(new_h)

def setup_inputs(seed: int = 0) -> dict:
    key = jax.random.key(seed)
    ks = jax.random.split(key, 32)
    f = jnp.float32
    D, W, E, F = D_MODEL, LRU_WIDTH, N_EXPERTS, D_FF
    nrm = lambda k, s, sc: jax.random.normal(k, s, f) * sc
    u = jax.random.uniform(ks[24], (N_LRU_LAYERS, W), f, 0.9, 0.999)
    p = u ** (1.0 / LRU_C)
    lam = jnp.log(p) - jnp.log1p(-p)
    return {
        "x_prompt": nrm(ks[0], (BATCH, SEQ, D), 1.0),
        "x_sample": nrm(ks[1], (DEC_BATCH, DEC_SEQ, D), 1.0),
        "c_prompt": nrm(ks[2], (BATCH, D), 1.0),
        "c_sample": nrm(ks[3], (DEC_BATCH, D), 1.0),
        "state_pool_buf": nrm(ks[4], (N_POOL_LAYERS, DEC_BATCH, POOL_BUF, D), 1.0),
        "state_conv_buf": nrm(ks[5], (N_LRU_LAYERS, DEC_BATCH, CONV_WIDTH - 1, W), 1.0),
        "state_lru_h": nrm(ks[6], (N_LRU_LAYERS, DEC_BATCH, W), 0.5),
        "w_mod": nrm(ks[7], (DEPTH, D, 6 * D), 0.5 * D ** -0.5),
        "b_mod": nrm(ks[8], (DEPTH, 6 * D), 0.02),
        "norm_g": 1.0 + nrm(ks[9], (DEPTH, 2, D), 0.1),
        "pool_w": nrm(ks[10], (N_POOL_LAYERS, POOL_GROUPS, POOL_GW, POOL_GW), POOL_GW ** -0.5),
        "pool_scale": 1.0 + nrm(ks[11], (N_POOL_LAYERS, D), 0.1),
        "lru_w_x": nrm(ks[12], (N_LRU_LAYERS, D, W), D ** -0.5),
        "lru_b_x": nrm(ks[13], (N_LRU_LAYERS, W), 0.02),
        "lru_w_y": nrm(ks[14], (N_LRU_LAYERS, D, W), D ** -0.5),
        "lru_b_y": nrm(ks[15], (N_LRU_LAYERS, W), 0.02),
        "conv_w": nrm(ks[16], (N_LRU_LAYERS, CONV_WIDTH, W), CONV_WIDTH ** -0.5),
        "conv_b": nrm(ks[17], (N_LRU_LAYERS, W), 0.02),
        "lru_w_a": nrm(ks[18], (N_LRU_LAYERS, LRU_BLOCKS, LRU_BW, LRU_BW), LRU_BW ** -0.5),
        "lru_b_a": nrm(ks[19], (N_LRU_LAYERS, W), 0.02),
        "lru_w_i": nrm(ks[20], (N_LRU_LAYERS, LRU_BLOCKS, LRU_BW, LRU_BW), LRU_BW ** -0.5),
        "lru_b_i": nrm(ks[21], (N_LRU_LAYERS, W), 0.02),
        "lru_lambda": lam,
        "lru_w_out": nrm(ks[22], (N_LRU_LAYERS, W, D), W ** -0.5),
        "lru_b_out": nrm(ks[23], (N_LRU_LAYERS, D), 0.02),
        "router_w": nrm(ks[25], (D, E), D ** -0.5),
        "router_b": nrm(ks[26], (E,), 0.01),
        "moe_w_gate": nrm(ks[27], (DEPTH, E, D, F), D ** -0.5),
        "moe_w_up": nrm(ks[28], (DEPTH, E, D, F), D ** -0.5),
        "moe_w_down": nrm(ks[29], (DEPTH, E, F, D), F ** -0.5),
        "final_g": 1.0 + nrm(ks[30], (D,), 0.1),
    }

def reference(x_prompt, x_sample, c_prompt, c_sample, state_pool_buf, state_conv_buf, state_lru_h,
              w_mod, b_mod, norm_g, pool_w, pool_scale, lru_w_x, lru_b_x, lru_w_y, lru_b_y,
              conv_w, conv_b, lru_w_a, lru_b_a, lru_w_i, lru_b_i, lru_lambda, lru_w_out, lru_b_out,
              router_w, router_b, moe_w_gate, moe_w_up, moe_w_down, final_g):
    bp = x_prompt.shape[0]
    dt = x_prompt.dtype
    pool0 = jnp.zeros((N_POOL_LAYERS, bp, POOL_BUF, D_MODEL), dt)
    conv0 = jnp.zeros((N_LRU_LAYERS, bp, CONV_WIDTH - 1, LRU_WIDTH), dt)
    h0 = jnp.zeros((N_LRU_LAYERS, bp, LRU_WIDTH), dt)
    y_prompt, new_pool_prompt, new_conv_prompt, new_h_prompt = trunk(
        x_prompt, c_prompt, 0, pool0, conv0, h0, w_mod, b_mod, norm_g, pool_w, pool_scale,
        lru_w_x, lru_b_x, lru_w_y, lru_b_y, conv_w, conv_b, lru_w_a, lru_b_a, lru_w_i, lru_b_i,
        lru_lambda, lru_w_out, lru_b_out, router_w, router_b, moe_w_gate, moe_w_up, moe_w_down, final_g)
    y_sample, new_pool_sample, new_conv_sample, new_h_sample = trunk(
        x_sample, c_sample, PAST_LEN, state_pool_buf, state_conv_buf, state_lru_h,
        w_mod, b_mod, norm_g, pool_w, pool_scale,
        lru_w_x, lru_b_x, lru_w_y, lru_b_y, conv_w, conv_b, lru_w_a, lru_b_a, lru_w_i, lru_b_i,
        lru_lambda, lru_w_out, lru_b_out, router_w, router_b, moe_w_gate, moe_w_up, moe_w_down, final_g)
    return (y_prompt, y_sample, new_pool_prompt, new_pool_sample, new_conv_prompt, new_conv_sample, new_h_prompt, new_h_sample)


_drawn_inputs = setup_inputs


def setup_inputs(seed=0):
    import zlib

    import numpy as np

    out = dict(_drawn_inputs(seed))
    spreads = {}
    factors = {'lru_b_y': 4.031, 'lru_b_a': 8.0, 'lru_b_i': 6.081, 'lru_b_out': 3.774}
    for name, (base, spread) in spreads.items():
        noise = np.random.default_rng([zlib.crc32(name.encode()), seed]).standard_normal(out[name].shape)
        drawn = base * np.exp(spread * noise) if base else spread * noise
        out[name] = __import__('jax').numpy.asarray(drawn.astype(out[name].dtype))
    for name, factor in factors.items():
        out[name] = (out[name] * factor).astype(out[name].dtype)
    return out
```

```python
from contextlib import ExitStack

import concourse.bass as bass
from concourse import mybir

P = 128
ALU = mybir.AluOpType
ACT = mybir.ActivationFunctionType
F32 = mybir.dt.float32
BF16 = mybir.dt.bfloat16
I32 = mybir.dt.int32
AX = mybir.AxisListType.X

POOL_WINDOWS = (2, 4, 8, 16)
LRU_C = 8.0
EPS = 1e-6
BIG = 1e30
GELU = ACT.Gelu_apprx_tanh


def hybrid_trunk_kernel(nc, x_prompt, x_sample, c_prompt, c_sample, state_pool_buf, state_conv_buf, state_lru_h,
                        w_mod, b_mod, norm_g, pool_w, pool_scale, lru_w_x, lru_b_x, lru_w_y, lru_b_y,
                        conv_w, conv_b, lru_w_a, lru_b_a, lru_w_i, lru_b_i, lru_lambda, lru_w_out, lru_b_out,
                        router_w, router_b, moe_w_gate, moe_w_up, moe_w_down, final_g,
                        y_prompt, y_sample, new_pool_prompt, new_pool_sample, new_conv_prompt, new_conv_sample,
                        new_h_prompt, new_h_sample):
    _, S, D = x_prompt.shape
    NB, SS, _ = x_sample.shape
    NS = NB * SS
    T = S + NS
    DC = D // P
    NQ = 1 + NB
    DEPTH = w_mod.shape[0]
    NM = 6 * DC
    PB = state_pool_buf.shape[2]
    CW = conv_w.shape[1]
    CH = CW - 1
    NE, F = moe_w_gate.shape[1], moe_w_gate.shape[3]
    FC = F // P
    NG = 4
    EG = NE // NG
    HALF = 512
    NT = (T + P - 1) // P
    TW = [min(P, T - j * P) for j in range(NT)]
    NPT = S // P
    NOV = (2 * T - NE) // P
    NL = NE + NOV
    RING = 6
    UNIT = DC * HALF
    assert UNIT == FC * D and D == 2 * HALF and S == HALF and F == HALF
    MOD_ROT = w_mod.shape[2] // HALF // RING
    NOWHERE = 4000

    with ExitStack() as ctx:
        def sb(name, shape, dt=F32):
            return ctx.enter_context(nc.sbuf_tensor(name, shape, dt))

        def sem(name):
            return ctx.enter_context(nc.semaphore(name))

        WORK = 18392
        ring = [sb(f"ring{i}", [P, UNIT]) for i in range(RING)]
        xT = sb("xT", [P, DC, T])
        hT = sb("hT", [P, DC, T])
        work = sb("work", [P, WORK])
        modT = sb("modT", [P, NM, NQ])
        gainT = sb("gainT", [P, DEPTH, 2, DC, NQ])
        shiftT = sb("shiftT", [P, DEPTH, 2, DC, NQ])
        gateT = sb("gateT", [P, DEPTH, 2, DC, NQ])
        gbT = sb("gbT", [P, DC, NQ])
        bmodT = sb("bmodT", [P, DEPTH * NM])
        VEC = ["norm_g0", "norm_g1", "norm_g2", "norm_g3", "pool_scale", "final_g", "b_x", "b_y",
               "cw0", "cw1", "cw2", "cw3", "conv_b", "b_a", "b_i"]
        vecT = sb("vecT", [P, (len(VEC) + 2) * DC])
        rw = sb("rw", [P, DC, NE])
        rb = sb("rb", [P, NE])
        ident = sb("ident", [P, P])
        mean_w = sb("mean_w", [P, P])
        ones_b = sb("ones_b", [P, P], BF16)
        before_b = sb("before_b", [P, P], BF16)
        iota_e = sb("iota_e", [P, NE])
        iota_y = sb("iota_y", [P, 2 * NT], I32)
        valid = sb("valid", [P, NT])
        invcnt = sb("invcnt", [P, 16])
        scT = sb("scT", [P, DC, NQ])
        poolT = work[:, 13312:13312 + DC * NB * PB].rearrange("p (c r) -> p c r", c=DC)
        rstd = work[:, WORK - T:WORK]
        convT = sb("convT", [P, DC, NB * CH])
        h0T = sb("h0T", [P, DC, NB])
        kdec = sb("kdec", [P, 2, DC])
        half_b = sb("half_b", [P, 2, DC])
        small = sb("small", [P, DC * NS])
        small2 = sb("small2", [P, DC * NS])
        nowhere = sb("nowhere", [P, NL], I32)
        wts = sb("wts", [P, 2, NT])
        tokl = sb("tokl", [P, NL], I32)
        yrow = sb("yrow", [P, NL], I32)
        toks = [sb(f"toks{b}", [P, 1], I32) for b in range(2)]
        yrows = [sb(f"yrows{b}", [P, 1], I32) for b in range(2)]
        consts = sb("consts", [P, 2])
        conv_tail = sb("conv_tail", [P, DC, CH * NQ])
        h_tail = sb("h_tail", [P, DC, NQ])
        picks = sb("picks", [P, NT, NE], BF16)
        ovinfo = sb("ovinfo", [1, NOV + 1], I32)

        bank = [ctx.enter_context(nc.psum_tensor(f"bank{i}", [P, HALF], F32)) for i in range(8)]

        def vec(name, c=None):
            n = VEC.index(name) if name in VEC else {"lam": len(VEC), "b_out": len(VEC) + 1}[name]
            return vecT[:, n * DC:(n + 1) * DC] if c is None else vecT[:, n * DC + c:n * DC + c + 1]

        def area(at, n):
            return work[:, at:at + n], at + n

        xtok, at = area(0, NPT * D)
        xtok = xtok.rearrange("p (j d) -> p j d", j=NPT)
        xtok_s, at = area(at, D)
        rows, at = area(at, 5 * P)
        rows = rows.rearrange("p (n d) -> p n d", n=5)
        st_rows, at = area(at, 3 * D)
        st_rows = st_rows.rearrange("p (n d) -> p n d", n=3)
        craw, at = area(at, NQ * DC)
        pooledT, at = area(0, DC * T)
        pooledT = pooledT.rearrange("p (c t) -> p c t", c=DC)
        pw, at = area(at, 2 * NG * 256)
        pw = pw.rearrange("p (g k n) -> p g k n", g=NG, k=2)
        psum_a, at = area(at, 2 * S)
        psum_b, at = area(at, 2 * S)
        psum_a, psum_b = [x.rearrange("p (c t) -> p c t", c=2) for x in (psum_a, psum_b)]
        sbuf_n = 2 * NB * (PB + SS)
        spool_a, at = area(at, sbuf_n)
        spool_b, at = area(at, sbuf_n)
        spool_a, spool_b = [x.rearrange("p (c b t) -> p c b t", c=2, b=NB) for x in (spool_a, spool_b)]
        tail_rows, at = area(at, 2 * D)
        tail_rows = tail_rows.rearrange("p (n d) -> p n d", n=2)
        assert at <= 13312
        at = 0
        xg, xe, sg, hid, hidT, ys = [], [], [], [], [], []
        for b in range(2):
            for lst, n in ((xg, D), (xe, D), (sg, F), (hid, F), (hidT, F), (ys, D)):
                v, at = area(at, n)
                lst.append(v)
        xe = [x.rearrange("p (c t) -> p c t", c=DC) for x in xe]
        hidT = [x.rearrange("p (c t) -> p c t", c=FC) for x in hidT]
        route, at = area(at, 24 * NT * NE)
        route = route.rearrange("p (n j e) -> p n j e", n=24, e=NE)
        lg, ex, sel, one, two, val_a, val_b = (route[:, n] for n in range(7))
        flat = route.rearrange("p n j e -> p (n j e)")
        gsc, gbest = (flat[:, n * NT * NE:n * NT * NE + NT * NG].rearrange("p (j g) -> p j g", g=NG) for n in (7, 8))
        tmp_b = flat[:, 9 * NT * NE:9 * NT * NE + 32]
        cnt_e, ov_e, cum_e = (flat[:, (10 + n) * NT * NE:(10 + n) * NT * NE + NE] for n in range(3))
        ov_f = flat[:, 13 * NT * NE:13 * NT * NE + NOV + 1]
        slot_i = flat[:, 14 * NT * NE:14 * NT * NE + 2 * NT].bitcast(I32)
        lt_f, lt_g = (flat[:, (15 + n) * NT * NE:(15 + n) * NT * NE + NL] for n in range(2))
        list_f = work[0:NL, at:at + P]
        list_i = work[0:NL, at + P:at + 2 * P].bitcast(I32)
        at += 2 * P
        htok = [ys[0], ys[1]]
        yl = [[xg[0], xe[0].rearrange("p c t -> p (c t)")], [xg[1], xe[1].rearrange("p c t -> p (c t)")]]
        ysum = [ys[0], ys[1]]
        assert at <= WORK
        at = 0
        xb, at = area(at, DC * (CH + S))
        xb = xb.rearrange("p (c t) -> p c t", c=DC)
        xcT, at = area(at, DC * T)
        ybT, at = area(at, DC * T)
        xcT, ybT = [x.rearrange("p (c t) -> p c t", c=DC) for x in (xcT, ybT)]
        xbs, at = area(at, DC * NB * (CH + SS))
        xbs = xbs.rearrange("p (c b t) -> p c b t", c=DC, b=NB)
        NBLK, BW = lru_w_a.shape[1], lru_w_a.shape[2]
        BC = BW // P
        wai, at = area(at, 2 * NBLK * BC * BW)
        wai = wai.rearrange("p (w g k n) -> p w g k n", w=2, g=NBLK, k=BC)
        tanh_i = []
        for b in range(2):
            v, at = area(at, S)
            tanh_i.append(v)
        assert at <= WORK, at
        def xcT_rows(n):
            return xcT.rearrange("p c t -> p (c t)")[:, n * D:(n + 1) * D]

        e2 = xb
        aT = hT

        h_rows = [nc.dram_tensor(f"h_rows{l}", [T, D], F32).ap() for l in range(DEPTH)]
        y_rows = [nc.dram_tensor(f"y_rows{l}", [2 * T, D], F32).ap() for l in range(DEPTH)]
        slots = [nc.dram_tensor(f"slots{l}", [NL * P, 1], I32).ap() for l in range(DEPTH)]

        slot_loaded = [sem(f"slot_loaded{i}") for i in range(RING)]
        gate_sem = sem("stage_gate")
        vec_step = sem("vec_step")
        act_step = sem("act_step")
        pool_step = sem("pool_step")
        in_loaded = sem("in_loaded")
        state_loaded = sem("state_loaded")
        small_loaded = sem("small_loaded")
        lists_filled = sem("lists_filled")
        blocks_loaded = sem("blocks_loaded")
        poolw_loaded = sem("poolw_loaded")
        stored = sem("stored")
        copied = sem("copied")
        turned = sem("turned")
        turned_out = sem("turned_out")
        mod_used = sem("mod_used")
        mod_done = sem("mod_done")
        silu_c = sem("silu_c")
        sq_ready = sem("sq_ready")
        mean_ready = sem("mean_ready")
        normed = sem("normed")
        pooled_ready = sem("pooled_ready")
        mixed = sem("mixed")
        mixed_added = sem("mixed_added")
        tail_turned = sem("tail_turned")
        x_done = sem("x_done")
        x_out = sem("x_out")
        lru_used = sem("lru_used")
        conv_done = sem("conv_done")
        sconv_done = sem("sconv_done")
        gates_done = sem("gates_done")
        a_ready = sem("a_ready")
        gates_read = sem("gates_read")
        mult_done = sem("mult_done")
        sgate_in = sem("sgate_in")
        stanh = sem("stanh")
        waits_seen = sem("waits_seen")
        std_ready = sem("std_ready")
        power_ready = sem("power_ready")
        root_ready = sem("root_ready")
        sdecay_in = sem("sdecay_in")
        sexp = sem("sexp")
        sgelu_in = sem("sgelu_in")
        sgelu = sem("sgelu")
        lam_exp = sem("lam_exp")
        x_added = sem("x_added")
        z_ready = sem("z_ready")
        o_done = sem("o_done")
        o_out = sem("o_out")
        o_added = sem("o_added")
        tails_ready = sem("tails_ready")
        yt_done = sem("yt_done")
        yt_out = sem("yt_out")
        yt_stored = [sem(f"yt_stored{b}") for b in range(2)]

        ROUTE = ["logits", "lmax", "ex", "count_in", "counts", "turn", "turn_out", "rows_stored0", "rows_stored1", "slots_ready",
                 "ids_stored", "list_loaded", "list_f", "list_t", "list_ready", "y_loaded0", "y_loaded1", "y_scaled",
                 "y_summed", "y_turned", "y_added"]
        TILE = ["toks_ready", "yrows_ready", "gathered0", "gathered1", "tx_done", "xe_copied", "g_done", "u_done", "silu_done",
                "hid_done", "th_done", "ht_copied", "y_done", "ys_copied", "scattered0", "scattered1"]
        rt = [{n: sem(f"r{l}_{n}") for n in ROUTE} for l in range(DEPTH)]
        ts = {n: sem(f"t_{n}") for n in TILE}
        ov = [{n: sem(f"o{l}_{n}") for n in TILE + ["loaded"]} for l in range(DEPTH)]

        block = ctx.enter_context(nc.Block())

        passed = {"pe": 0, "act": 0, "dve": 0, "pool": 0}

        def stage_end(eng, name):
            passed[name] += 1
            eng.drain().then_inc(gate_sem, 1)
            eng.wait_ge(gate_sem, 4 * passed[name])

        SMALL = ((b_mod.rearrange("l (r p) -> (l r) p", p=P), 0, 0), (norm_g.rearrange("l n (r p) -> (l n r) p", p=P), 1, 0),
                 (pool_scale, 1, 32), (final_g.rearrange("(o d) -> o d", o=1), 1, 40), (lru_b_x, 1, 48), (lru_b_y, 1, 56),
                 (conv_w[0], 1, 64), (conv_b, 2, 0), (lru_b_a, 2, 8), (lru_b_i, 2, 16), (lru_lambda, 2, 24),
                 (lru_b_out, 2, 32), (c_prompt, 3, 0), (c_sample, 3, DC))
        N_SMALL = len(SMALL) + 2

        def param_groups():
            return [[(rows[0:DEPTH * NM, 0, :], 0)], [(rows[0:96, 1, :], 0)], [(rows[0:40, 2, :], 0)],
                    [(rows[0:NQ * DC, 3, :], 0)]]

        def state_groups():
            def cut(n, h, c):
                return st_rows[0:h, n, c * P:(c + 1) * P]
            return [[(cut(0, NB * PB, c), (c % 4) * NB * PB) for c in range(4 * g, 4 * g + 4)] for g in range(2)] + [
                [(cut(1, NB * CH, c), c * NB * CH) for c in range(DC)], [(cut(2, NB, c), c * NB) for c in range(DC)]]

        def x_groups():
            return [[(xtok[:, j, c * P:(c + 1) * P], j * P) for j in range(NPT)] for c in range(DC)] + [
                [(xtok_s[0:NS, c * P:(c + 1) * P], c * NS) for c in range(DC)]]

        @block.sync
        def _(sp):
            rot = 0

            def wait_free(prev, s):
                if prev is None:
                    return
                kind, l = prev
                if kind == "mod":
                    sp.wait_ge(mod_used, RING * (MOD_ROT * (l + 1) - 1) + s + 1)
                elif kind == "moe":
                    b, part = s // 3, s % 3
                    name, n = (("g_done", 1), ("u_done", 1), ("y_done", 2))[part]
                    sp.wait_ge(ts[name], n * (NE * l + NE - 2 + b + 1))
                else:
                    sp.wait_ge(lru_used, s + 1)

            def load_mod(l, prev):
                src = w_mod[l].rearrange("(k p) n -> p k n", p=P)
                for r in range(MOD_ROT):
                    for s in range(RING):
                        if r == 0:
                            wait_free(prev, s)
                        else:
                            sp.wait_ge(mod_used, RING * (MOD_ROT * l + r - 1) + s + 1)
                        at = (r * RING + s) * HALF
                        sp.dma_start(ring[s][:, :].rearrange("p (k n) -> p k n", k=DC),
                                     src[:, :, at:at + HALF]).then_inc(slot_loaded[s], 16)

            def load_expert(l, e, b, loaded, wait):
                for part, w in enumerate((moe_w_gate, moe_w_up, moe_w_down)):
                    s = 3 * b + part
                    wait(s)
                    one = w[l][bass.ds(e, 1)]
                    src = one.rearrange("o (k p) n -> p (o k) n", p=P)
                    sp.dma_start(ring[s][:, :].rearrange("p (k n) -> p k n", k=src.shape[1]),
                                 src).then_inc(loaded(s), 16)

            def load_moe(l, prev):
                for b in range(2):
                    load_expert(l, b, b, lambda s: slot_loaded[s], lambda s: wait_free(prev, s))
                with sp.Fori(1, NE // 2) as it:
                    for b in range(2):
                        def used(s, b=b):
                            name, n = (("g_done", 1), ("u_done", 1), ("y_done", 2))[s % 3]
                            sp.wait_ge(ts[name], it * (2 * n) + n * (NE * l + b - 1))
                        load_expert(l, it * 2 + b, b, lambda s: slot_loaded[s], used)

            def load_overflow(l):
                sp.wait_ge(rt[l]["list_ready"], 2)
                n_ov = sp.value_load(ovinfo[0:1, NOV:NOV + 1], min_val=0, max_val=NOV)
                with sp.If(n_ov > 0):
                    sp.wait_ge(ts["y_done"], 2 * NE * (l + 1))
                    with sp.Fori(0, n_ov) as i:
                        e = sp.value_load(ovinfo[0:1, bass.ds(i, 1)], min_val=0, max_val=NE - 1)
                        load_expert(l, e, 0, lambda s: ov[l]["loaded"], lambda s: None)
                        sp.wait_ge(ov[l]["y_done"], (i + 1) * 2)
                        sp.sem_inc(waits_seen, 1)

            def load_lru(prev):
                s = 0
                for w in (lru_w_x, lru_w_y, lru_w_out):
                    for half in range(2):
                        wait_free(prev, s)
                        sp.dma_start(ring[s][:, :].rearrange("p (k n) -> p k n", k=DC),
                                     w[0].rearrange("(k p) n -> p k n", p=P)[:, :, half * HALF:(half + 1) * HALF]
                                     ).then_inc(slot_loaded[s], 16)
                        s += 1

            load_mod(0, None)
            sp.dma_start(new_pool_sample[0][:, 0:PB - SS, :], state_pool_buf[0][:, SS:PB, :]).then_inc(copied, 16)
            load_mod(1, ("mod", 0))
            load_moe(0, ("mod", 1))
            load_overflow(0)
            load_lru(("moe", 0))
            load_moe(1, ("lru", 0))
            load_overflow(1)
            sp.wait_ge(copied, 16)

        MOD0_ROT, MOD1_ROT, MOE0_ROT = 0, MOD_ROT, 2 * MOD_ROT
        LRU_ROT = MOE0_ROT + NE // 2
        MOE_ROT = [MOE0_ROT, LRU_ROT + 1]

        @block.tensor
        def _(pe):
            def turn_rows(groups, n):
                for bk, parts in groups:
                    if n >= 8:
                        pe.wait_ge(turned_out, n - 7)
                    for src, col in parts:
                        w = src.shape[0]
                        last = pe.transpose(bank[bk][:, col:col + w], src, ident[0:w, 0:w])
                    last.then_inc(turned, 1)
                    n += 1
                return n

            pe.wait_ge(pool_step, 3)
            pe.wait_ge(small_loaded, 16 * N_SMALL)
            n = turn_rows([(i, g) for i, g in enumerate(param_groups())], 0)
            pe.wait_ge(state_loaded, 16 * 3)
            n = turn_rows([((n + i) % 8, g) for i, g in enumerate(state_groups())], n)
            pe.wait_ge(in_loaded, 16 * 2)
            n = turn_rows([((n + i) % 8, g) for i, g in enumerate(x_groups())], n)
            stage_end(pe, "pe")

            def mod(l, rot0):
                if l == 0:
                    pe.wait_ge(silu_c, 1)
                with pe.Fori(0, MOD_ROT) as r:
                    for s in range(RING):
                        pe.wait_ge(slot_loaded[s], (r + (rot0 + 1)) * 16)
                        w = ring[s][:, :].rearrange("p (k n) -> p k n", k=DC)
                        for m in range(4):
                            for k in range(DC):
                                last = pe.matmul(bank[7][:, bass.ds(r * (RING * 4 * NQ) + (s * 4 + m) * NQ, NQ)],
                                                 w[:, k, m * P:(m + 1) * P], scT[:, k, :],
                                                 start=(k == 0), stop=(k == DC - 1))
                        last.then_inc(mod_used, 1)
                pe.drain().then_inc(mod_done, 1)

            def mean(n):
                for c in range(DC):
                    pe.wait_ge(sq_ready, n * DC + c + 1)
                    pe.matmul(bank[0][:, :], mean_w[:, :], hT[:, c, 0:S], start=(c == 0), stop=(c == DC - 1))
                    last = pe.matmul(bank[1][:, 0:NS], mean_w[:, :], hT[:, c, S:T], start=(c == 0), stop=(c == DC - 1))
                last.then_inc(mean_ready, 1)

            def tail(bk, srcs):
                for c in range(DC):
                    src = srcs(c)
                    w = src.shape[-1]
                    last = pe.transpose(bank[bk + c // 4][0:w, (c % 4) * P:(c % 4 + 1) * P], src, ident[:, :])
                last.then_inc(tail_turned, 1)

            def pool_mix():
                tail(4, lambda c: hT[:, c, S - PB:S])
                tail(6, lambda c: hT[:, c, S:T])
                pe.wait_ge(poolw_loaded, 16)
                for g in range(NG):
                    pe.wait_ge(pooled_ready, g + 1)
                    for m in range(2):
                        i = 2 * g + m
                        if i >= 2:
                            pe.wait_ge(mixed_added, i - 1)
                        for k in range(2):
                            pe.matmul(bank[i % 2][:, :], pw[:, g, k, m * P:(m + 1) * P], pooledT[:, 2 * g + k, 0:S],
                                      start=(k == 0), stop=(k == 1))
                        for k in range(2):
                            last = pe.matmul(bank[2][:, i * NS:(i + 1) * NS], pw[:, g, k, m * P:(m + 1) * P],
                                             pooledT[:, 2 * g + k, S:T], start=(k == 0), stop=(k == 1))
                        last.then_inc(mixed, 1)
                stage_end(pe, "pe")

            def tx(q, b, n, first, got):
                got(b)
                if not first:
                    pe.wait_ge(q["xe_copied"], n * 2)
                for c in range(DC):
                    last = pe.transpose(bank[4 + c // 4][:, (c % 4) * P:(c % 4 + 1) * P],
                                        xg[b][:, c * P:(c + 1) * P], ident[:, :])
                last.then_inc(q["tx_done"], 1)

            def tile(q, b, n, first, loaded, tx_next):
                pe.wait_ge(q["xe_copied"], n * 2 + 2)
                for part, (bk, done) in enumerate(((0, "g_done"), (1, "u_done"))):
                    loaded(3 * b + part)
                    if not first:
                        pe.wait_ge(q[("silu_done", "hid_done")[part]], n)
                    w = ring[3 * b + part][:, :].rearrange("p (k n) -> p k n", k=DC)
                    for k in range(DC):
                        last = pe.matmul(bank[bk][:, :], xe[b][:, k, :], w[:, k, :], start=(k == 0), stop=(k == DC - 1))
                    last.then_inc(q[done], 1)
                tx_next()
                pe.wait_ge(q["hid_done"], n + 1)
                if not first:
                    pe.wait_ge(q["ht_copied"], n * 2)
                for c in range(FC):
                    last = pe.transpose(bank[6 + c // 2][:, (c % 2) * P:(c % 2 + 1) * P], hid[b][:, c * P:(c + 1) * P], ident[:, :])
                last.then_inc(q["th_done"], 1)
                pe.wait_ge(q["ht_copied"], n * 2 + 2)
                loaded(3 * b + 2)
                if not first:
                    pe.wait_ge(q["ys_copied"], n * 2)
                w = ring[3 * b + 2][:, :].rearrange("p (k n) -> p k n", k=FC)
                for half in range(2):
                    for k in range(FC):
                        last = pe.matmul(bank[2 + half][:, :], hidT[b][:, k, :], w[:, k, half * HALF:(half + 1) * HALF],
                                         start=(k == 0), stop=(k == FC - 1))
                    last.then_inc(q["y_done"], 1)

            def moe(l):
                r, q = rt[l], ts
                for j in range(NT):
                    w = TW[j]
                    for c in range(DC):
                        last = pe.matmul(bank[2][0:w, j * NE:(j + 1) * NE], hT[:, c, j * P:j * P + w], rw[:, c, :],
                                         start=(c == 0), stop=(c == DC - 1))
                last.then_inc(r["logits"], 1)
                for j in range(NT):
                    w = TW[j]
                    for half in range(2):
                        i = 2 * j + half
                        if i >= 2:
                            pe.wait_ge(r["turn_out"], i - 1)
                        for c in range(4):
                            last = pe.transpose(bank[half][0:w, c * P:(c + 1) * P],
                                                hT[:, 4 * half + c, j * P:j * P + w], ident[:, :])
                        last.then_inc(r["turn"], 1)
                pe.wait_ge(r["count_in"], 1)
                for j in range(NT):
                    for i in range(j):
                        pe.matmul(bank[3][:, j * NE:(j + 1) * NE], ones_b[:, :], picks[:, i, :], start=(i == 0), stop=False)
                    pe.matmul(bank[3][:, j * NE:(j + 1) * NE], before_b[:, :], picks[:, j, :], start=(j == 0), stop=True)
                for i in range(NT):
                    last = pe.matmul(bank[3][:, NT * NE:(NT + 1) * NE], ones_b[:, :], picks[:, i, :],
                                     start=(i == 0), stop=(i == NT - 1))
                last.then_inc(r["counts"], 1)
                if l == 0:
                    mod(1, MOD1_ROT)
                pe.wait_ge(r["list_f"], 1)
                pe.transpose(bank[3][:, 0:NL], list_f, ident[0:NL, 0:NL]).then_inc(r["list_t"], 1)
                stage_end(pe, "pe")

                rot0 = MOE_ROT[l]

                def step(it, b, first=False, last=False):
                    t = it * 2 + (b + NE * l)

                    def loaded(s):
                        pe.wait_ge(slot_loaded[s], (it + (rot0 + 1)) * 16)

                    def tx_next():
                        if not last:
                            nb = 1 - b
                            nit = it + b
                            tx(q, nb, t + 1, False,
                               lambda _: pe.wait_ge(q[f"gathered{nb}"], (nit + (l * (NE // 2) + 1)) * 16))

                    tile(q, b, t, first, loaded, tx_next)

                tx(q, 0, l * NE, True, lambda _: pe.wait_ge(q["gathered0"], (l * (NE // 2) + 1) * 16))
                step(0, 0, first=True)
                step(0, 1)
                with pe.Fori(1, NE // 2 - 1) as it:
                    step(it, 0)
                    step(it, 1)
                step(NE // 2 - 1, 0)
                step(NE // 2 - 1, 1, last=True)
                o = ov[l]
                n_ov = pe.value_load(ovinfo[0:1, NOV:NOV + 1], min_val=0, max_val=NOV)
                with pe.If(n_ov > 0):
                    with pe.Fori(0, n_ov) as i:
                        tx(o, 0, i, True, lambda _: pe.wait_ge(o["gathered0"], (i + 1) * 16))
                        tile(o, 0, i, True, lambda s: pe.wait_ge(o["loaded"], (i + 1) * 48), lambda: None)
                stage_end(pe, "pe")
                for j in range(NT):
                    w = TW[j]
                    pe.wait_ge(r["y_summed"], j + 1)
                    if j >= 2:
                        pe.wait_ge(r["y_added"], j - 1)
                    for c in range(DC):
                        bk = 2 * (j % 2) + c // 4
                        last = pe.transpose(bank[bk][:, (c % 4) * P:(c % 4) * P + w],
                                            ysum[j % 2][0:w, c * P:(c + 1) * P], ident[0:w, 0:w])
                    last.then_inc(r["y_turned"], 1)
                stage_end(pe, "pe")

            def lru():
                for br in range(2):
                    for m in range(DC):
                        i = br * DC + m
                        s = 2 * br + m // 4
                        if m % 4 == 0:
                            pe.wait_ge(slot_loaded[s], 16 * (LRU_ROT + 1))
                        if i >= 2:
                            pe.wait_ge(x_out, i - 1)
                        w = ring[s][:, :].rearrange("p (k n) -> p k n", k=DC)[:, :, (m % 4) * P:(m % 4 + 1) * P]
                        for k in range(DC):
                            pe.matmul(bank[i % 2][:, :], w[:, k, :], hT[:, k, 0:S], start=(k == 0), stop=(k == DC - 1))
                        for k in range(DC):
                            last = pe.matmul(bank[2 + br][:, m * NS:(m + 1) * NS], w[:, k, :], hT[:, k, S:T],
                                             start=(k == 0), stop=(k == DC - 1))
                        last.then_inc(x_done, 1)
                        if m % 4 == 3:
                            pe.drain().then_inc(lru_used, 1)
                pe.wait_ge(blocks_loaded, 32)
                pe.wait_ge(x_out, 2 * DC)
                pe.wait_ge(sconv_done, 1)
                for g in range(NBLK):
                    pe.wait_ge(conv_done, BC * (g + 1))
                    for m in range(BC):
                        i = g * BC + m
                        if i >= 2:
                            pe.wait_ge(gates_read, i - 1)
                        for which in range(2):
                            bk = 4 + 2 * (i % 2) + which
                            for k in range(BC):
                                pe.matmul(bank[bk][:, :], wai[:, which, g, k, m * P:(m + 1) * P],
                                          xcT[:, BC * g + k, 0:S], start=(k == 0), stop=(k == BC - 1))
                            for k in range(BC):
                                last = pe.matmul(bank[which][:, i * NS:(i + 1) * NS], wai[:, which, g, k, m * P:(m + 1) * P],
                                                 xcT[:, BC * g + k, S:T], start=(k == 0), stop=(k == BC - 1))
                        last.then_inc(gates_done, 1)
                for s in (4, 5):
                    pe.wait_ge(slot_loaded[s], 16 * (LRU_ROT + 1))
                pe.wait_ge(z_ready, DC + 1)
                for m in range(DC):
                    s = 4 + m // 4
                    if m >= 2:
                        pe.wait_ge(o_out, m - 1)
                    w = ring[s][:, :].rearrange("p (k n) -> p k n", k=DC)[:, :, (m % 4) * P:(m % 4 + 1) * P]
                    for k in range(DC):
                        pe.matmul(bank[4 + m % 2][:, :], w[:, k, :], ybT[:, k, 0:S], start=(k == 0), stop=(k == DC - 1))
                    for k in range(DC):
                        last = pe.matmul(bank[2][:, m * NS:(m + 1) * NS], w[:, k, :], ybT[:, k, S:T],
                                         start=(k == 0), stop=(k == DC - 1))
                    last.then_inc(o_done, 1)
                    if m % 4 == 3:
                        pe.drain().then_inc(lru_used, 1)
                pe.wait_ge(tails_ready, 1)
                tail(6, lambda c: conv_tail[:, c, :])
                tail(0, lambda c: h_tail[:, c, :])
                stage_end(pe, "pe")

            mod(0, MOD0_ROT)
            stage_end(pe, "pe")
            mean(0)
            stage_end(pe, "pe")
            pool_mix()
            mean(1)
            stage_end(pe, "pe")
            moe(0)
            mean(2)
            stage_end(pe, "pe")
            lru()
            mean(3)
            stage_end(pe, "pe")
            moe(1)
            mean(4)
            stage_end(pe, "pe")
            for j in range(NT):
                w = TW[j]
                for half in range(2):
                    i = 2 * j + half
                    if i >= 4:
                        pe.wait_ge(yt_out, i - 3)
                    for c in range(4):
                        last = pe.transpose(bank[i % 4][0:w, c * P:(c + 1) * P],
                                            hT[:, 4 * half + c, j * P:j * P + w], ident[:, :])
                    last.then_inc(yt_done, 1)

        @block.scalar
        def _(act):
            n_own = [0]
            n_stored = [0]

            def own(ins):
                n_own[0] += 1
                ins.then_inc(act_step, 1)
                act.wait_ge(act_step, n_own[0])

            def store(dst, src):
                n_stored[0] += 16
                act.dma_start(dst, src).then_inc(stored, 16)

            for src, n, r in SMALL:
                if len(src.shape) == 2 and src.shape[1] != P:
                    src = src.rearrange("n (r p) -> (n r) p", p=P)
                act.dma_start(rows[r:r + src.shape[0], n, :], src).then_inc(small_loaded, 16)
            act.dma_start(rw[:, :, :], router_w.rearrange("(k p) e -> p k e", p=P)).then_inc(small_loaded, 16)
            act.dma_start(rb[:, :], router_b.partition_broadcast(P)).then_inc(small_loaded, 16)
            act.dma_start(xtok, x_prompt[0].rearrange("(j p) d -> p j d", p=P)).then_inc(in_loaded, 16)
            act.dma_start(xtok_s[0:NS, :], x_sample.rearrange("b s d -> (b s) d")).then_inc(in_loaded, 16)
            act.dma_start(st_rows[0:NB * PB, 0, :], state_pool_buf[0].rearrange("b r d -> (b r) d")).then_inc(state_loaded, 16)
            act.dma_start(st_rows[0:NB * CH, 1, :], state_conv_buf[0].rearrange("b r d -> (b r) d")).then_inc(state_loaded, 16)
            act.dma_start(st_rows[0:NB, 2, :], state_lru_h[0]).then_inc(state_loaded, 16)
            act.wait_ge(lam_exp, 1)
            act.activation(small2[:, DC:2 * DC], small2[:, 0:DC], ACT.Exp).then_inc(lam_exp, 1)
            act.wait_ge(turned_out, 4)
            act.activation(scT[:, :, :].rearrange("p c n -> p n c"), craw.rearrange("p (n c) -> p n c", n=NQ),
                           ACT.Silu).then_inc(silu_c, 1)
            stage_end(act, "act")
            act.dma_start(pw, pool_w[0].rearrange("g (k p) n -> p g k n", p=P)).then_inc(poolw_loaded, 16)
            stage_end(act, "act")

            def norm(n, layer, which, last=False):
                for c in range(DC):
                    act.activation(hT[:, c, :], xT[:, c, :], ACT.Square).then_inc(sq_ready, 1)
                act.wait_ge(mean_ready, n + 1)
                act.activation(rstd[:, 0:S], bank[0][:, :], ACT.Sqrt, bias=consts[:, 0:1])
                act.activation(rstd[:, S:T], bank[1][:, 0:NS], ACT.Sqrt, bias=consts[:, 0:1]).then_inc(std_ready, 1)
                for c in range(DC):
                    act.wait_ge(normed, n * DC + c + 1)
                    if last:
                        act.activation(hT[:, c, :], hT[:, c, :], ACT.Copy, scale=vec("final_g", c))
                    else:
                        act.activation(hT[:, c, 0:S], hT[:, c, 0:S], ACT.Identity,
                                       scale=gainT[:, layer, which, c, 0:1], bias=shiftT[:, layer, which, c, 0:1])
                stage_end(act, "act")

            def tail_rows_out(w0, stores, n, bk=4):
                act.wait_ge(tail_turned, n)
                for half in range(2):
                    ins = act.copy(w0[:, half * HALF:(half + 1) * HALF], bank[bk + half][0:w0.shape[0], :])
                own(ins)
                for dst, lo, hi in stores:
                    store(dst, w0[lo:hi, :])

            def pool_mix():
                tail_rows_out(tail_rows[0:PB, 0, :], [(new_pool_prompt[0, 0], 0, PB)], 1, 4)
                tail_rows_out(tail_rows[0:NS, 1, :],
                              [(new_pool_sample[0, b, PB - SS:PB, :], b * SS, (b + 1) * SS) for b in range(NB)], 2, 6)
                act.wait_ge(stored, n_stored[0])
                stage_end(act, "act")
                act.dma_start(wai[:, 0], lru_w_a[0].rearrange("g (k p) n -> p g k n", p=P)).then_inc(blocks_loaded, 16)
                act.dma_start(wai[:, 1], lru_w_i[0].rearrange("g (k p) n -> p g k n", p=P)).then_inc(blocks_loaded, 16)

            def moe(l):
                r, q = rt[l], ts
                act.wait_ge(r["lmax"], 1)
                act.activation(ex, lg, ACT.Exp).then_inc(r["ex"], 1)
                for j in range(NT):
                    w = TW[j]
                    if j >= 2:
                        act.wait_ge(r[f"rows_stored{j % 2}"], 16 * (j // 2))
                    for half in range(2):
                        act.wait_ge(r["turn"], 2 * j + half + 1)
                        ins = act.copy(htok[j % 2][0:w, half * HALF:(half + 1) * HALF], bank[half][0:w, :])
                        ins.then_inc(r["turn_out"], 1)
                    act.wait_ge(r["turn_out"], 2 * j + 2)
                    act.dma_start(h_rows[l][j * P:j * P + w, :], htok[j % 2][0:w, :]).then_inc(r[f"rows_stored{j % 2}"], 16)
                stage_end(act, "act")

                def xe_copy(q, b, n, used):
                    act.wait_ge(q["tx_done"], n + 1)
                    used()
                    act.copy(xe[b][:, 0:4, :], bank[4][:, :].rearrange("p (c t) -> p c t", c=4)).then_inc(q["xe_copied"], 1)

                def tile(q, b, n, first, x_next, ys_free):
                    act.wait_ge(q["g_done"], n + 1)
                    if not first:
                        act.wait_ge(q["hid_done"], n - 1)
                    act.activation(sg[b], bank[0][:, :], ACT.Silu).then_inc(q["silu_done"], 1)
                    x_next()
                    act.wait_ge(q["th_done"], n + 1)
                    if not first:
                        act.wait_ge(q["y_done"], n * 2 - 2)
                    act.copy(hidT[b][:, 0:2, :], bank[6][:, 0:2 * P].rearrange("p (c t) -> p c t", c=2)
                             ).then_inc(q["ht_copied"], 1)
                    act.wait_ge(q["y_done"], n * 2 + 1)
                    ys_free()
                    act.copy(ys[b][:, 0:HALF], bank[2][:, :]).then_inc(q["ys_copied"], 1)

                def step(it, b, first=False, last=False):
                    t = it * 2 + (b + NE * l)
                    nb = 1 - b

                    def x_next():
                        if not last:
                            xe_copy(q, nb, t + 1, lambda: None if first and b == 0 else act.wait_ge(q["u_done"], t))

                    tile(q, b, t, first, x_next,
                         lambda: None if first else act.wait_ge(q[f"scattered{b}"], it * 16 + l * (NE * 8)))

                xe_copy(q, 0, NE * l, lambda: None)
                step(0, 0, first=True)
                step(0, 1, first=True)
                with act.Fori(1, NE // 2 - 1) as it:
                    step(it, 0)
                    step(it, 1)
                step(NE // 2 - 1, 0)
                step(NE // 2 - 1, 1, last=True)
                o = ov[l]
                n_ov = act.value_load(ovinfo[0:1, NOV:NOV + 1], min_val=0, max_val=NOV)
                with act.If(n_ov > 0):
                    with act.Fori(0, n_ov) as i:
                        xe_copy(o, 0, i, lambda: None)
                        tile(o, 0, i, True, lambda: None, lambda: None)
                stage_end(act, "act")
                for j in range(NT):
                    w = TW[j]
                    act.wait_ge(r[f"y_loaded{j % 2}"], 32 * (j // 2 + 1))
                    if j >= 2:
                        act.wait_ge(r["y_turned"], j - 1)
                    act.activation(ysum[j % 2][0:w, :], yl[j % 2][0][0:w, :], ACT.Copy,
                                   scale=wts[0:w, 0, j:j + 1]).then_inc(r["y_scaled"], 1)
                stage_end(act, "act")

            def lru():
                for br in range(2):
                    for m in range(DC):
                        i = br * DC + m
                        act.wait_ge(x_done, i + 1)
                        if br == 0:
                            act.activation(xb[:, m, CH:CH + S], bank[i % 2][:, :], ACT.Identity,
                                           bias=vec("b_x", m)).then_inc(x_out, 1)
                        else:
                            act.activation(ybT[:, m, 0:S], bank[i % 2][:, :], GELU, bias=vec("b_y", m)).then_inc(x_out, 1)
                act.wait_ge(sgelu_in, 1)
                act.activation(ybT[:, :, S:T], small[:, :].rearrange("p (c t) -> p c t", c=DC), GELU).then_inc(sgelu, 1)
                for i in range(DC):
                    act.wait_ge(gates_done, i + 1)
                    if i >= 2:
                        act.wait_ge(mult_done, i - 1)
                    a = aT[:, i, 0:S]
                    act.activation(a, bank[4 + 2 * (i % 2)][:, :], ACT.Tanh, scale=0.5, bias=half_b[:, 0, i:i + 1])
                    ins = act.activation(tanh_i[i % 2], bank[5 + 2 * (i % 2)][:, :], ACT.Tanh, scale=0.5,
                                         bias=half_b[:, 1, i:i + 1])
                    ins.then_inc(gates_read, 1)
                    act.wait_ge(gates_read, i + 1)
                    act.activation(e2[:, i, 0:S], a, ACT.Exp, scale=kdec[:, 1, i:i + 1], bias=kdec[:, 1, i:i + 1])
                    act.activation(a, a, ACT.Exp, scale=kdec[:, 0, i:i + 1], bias=kdec[:, 0, i:i + 1]).then_inc(a_ready, 1)
                act.wait_ge(sgate_in, 2)
                act.activation(small[:, :], small[:, :], ACT.Tanh, scale=0.5)
                act.activation(small2[:, :], small2[:, :], ACT.Tanh, scale=0.5).then_inc(stanh, 1)
                act.wait_ge(sdecay_in, 1)
                act.activation(aT[:, :, S:T], small[:, :].rearrange("p (c t) -> p c t", c=DC), ACT.Exp)
                act.activation(small[:, :], small[:, :], ACT.Exp, scale=2.0).then_inc(sexp, 1)
                for i in range(DC):
                    act.wait_ge(power_ready, i + 1)
                    act.activation(e2[:, i, 0:S], e2[:, i, 0:S], ACT.Sqrt, bias=consts[:, 1:2]).then_inc(root_ready, 1)
                act.wait_ge(power_ready, DC + 1)
                act.activation(small[:, :], small[:, :], ACT.Sqrt, bias=consts[:, 1:2]).then_inc(root_ready, 1)
                for m in range(DC):
                    act.wait_ge(o_done, m + 1)
                    if m >= 2:
                        act.wait_ge(o_added, m - 1)
                    act.activation(tanh_i[m % 2], bank[4 + m % 2][:, :], ACT.Identity, scale=gateT[:, 1, 0, m, 0:1],
                                   bias=gbT[:, m, 0:1]).then_inc(o_out, 1)
                tail_rows_out(xcT_rows(0)[0:CH * NQ, :],
                              [(new_conv_prompt[0, 0], 0, CH),
                               (new_conv_sample[0].rearrange("b r d -> (b r) d"), CH, CH * NQ)], 3, 6)
                tail_rows_out(xcT_rows(1)[0:NQ, :], [(new_h_prompt[0], 0, 1), (new_h_sample[0], 1, NQ)], 4, 0)
                act.wait_ge(stored, n_stored[0])
                stage_end(act, "act")

            norm(0, 0, 0)
            pool_mix()
            norm(1, 0, 1)
            moe(0)
            norm(2, 1, 0)
            lru()
            norm(3, 1, 1)
            moe(1)
            norm(4, None, None, last=True)
            for j in range(NT):
                w = TW[j]
                if j >= 2:
                    act.wait_ge(yt_stored[j % 2], 16 * (j // 2))
                for half in range(2):
                    i = 2 * j + half
                    act.wait_ge(yt_done, i + 1)
                    act.copy(ysum[j % 2][0:w, half * HALF:(half + 1) * HALF], bank[i % 4][0:w, :]).then_inc(yt_out, 1)
                act.wait_ge(yt_out, 2 * j + 2)
                dst = y_prompt[0, j * P:(j + 1) * P, :] if w == P else y_sample.rearrange("b s d -> (b s) d")
                act.dma_start(dst, ysum[j % 2][0:w, :]).then_inc(yt_stored[j % 2], 16)
            for b in range(2):
                act.wait_ge(yt_stored[b], 16 * ((NT + 1 - b) // 2))

        @block.vector
        def _(dve):
            n_own = [0]

            def own(ins):
                n_own[0] += 1
                ins.then_inc(vec_step, 1)
                dve.wait_ge(vec_step, n_own[0])

            def tt(out, a, b, op):
                own(dve.tensor_tensor(out, a, b, op))

            def spread(a, n):
                return a.unsqueeze(len(a.shape)).to_broadcast(list(a.shape) + [n])

            dve.memset(mean_w[:, :], 1.0 / D)
            dve.memset(ones_b[:, :], 1.0)
            dve.memset(nowhere[:, :], NOWHERE)
            dve.memset(consts[:, 0:1], EPS)
            dve.memset(consts[:, 1:2], 0.25)
            own(dve.memset(valid[:, :], 1.0))
            own(dve.memset(nowhere[:, :], NOWHERE))
            n = 0

            def out_copy(dst, src):
                dve.tensor_copy(dst, src).then_inc(turned_out, 1)

            dve.wait_ge(turned, 1)
            out_copy(bmodT[:, :], bank[0][:, 0:DEPTH * NM])
            dve.wait_ge(turned, 2)
            out_copy(vecT[:, 0:96], bank[1][:, 0:96])
            dve.wait_ge(turned, 3)
            out_copy(vecT[:, 96:136], bank[2][:, 0:40])
            dve.wait_ge(turned, 4)
            out_copy(craw, bank[3][:, 0:NQ * DC])
            for g in range(2):
                dve.wait_ge(turned, 5 + g)
                out_copy(poolT[:, 4 * g:4 * g + 4, :], bank[4 + g][:, 0:4 * NB * PB].rearrange("p (c r) -> p c r", c=4))
            dve.wait_ge(turned, 7)
            out_copy(convT[:, :, :], bank[6][:, 0:DC * NB * CH].rearrange("p (c r) -> p c r", c=DC))
            dve.wait_ge(turned, 8)
            out_copy(h0T[:, :, :], bank[7][:, 0:DC * NB].rearrange("p (c r) -> p c r", c=DC))
            for c in range(DC):
                dve.wait_ge(turned, 9 + c)
                out_copy(xT[:, c, 0:S], bank[c][:, :])
            dve.wait_ge(turned, 9 + DC)
            out_copy(xT[:, :, S:T], bank[0][:, 0:DC * NS].rearrange("p (c t) -> p c t", c=DC))
            dve.wait_ge(turned_out, 17)
            lam = vec("lam")
            k0, k1 = kdec[:, 0, :], kdec[:, 1, :]
            z, z2 = small[:, 0:DC], small[:, DC:2 * DC]
            own(dve.tensor_scalar(z, lam, -1.0, None, ALU.mult))
            tt(z, z, lam, ALU.min)
            dve.tensor_copy(small2[:, 0:DC], z).then_inc(lam_exp, 1)
            dve.wait_ge(lam_exp, 2)
            own(dve.tensor_scalar(z2, small2[:, DC:2 * DC], 2.0, None, ALU.add))
            own(dve.reciprocal(z2, z2))
            tt(z, small2[:, DC:2 * DC], z2, ALU.mult)
            tt(z2, z, z, ALU.mult)
            own(dve.tensor_scalar(k0, z2, 1.0 / 19, 1.0 / 17, ALU.mult, ALU.add))
            for d in (15, 13, 11, 9, 7, 5, 3, 1):
                tt(k0, k0, z2, ALU.mult)
                own(dve.tensor_scalar(k0, k0, 1.0 / d, None, ALU.add))
            tt(k0, k0, z, ALU.mult)
            own(dve.tensor_scalar(z2, lam, -1.0, 0.0, ALU.mult, ALU.max))
            own(dve.scalar_tensor_tensor(k0, k0, 2.0, z2, ALU.mult, ALU.add))
            own(dve.tensor_scalar(k0, k0, -LRU_C / 2, None, ALU.mult))
            dve.tensor_scalar(k1, k0, 2.0, None, ALU.mult)
            dve.tensor_scalar(half_b[:, 0, :], vec("b_a"), 0.5, None, ALU.mult)
            dve.tensor_scalar(half_b[:, 1, :], vec("b_i"), 0.5, None, ALU.mult)
            dve.wait_ge(pool_step, 5)
            own(dve.tensor_copy(invcnt[:, :], iota_e[:, 0:16]))
            own(dve.tensor_scalar(invcnt[:, :], invcnt[:, :], 1.0, None, ALU.add))
            own(dve.reciprocal(invcnt[:, :], invcnt[:, :]))
            stage_end(dve, "dve")

            def adaln(l):
                dve.wait_ge(mod_done, l + 1)
                tt(modT[:, :, :], bank[7][:, 0:NM * NQ].rearrange("p (m n) -> p m n", m=NM),
                   spread(bmodT[:, l * NM:(l + 1) * NM], NQ), ALU.add)
                for which in range(2):
                    m0 = 3 * DC * which
                    g = spread(vecT[:, (2 * l + which) * DC:(2 * l + which + 1) * DC], NQ)
                    own(dve.scalar_tensor_tensor(gainT[:, l, which], modT[:, m0 + DC:m0 + 2 * DC, :], 1.0, g,
                                                 ALU.add, ALU.mult))
                    own(dve.tensor_copy(shiftT[:, l, which], modT[:, m0:m0 + DC, :]))
                    own(dve.tensor_copy(gateT[:, l, which], modT[:, m0 + 2 * DC:m0 + 3 * DC, :]))
                if l == 0:
                    tt(gateT[:, 0, 0], gateT[:, 0, 0], spread(vec("pool_scale"), NQ), ALU.mult)
                else:
                    tt(gbT[:, :, :], gateT[:, 1, 0], spread(vec("b_out"), NQ), ALU.mult)

            adaln(0)
            stage_end(dve, "dve")

            def seqs(a):
                return a.rearrange("p c (b s) -> p c b s", b=NB)

            def norm(n, layer, which, last=False):
                dve.wait_ge(std_ready, n + 1)
                own(dve.reciprocal(rstd, rstd))
                for c in range(DC):
                    dve.tensor_tensor(hT[:, c, :], xT[:, c, :], rstd, ALU.mult).then_inc(normed, 1)
                if not last:
                    dve.wait_ge(normed, (n + 1) * DC)
                    h = seqs(hT[:, :, S:T])
                    tt(h, h, spread(gainT[:, layer, which, :, 1:NQ], SS), ALU.mult)
                    tt(h, h, spread(shiftT[:, layer, which, :, 1:NQ], SS), ALU.add)
                stage_end(dve, "dve")

            def add_samples(src, layer, which):
                t = small[:, :].rearrange("p (c t) -> p c t", c=DC)
                tt(seqs(t), seqs(src), spread(gateT[:, layer, which, :, 1:NQ], SS), ALU.mult)
                tt(xT[:, :, S:T], xT[:, :, S:T], t, ALU.add)

            def pool_mix():
                for g, w in enumerate(POOL_WINDOWS):
                    h = hT[:, 2 * g:2 * g + 2, 0:S]
                    src, dst, d = h, psum_a, 1
                    s_src, s_dst = spool_a, spool_b
                    dve.tensor_copy(spool_a[:, :, :, 0:PB],
                                    poolT[:, 2 * g:2 * g + 2, :].rearrange("p c (b r) -> p c b r", b=NB))
                    own(dve.tensor_copy(spool_a[:, :, :, PB:PB + SS], seqs(hT[:, 2 * g:2 * g + 2, S:T])))
                    while d < w:
                        dve.tensor_copy(dst[:, :, 0:d], src[:, :, 0:d])
                        dve.tensor_tensor(dst[:, :, d:S], src[:, :, d:S], src[:, :, 0:S - d], ALU.add)
                        tt(s_dst[:, :, :, 2 * d - 1:PB + SS], s_src[:, :, :, 2 * d - 1:PB + SS],
                           s_src[:, :, :, d - 1:PB + SS - d], ALU.add)
                        src, dst = dst, (psum_b if dst is psum_a else psum_a)
                        s_src, s_dst = s_dst, s_src
                        d *= 2
                    out = pooledT[:, 2 * g:2 * g + 2, :]
                    cnt = invcnt[:, 0:w - 1].unsqueeze(1).to_broadcast([P, 2, w - 1])
                    tt(dst[:, :, 0:w - 1], src[:, :, 0:w - 1], cnt, ALU.mult)
                    dve.tensor_tensor(out[:, :, 0:w - 1], dst[:, :, 0:w - 1], h[:, :, 0:w - 1], ALU.subtract)
                    dve.scalar_tensor_tensor(out[:, :, w - 1:S], src[:, :, w - 1:S], 1.0 / w, h[:, :, w - 1:S],
                                             ALU.mult, ALU.subtract)
                    own(dve.tensor_scalar(s_dst[:, :, :, PB:PB + SS], s_src[:, :, :, PB:PB + SS], 1.0 / w, None, ALU.mult))
                    dve.tensor_tensor(seqs(out[:, :, S:T]), s_dst[:, :, :, PB:PB + SS],
                                      seqs(hT[:, 2 * g:2 * g + 2, S:T]), ALU.subtract).then_inc(pooled_ready, 1)
                    dve.wait_ge(pooled_ready, g + 1)
                for i in range(DC):
                    dve.wait_ge(mixed, i + 1)
                    dve.scalar_tensor_tensor(xT[:, i, 0:S], bank[i % 2][:, :], gateT[:, 0, 0, i, 0:1], xT[:, i, 0:S],
                                             ALU.mult, ALU.add).then_inc(mixed_added, 1)
                add_samples(bank[2][:, 0:DC * NS].rearrange("p (c t) -> p c t", c=DC), 0, 0)
                stage_end(dve, "dve")

            def first_max(out, vals, n, shape):
                rows_n = shape
                top = tmp_b[:, 0:rows_n]
                own(dve.tensor_reduce(top, vals, AX, ALU.max))
                tt(out, vals, spread(top, n), ALU.is_ge)
                it = iota_e[:, 0:n].unsqueeze(1).to_broadcast([P, rows_n, n])
                own(dve.scalar_tensor_tensor(out, out, -64.0, it, ALU.mult, ALU.add))
                own(dve.tensor_reduce(top, out, AX, ALU.min))
                tt(out, out, spread(top, n), ALU.is_equal)

            def moe(l):
                r, q = rt[l], ts
                own(dve.memset(lg, 0.0))
                dve.wait_ge(r["logits"], 1)
                own(dve.tensor_copy(lg[:, 0:NPT, :], bank[2][:, 0:NPT * NE].rearrange("p (j e) -> p j e", j=NPT)))
                own(dve.tensor_copy(lg[0:TW[-1], NPT, :], bank[2][0:TW[-1], NPT * NE:NT * NE]))
                own(dve.tensor_reduce(tmp_b[:, 0:NT], lg, AX, ALU.max))
                dve.tensor_tensor(lg, lg, spread(tmp_b[:, 0:NT], NE), ALU.subtract).then_inc(r["lmax"], 1)
                dve.wait_ge(r["ex"], 1)
                own(dve.tensor_reduce(tmp_b[:, 0:NT], ex, AX, ALU.add))
                own(dve.reciprocal(tmp_b[:, 0:NT], tmp_b[:, 0:NT]))
                tt(ex, ex, spread(tmp_b[:, 0:NT], NE), ALU.mult)
                tt(sel, ex, rb[:, :].unsqueeze(1).to_broadcast([P, NT, NE]), ALU.add)
                s4 = sel.rearrange("p j (g e) -> p (j g) e", g=NG)
                hi, lo = [x.rearrange("p j (g e) -> p (j g) e", g=NG) for x in (val_a, val_b)]
                tt(hi[:, :, 0:2], s4[:, :, 0:2], s4[:, :, 2:4], ALU.max)
                tt(lo[:, :, 0:2], s4[:, :, 0:2], s4[:, :, 2:4], ALU.min)
                tt(hi[:, :, 2:3], hi[:, :, 0:1], hi[:, :, 1:2], ALU.max)
                tt(hi[:, :, 3:4], hi[:, :, 0:1], hi[:, :, 1:2], ALU.min)
                tt(lo[:, :, 2:3], lo[:, :, 0:1], lo[:, :, 1:2], ALU.max)
                tt(lo[:, :, 3:4], lo[:, :, 2:3], hi[:, :, 3:4], ALU.max)
                gs = gsc.rearrange("p j g -> p (j g)")
                tt(gs.unsqueeze(2), lo[:, :, 3:4], hi[:, :, 2:3], ALU.add)
                first_max(gbest, gsc, NG, NT)
                own(dve.tensor_scalar(gbest, gbest, BIG, -BIG, ALU.mult, ALU.add))
                tt(s4, s4, spread(gbest.rearrange("p j g -> p (j g)"), EG), ALU.add)
                first_max(one, sel, NE, NT)
                own(dve.scalar_tensor_tensor(sel, one, -3 * BIG, sel, ALU.mult, ALU.add))
                first_max(two, sel, NE, NT)
                for k, pick in enumerate((one, two)):
                    tt(val_a, ex, pick, ALU.mult)
                    own(dve.tensor_reduce(wts[:, k, :], val_a, AX, ALU.add))
                tt(tmp_b[:, 0:NT], wts[:, 0, :], wts[:, 1, :], ALU.add)
                own(dve.reciprocal(tmp_b[:, 0:NT], tmp_b[:, 0:NT]))
                for k in range(2):
                    tt(wts[:, k, :], wts[:, k, :], tmp_b[:, 0:NT], ALU.mult)
                tt(val_a, one, two, ALU.add)
                dve.tensor_tensor(picks[:, :, :], val_a, spread(valid[:, :], NE), ALU.mult).then_inc(r["count_in"], 1)
                dve.wait_ge(r["counts"], 1)
                own(dve.tensor_copy(sel, bank[3][:, 0:NT * NE].rearrange("p (j e) -> p j e", j=NT)))
                own(dve.tensor_copy(cnt_e, bank[3][:, NT * NE:(NT + 1) * NE]))
                own(dve.tensor_scalar(ov_e, cnt_e, float(P), None, ALU.is_gt))
                for k in range(2, (T + P - 1) // P):
                    own(dve.tensor_scalar(cum_e, cnt_e, float(k * P), None, ALU.is_gt))
                    tt(ov_e, ov_e, cum_e, ALU.add)
                own(dve.tensor_scalar(cnt_e, cnt_e, 0.0, 1.0, ALU.mult, ALU.add))
                own(dve.tensor_tensor_scan(cum_e, cnt_e, ov_e, 0.0, ALU.mult, ALU.add))
                for t in range(NOV):
                    own(dve.tensor_scalar(cnt_e, cum_e, float(t), None, ALU.is_le))
                    own(dve.tensor_reduce(ov_f[:, t:t + 1], cnt_e, AX, ALU.add))
                own(dve.tensor_copy(ov_f[:, NOV:NOV + 1], cum_e[:, NE - 1:NE]))
                own(dve.tensor_copy(ovinfo[:, :], ov_f[0:1, :]))
                tt(cum_e, cum_e, ov_e, ALU.subtract)
                tt(cum_e, cum_e, iota_e[:, :], ALU.subtract)
                own(dve.tensor_scalar(cum_e, cum_e, float(NE - 1), float(P), ALU.add, ALU.mult))
                own(dve.tensor_scalar(val_a, sel, float(P), None, ALU.is_ge))
                tt(val_a, val_a, cum_e.unsqueeze(1).to_broadcast([P, NT, NE]), ALU.mult)
                tt(val_a, val_a, sel, ALU.add)
                own(dve.tensor_scalar(cum_e, iota_e[:, :], float(P), None, ALU.mult))
                tt(val_a, val_a, cum_e.unsqueeze(1).to_broadcast([P, NT, NE]), ALU.add)
                for k, pick in enumerate((one, two)):
                    tt(val_b, val_a, pick, ALU.mult)
                    own(dve.tensor_reduce(tmp_b[:, 0:NT], val_b, AX, ALU.add))
                    ins = dve.tensor_copy(slot_i[:, k * NT:(k + 1) * NT], tmp_b[:, 0:NT])
                    own(ins)
                dve.drain().then_inc(r["slots_ready"], 1)
                dve.wait_ge(r["list_loaded"], 16)
                dve.tensor_copy(list_f, list_i).then_inc(r["list_f"], 1)
                dve.wait_ge(r["list_t"], 1)
                own(dve.tensor_copy(lt_f, bank[3][:, 0:NL]))
                own(dve.tensor_copy(yrow[:, :], lt_f))
                own(dve.tensor_scalar(lt_g, lt_f, float(T), float(-T), ALU.is_ge, ALU.mult))
                tt(lt_f, lt_f, lt_g, ALU.add)
                own(dve.tensor_copy(tokl[:, :], lt_f))
                dve.drain().then_inc(r["list_ready"], 2)
                if l == 0:
                    adaln(1)
                stage_end(dve, "dve")

                def xe_copy(q, b, n, used):
                    dve.wait_ge(q["tx_done"], n + 1)
                    used()
                    dve.tensor_copy(xe[b][:, 4:8, :], bank[5][:, :].rearrange("p (c t) -> p c t", c=4)
                                    ).then_inc(q["xe_copied"], 1)

                def tile(q, b, n, first, x_next, ys_free):
                    dve.wait_ge(q["silu_done"], n + 1)
                    dve.wait_ge(q["u_done"], n + 1)
                    if not first:
                        dve.wait_ge(q["th_done"], n - 1)
                    dve.tensor_tensor(hid[b], sg[b], bank[1][:, :], ALU.mult).then_inc(q["hid_done"], 1)
                    x_next()
                    dve.wait_ge(q["th_done"], n + 1)
                    if not first:
                        dve.wait_ge(q["y_done"], n * 2 - 2)
                    dve.tensor_copy(hidT[b][:, 2:4, :], bank[7][:, 0:2 * P].rearrange("p (c t) -> p c t", c=2)
                                    ).then_inc(q["ht_copied"], 1)
                    dve.wait_ge(q["y_done"], n * 2 + 2)
                    ys_free()
                    dve.tensor_copy(ys[b][:, HALF:D], bank[3][:, :]).then_inc(q["ys_copied"], 1)

                def step(it, b, first=False, last=False):
                    t = it * 2 + (b + NE * l)
                    nb = 1 - b

                    def x_next():
                        if not last:
                            xe_copy(q, nb, t + 1, lambda: None if first and b == 0 else dve.wait_ge(q["u_done"], t))

                    tile(q, b, t, first, x_next,
                         lambda: None if first else dve.wait_ge(q[f"scattered{b}"], it * 16 + l * (NE * 8)))

                xe_copy(q, 0, NE * l, lambda: None)
                step(0, 0, first=True)
                step(0, 1, first=True)
                with dve.Fori(1, NE // 2 - 1) as it:
                    step(it, 0)
                    step(it, 1)
                step(NE // 2 - 1, 0)
                step(NE // 2 - 1, 1, last=True)
                o = ov[l]
                n_ov = dve.value_load(ovinfo[0:1, NOV:NOV + 1], min_val=0, max_val=NOV)
                with dve.If(n_ov > 0):
                    with dve.Fori(0, n_ov) as i:
                        xe_copy(o, 0, i, lambda: None)
                        tile(o, 0, i, True, lambda: None, lambda: None)
                stage_end(dve, "dve")
                def add_tile(j):
                    w = TW[j]
                    dve.wait_ge(r["y_turned"], j + 1)
                    bks = [bank[2 * (j % 2) + h][:, :].rearrange("p (c t) -> p c t", c=4) for h in range(2)]
                    if w == P:
                        for c in range(DC):
                            ins = dve.scalar_tensor_tensor(xT[:, c, j * P:(j + 1) * P], bks[c // 4][:, c % 4, :],
                                                           gateT[:, l, 1, c, 0:1], xT[:, c, j * P:(j + 1) * P],
                                                           ALU.mult, ALU.add)
                        ins.then_inc(r["y_added"], 1)
                    else:
                        s2 = small2[:, :].rearrange("p (c t) -> p c t", c=DC)
                        for h in range(2):
                            own(dve.tensor_copy(s2[:, 4 * h:4 * h + 4, :], bks[h][:, :, 0:w]))
                        add_samples(s2, l, 1)

                for j in range(NT):
                    w = TW[j]
                    dve.wait_ge(r["y_scaled"], j + 1)
                    dve.scalar_tensor_tensor(ysum[j % 2][0:w, :], yl[j % 2][1][0:w, :], wts[0:w, 1, j:j + 1],
                                             ysum[j % 2][0:w, :], ALU.mult, ALU.add).then_inc(r["y_summed"], 1)
                    if j >= 1:
                        add_tile(j - 1)
                add_tile(NT - 1)
                stage_end(dve, "dve")

            def lru():
                xs = [small[:, :].rearrange("p (c t) -> p c t", c=DC), small2[:, :].rearrange("p (c t) -> p c t", c=DC)]

                def sbank(b):
                    return bank[b][:, 0:DC * NS].rearrange("p (c t) -> p c t", c=DC)

                dve.memset(xb[:, :, 0:CH], 0.0)
                own(dve.tensor_copy(xbs[:, :, :, 0:CH], convT[:, :, :].rearrange("p c (b r) -> p c b r", b=NB)))
                for m in range(DC):
                    dve.wait_ge(x_out, m + 1)
                    own(dve.tensor_scalar(xcT[:, m, 0:S], xb[:, m, 0:S], vec("cw0", m), vec("conv_b", m), ALU.mult, ALU.add))
                    for k in range(1, CW):
                        ins = dve.scalar_tensor_tensor(xcT[:, m, 0:S], xb[:, m, k:k + S], vec(f"cw{k}", m),
                                                       xcT[:, m, 0:S], ALU.mult, ALU.add)
                        own(ins)
                    dve.drain().then_inc(conv_done, 1)
                tt(xbs[:, :, :, CH:CH + SS], seqs(sbank(2)), spread(spread(vec("b_x"), NB), SS), ALU.add)
                xc_s = seqs(xcT[:, :, S:T])
                t_s = seqs(xs[0])
                tt(xc_s, xbs[:, :, :, 0:SS], spread(spread(vec("cw0"), NB), SS), ALU.mult)
                for k in range(1, CW):
                    tt(t_s, xbs[:, :, :, k:k + SS], spread(spread(vec(f"cw{k}"), NB), SS), ALU.mult)
                    tt(xc_s, xc_s, t_s, ALU.add)
                tt(xcT[:, :, S:T], xcT[:, :, S:T], spread(vec("conv_b"), NS), ALU.add)
                own(dve.tensor_copy(conv_tail[:, :, 0:CH], xb[:, :, S:S + CH]))
                own(dve.tensor_copy(conv_tail[:, :, CH:CH * NQ].rearrange("p c (b r) -> p c b r", b=NB),
                                    xbs[:, :, :, SS:SS + CH]))
                dve.drain().then_inc(sconv_done, 1)
                dve.wait_ge(x_done, 2 * DC)
                dve.tensor_tensor(xs[0], sbank(3), spread(vec("b_y"), NS), ALU.add).then_inc(sgelu_in, 1)
                for i in range(DC):
                    g = i // BC
                    dve.wait_ge(gates_done, BC * (g + 1))
                    dve.wait_ge(gates_read, i + 1)
                    own(dve.scalar_tensor_tensor(xcT[:, i, 0:S], tanh_i[i % 2], 1.0, xcT[:, i, 0:S], ALU.add, ALU.mult))
                    dve.drain().then_inc(mult_done, 1)
                    dve.wait_ge(a_ready, i + 1)
                    dve.tensor_scalar(e2[:, i, 0:S], e2[:, i, 0:S], 1.0, -0.25, ALU.min, ALU.mult).then_inc(power_ready, 1)
                dve.wait_ge(sgelu, 1)
                dve.tensor_tensor(xs[0], sbank(0), spread(vec("b_a"), NS), ALU.add).then_inc(sgate_in, 1)
                dve.tensor_tensor(xs[1], sbank(1), spread(vec("b_i"), NS), ALU.add).then_inc(sgate_in, 1)
                dve.wait_ge(stanh, 1)
                own(dve.scalar_tensor_tensor(xcT[:, :, S:T], xs[1], 1.0, xcT[:, :, S:T], ALU.add, ALU.mult))
                dve.scalar_tensor_tensor(xs[0], xs[0], 1.0, spread(kdec[:, 0, :], NS), ALU.add, ALU.mult).then_inc(sdecay_in, 1)
                dve.wait_ge(sexp, 1)
                dve.tensor_scalar(xs[0], xs[0], 1.0, -0.25, ALU.min, ALU.mult).then_inc(power_ready, 1)
                for i in range(DC):
                    dve.wait_ge(root_ready, i + 1)
                    own(dve.memset(e2[:, i, 0:1], 0.5))
                    tt(xcT[:, i, 0:S], xcT[:, i, 0:S], e2[:, i, 0:S], ALU.mult)
                    own(dve.tensor_tensor_scan(e2[:, i, 0:S], aT[:, i, 0:S], xcT[:, i, 0:S], 0.0, ALU.mult, ALU.add))
                    own(dve.tensor_copy(h_tail[:, i, 0:1], e2[:, i, S - 1:S]))
                    dve.wait_ge(x_out, DC + i + 1)
                    dve.tensor_tensor(ybT[:, i, 0:S], e2[:, i, 0:S], ybT[:, i, 0:S], ALU.mult).then_inc(z_ready, 1)
                dve.wait_ge(root_ready, DC + 1)
                tt(xs[0], xs[0], xcT[:, :, S:T], ALU.mult)
                a_s, b_s = seqs(aT[:, :, S:T]), seqs(xs[0])
                prev = h0T[:, :, :]
                for s in range(SS):
                    cur = seqs(xs[1])[:, :, :, s]
                    tt(cur, a_s[:, :, :, s], prev, ALU.mult)
                    tt(cur, cur, b_s[:, :, :, s], ALU.add)
                    prev = cur
                own(dve.tensor_copy(h_tail[:, :, 1:NQ], prev))
                dve.tensor_tensor(ybT[:, :, S:T], xs[1], ybT[:, :, S:T], ALU.mult).then_inc(z_ready, 1)
                dve.drain().then_inc(tails_ready, 1)
                for m in range(DC):
                    dve.wait_ge(o_out, m + 1)
                    dve.tensor_tensor(xT[:, m, 0:S], xT[:, m, 0:S], tanh_i[m % 2], ALU.add).then_inc(o_added, 1)
                add_samples(sbank(2), 1, 0)
                tt(seqs(xT[:, :, S:T]), seqs(xT[:, :, S:T]), spread(gbT[:, :, 1:NQ], SS), ALU.add)
                stage_end(dve, "dve")

            norm(0, 0, 0)
            pool_mix()
            norm(1, 0, 1)
            moe(0)
            norm(2, 1, 0)
            lru()
            norm(3, 1, 1)
            moe(1)
            norm(4, None, None, last=True)

        @block.gpsimd
        def _(pool):
            def own(ins, sem_=pool_step):
                own.n += 1
                ins.then_inc(pool_step, 1)
                pool.wait_ge(pool_step, own.n)
            own.n = 0
            own(pool.memset(ident[:, :], 0.0))
            own(pool.affine_select(ident[:, :], ident[:, :], [[-1, P]], ALU.not_equal, 1.0, base=0, channel_multiplier=1))
            own(pool.memset(before_b[:, :], 1.0))
            own(pool.affine_select(before_b[:, :], before_b[:, :], [[1, P]], ALU.is_gt, 0.0, base=0, channel_multiplier=-1))
            own(pool.iota(iota_e[:, :], [[1, NE]], base=0, channel_multiplier=0, allow_small_or_imprecise_dtypes=True))
            own(pool.iota(iota_y[:, 0:NT], [[P, NT]], base=0, channel_multiplier=1))
            own(pool.iota(iota_y[:, NT:2 * NT], [[P, NT]], base=T, channel_multiplier=1))
            pool.wait_ge(vec_step, 2)
            own(pool.affine_select(valid[:, :], valid[:, :], [[-P, NT]], ALU.is_gt, 0.0, base=T, channel_multiplier=-1))
            for l in range(DEPTH):
                pool.dma_start(slots[l].rearrange("(a t) o -> a (t o)", a=P), nowhere[:, :]).then_inc(lists_filled, 16)
            pool.wait_ge(lists_filled, 16 * DEPTH)
            stage_end(pool, "pool")
            stage_end(pool, "pool")

            def moe(l):
                r, q = rt[l], ts
                for b in range(2):
                    pool.memset(xg[b], 0.0)
                pool.wait_ge(r["slots_ready"], 1)
                for k in range(2):
                    for j in range(NT):
                        i = k * NT + j
                        w = TW[j]
                        pool.indirect_dma_start(slots[l], bass.IndirectOffsetOnAxis(slot_i[0:w, i:i + 1], 0),
                                                iota_y[0:w, i:i + 1], None, bounds_check=NL * P - 1,
                                                oob_is_err=False).then_inc(r["ids_stored"], 16)
                pool.wait_ge(r["ids_stored"], 16 * 2 * NT)
                pool.dma_start(list_i, slots[l].rearrange("(t p) o -> t (p o)", p=P)).then_inc(r["list_loaded"], 16)
                for b in range(2):
                    pool.wait_ge(r[f"rows_stored{b}"], 16 * ((NT + 1 - b) // 2))
                stage_end(pool, "pool")

                def gather(q, b, n, t):
                    pool.tensor_copy(toks[b][:, :], tokl[:, bass.ds(t, 1)]).then_inc(q["toks_ready"], 1)
                    pool.wait_ge(q["toks_ready"], n + 1)
                    pool.sem_inc(waits_seen, 1)
                    pool.indirect_dma_start(xg[b], None, h_rows[l], bass.IndirectOffsetOnAxis(toks[b][:, :], 0),
                                            bounds_check=T - 1, oob_is_err=False).then_inc(q[f"gathered{b}"], 16)

                def scatter(q, b, n, t):
                    pool.tensor_copy(yrows[b][:, :], yrow[:, bass.ds(t, 1)]).then_inc(q["yrows_ready"], 1)
                    pool.wait_ge(q["yrows_ready"], n + 1)
                    pool.wait_ge(q["ys_copied"], n * 2 + 2)
                    pool.sem_inc(waits_seen, 1)
                    pool.indirect_dma_start(y_rows[l], bass.IndirectOffsetOnAxis(yrows[b][:, :], 0), ys[b], None,
                                            bounds_check=2 * T - 1, oob_is_err=False).then_inc(q[f"scattered{b}"], 16)

                def step(it, b, first=False, last=False):
                    t = it * 2 + b
                    n = it * 2 + (b + NE * l)
                    if not last:
                        pool.wait_ge(q["tx_done"], n + 1)
                        gather(q, b, n + 2, t + 2)
                    if not first:
                        pool.wait_ge(q[f"scattered{b}"], it * 16 + l * (NE * 8))
                    scatter(q, b, n, t)

                gather(q, 0, NE * l, 0)
                gather(q, 1, NE * l + 1, 1)
                step(0, 0, first=True)
                step(0, 1, first=True)
                with pool.Fori(1, NE // 2 - 1) as it:
                    step(it, 0)
                    step(it, 1)
                step(NE // 2 - 1, 0, last=True)
                step(NE // 2 - 1, 1, last=True)
                for b in range(2):
                    pool.wait_ge(q[f"scattered{b}"], (l + 1) * (NE * 8))
                o = ov[l]
                n_ov = pool.value_load(ovinfo[0:1, NOV:NOV + 1], min_val=0, max_val=NOV)
                with pool.If(n_ov > 0):
                    with pool.Fori(0, n_ov) as i:
                        gather(o, 0, i, i + NE)
                        scatter(o, 0, i, i + NE)
                        pool.wait_ge(o["scattered0"], (i + 1) * 16)
                stage_end(pool, "pool")
                for j in range(NT):
                    w = TW[j]
                    if j >= 2:
                        pool.wait_ge(r["y_summed"], j - 1)
                    for k in range(2):
                        pool.dma_start(yl[j % 2][k][0:w, :], y_rows[l][k * T + j * P:k * T + j * P + w, :]
                                       ).then_inc(r[f"y_loaded{j % 2}"], 16)
                stage_end(pool, "pool")

            stage_end(pool, "pool")
            stage_end(pool, "pool")
            stage_end(pool, "pool")
            moe(0)
            stage_end(pool, "pool")
            stage_end(pool, "pool")
            stage_end(pool, "pool")
            moe(1)
            stage_end(pool, "pool")


_INS = ['x_prompt', 'x_sample', 'c_prompt', 'c_sample', 'state_pool_buf', 'state_conv_buf', 'state_lru_h',
        'w_mod', 'b_mod', 'norm_g', 'pool_w', 'pool_scale', 'lru_w_x', 'lru_b_x', 'lru_w_y', 'lru_b_y',
        'conv_w', 'conv_b', 'lru_w_a', 'lru_b_a', 'lru_w_i', 'lru_b_i', 'lru_lambda', 'lru_w_out', 'lru_b_out',
        'router_w', 'router_b', 'moe_w_gate', 'moe_w_up', 'moe_w_down', 'final_g']
_OUTS = [(1, 512, 1024), (8, 4, 1024), (1, 1, 15, 1024), (1, 8, 15, 1024), (1, 1, 3, 1024), (1, 8, 3, 1024),
         (1, 1, 1024), (1, 8, 1024)]


def kernel(**inputs):
    import numpy as _np
    import concourse.bacc as _bacc
    from concourse import mybir as _mybir
    from concourse.bass_utils import run_bass_kernel_spmd as _run

    nc = _bacc.Bacc("TRN2", target_bir_lowering=False, num_devices=1, dynamic_dma_scratch_size=8192)
    arrays, args = {}, []
    for name in _INS:
        a = _np.ascontiguousarray(inputs[name])
        arrays[f"in_{name}_dram"] = a
        args.append(nc.dram_tensor(f"in_{name}_dram", a.shape, _mybir.dt.from_np(a.dtype), kind="ExternalInput").ap())
    for i, shape in enumerate(_OUTS):
        args.append(nc.dram_tensor(f"out_{i}_dram", shape, _mybir.dt.float32, kind="ExternalOutput").ap())
    hybrid_trunk_kernel(nc, *args)
    r = _run(nc, [arrays], core_ids=[0])
    return tuple(r.results[0][f"out_{i}_dram"] for i in range(len(_OUTS)))
```

```python
from contextlib import ExitStack

import concourse.bass as bass
from concourse import mybir

P = 128
ALU = mybir.AluOpType
ACT = mybir.ActivationFunctionType
F32 = mybir.dt.float32
BF16 = mybir.dt.bfloat16
I32 = mybir.dt.int32
AX = mybir.AxisListType.X

POOL_WINDOWS = (2, 4, 8, 16)
LRU_C = 8.0
EPS = 1e-6
BIG = 1e30
GELU = ACT.Gelu_apprx_tanh


def hybrid_trunk_kernel(nc, x_prompt, x_sample, c_prompt, c_sample, state_pool_buf, state_conv_buf, state_lru_h,
                        w_mod, b_mod, norm_g, pool_w, pool_scale, lru_w_x, lru_b_x, lru_w_y, lru_b_y,
                        conv_w, conv_b, lru_w_a, lru_b_a, lru_w_i, lru_b_i, lru_lambda, lru_w_out, lru_b_out,
                        router_w, router_b, moe_w_gate, moe_w_up, moe_w_down, final_g,
                        y_prompt, y_sample, new_pool_prompt, new_pool_sample, new_conv_prompt, new_conv_sample,
                        new_h_prompt, new_h_sample):
    _, S, D = x_prompt.shape
    NB, SS, _ = x_sample.shape
    NS = NB * SS
    T = S + NS
    DC = D // P
    NQ = 1 + NB
    DEPTH = w_mod.shape[0]
    NM = 6 * DC
    PB = state_pool_buf.shape[2]
    CW = conv_w.shape[1]
    CH = CW - 1
    NE, F = moe_w_gate.shape[1], moe_w_gate.shape[3]
    FC = F // P
    NG = 4
    EG = NE // NG
    HALF = 512
    H2 = T // 2
    HP = S - H2
    NT = (T + P - 1) // P
    TW = [min(P, T - j * P) for j in range(NT)]
    NPT = S // P
    NOV = (2 * T - NE) // P
    NL = NE + NOV
    RING = 6
    UNIT = DC * HALF
    assert UNIT == FC * D and D == 2 * HALF and S == HALF and F == HALF
    MOD_ROT = w_mod.shape[2] // HALF // RING
    NOWHERE = 4000

    with ExitStack() as ctx:
        def sb(name, shape, dt=F32):
            return ctx.enter_context(nc.sbuf_tensor(name, shape, dt))

        def sem(name):
            return ctx.enter_context(nc.semaphore(name))

        WORK = 18688
        ring = [sb(f"ring{i}", [P, UNIT]) for i in range(RING)]
        xT = sb("xT", [P, DC, T])
        hT = sb("hT", [P, DC, T])
        work = sb("work", [P, WORK])
        modT = sb("modT", [P, NM, NQ])
        gainT = sb("gainT", [P, DEPTH, 2, DC, NQ])
        shiftT = sb("shiftT", [P, DEPTH, 2, DC, NQ])
        gateT = sb("gateT", [P, DEPTH, 2, DC, NQ])
        gbT = sb("gbT", [P, DC, NQ])
        bmodT = sb("bmodT", [P, DEPTH * NM])
        VEC = ["norm_g0", "norm_g1", "norm_g2", "norm_g3", "pool_scale", "final_g", "b_x", "b_y",
               "cw0", "cw1", "cw2", "cw3", "conv_b", "b_a", "b_i"]
        vecT = sb("vecT", [P, (len(VEC) + 2) * DC])
        rw = sb("rw", [P, DC, NE])
        rb = sb("rb", [P, NE])
        ident = sb("ident", [P, P])
        mean_w = sb("mean_w", [P, P])
        ones_b = sb("ones_b", [P, P], BF16)
        before_b = sb("before_b", [P, P], BF16)
        iota_e = sb("iota_e", [P, NE])
        row_number = sb("row_number", [P, 2 * NT])
        tile_at = sb("tile_at", [P, NL + 1])
        valid = sb("valid", [P, NT])
        invcnt = sb("invcnt", [P, 16])
        scT = sb("scT", [P, DC, NQ])
        poolT = work[:, 13312:13312 + DC * NB * PB].rearrange("p (c r) -> p c r", c=DC)
        rstd = work[:, WORK - T:WORK]
        convT = sb("convT", [P, DC, NB * CH])
        h0T = sb("h0T", [P, DC, NB])
        kdec = sb("kdec", [P, 2, DC])
        half_b = sb("half_b", [P, 2, DC])
        mrow = [work[0:NQ, 14336 + b * HALF:14336 + (b + 1) * HALF] for b in range(2)]
        small = sb("small", [P, DC * NS])
        small2 = sb("small2", [P, DC * NS])
        wts = sb("wts", [P, 2, NT])
        tokl = sb("tokl", [P, NL], I32)
        yrow = sb("yrow", [P, NL], I32)
        toks = [sb(f"toks{b}", [P, 1], I32) for b in range(2)]
        yrows = [sb(f"yrows{b}", [P, 1], I32) for b in range(2)]
        consts = sb("consts", [P, 2])
        spent = modT[:, :, :].rearrange("p m n -> p (m n)")
        conv_tail = spent[:, 0:DC * CH * NQ].rearrange("p (c n) -> p c n", c=DC)
        h_tail = spent[:, DC * CH * NQ:DC * (CH + 1) * NQ].rearrange("p (c n) -> p c n", c=DC)
        picks = sb("picks", [P, NT, NE], BF16)
        ovinfo = sb("ovinfo", [1, NOV + 1], I32)

        bank = [ctx.enter_context(nc.psum_tensor(f"bank{i}", [P, HALF], F32)) for i in range(8)]

        def vec(name, c=None):
            n = VEC.index(name) if name in VEC else {"lam": len(VEC), "b_out": len(VEC) + 1}[name]
            return vecT[:, n * DC:(n + 1) * DC] if c is None else vecT[:, n * DC + c:n * DC + c + 1]

        def area(at, n):
            return work[:, at:at + n], at + n

        xtok, at = area(0, NPT * D)
        xtok = xtok.rearrange("p (j d) -> p j d", j=NPT)
        xtok_s, at = area(at, D)
        rows, at = area(at, 5 * P)
        rows = rows.rearrange("p (n d) -> p n d", n=5)
        st_rows, at = area(at, 3 * D)
        st_rows = st_rows.rearrange("p (n d) -> p n d", n=3)
        craw, at = area(at, NQ * DC)
        pooledT, at = area(0, DC * T)
        pooledT = pooledT.rearrange("p (c t) -> p c t", c=DC)
        pw, at = area(at, 2 * NG * 256)
        pw = pw.rearrange("p (g k n) -> p g k n", g=NG, k=2)
        psum_a, at = area(at, 2 * S)
        psum_b, at = area(at, 2 * S)
        psum_a, psum_b = [x.rearrange("p (c t) -> p c t", c=2) for x in (psum_a, psum_b)]
        sbuf_n = 2 * NB * (PB + SS)
        spool_a, at = area(at, sbuf_n)
        spool_b, at = area(at, sbuf_n)
        spool_a, spool_b = [x.rearrange("p (c b t) -> p c b t", c=2, b=NB) for x in (spool_a, spool_b)]
        tail_rows, at = area(at, 2 * D)
        tail_rows = tail_rows.rearrange("p (n d) -> p n d", n=2)
        assert at <= 13312
        at = 0
        xg, xe, sg, hid, hidT, ys = [], [], [], [], [], []
        for b in range(2):
            for lst, n in ((xg, D), (xe, D), (sg, F), (hid, F), (hidT, F), (ys, D)):
                v, at = area(at, n)
                lst.append(v)
        xe = [x.rearrange("p (c t) -> p c t", c=DC) for x in xe]
        hidT = [x.rearrange("p (c t) -> p c t", c=FC) for x in hidT]
        route, at = area(at, 24 * NT * NE)
        route = route.rearrange("p (n j e) -> p n j e", n=24, e=NE)
        lg, ex, sel, one, two, val_a, val_b = (route[:, n] for n in range(7))
        flat = route.rearrange("p n j e -> p (n j e)")
        gsc, gbest = (flat[:, n * NT * NE:n * NT * NE + NT * NG].rearrange("p (j g) -> p j g", g=NG) for n in (7, 8))
        tmp_b = flat[:, 9 * NT * NE:9 * NT * NE + 32]
        cnt_e, ov_e, cum_e = (flat[:, (10 + n) * NT * NE:(10 + n) * NT * NE + NE] for n in range(3))
        end_e = flat[:, 17 * NT * NE:17 * NT * NE + NE]
        ov_f = flat[:, 13 * NT * NE:13 * NT * NE + NOV + 1]
        slot_f, tile_of, place_of = (flat[:, 14 * NT * NE + n * 16:14 * NT * NE + n * 16 + 2 * NT] for n in range(3))
        lt_f, lt_g = (flat[:, (15 + n) * NT * NE:(15 + n) * NT * NE + NL] for n in range(2))
        reached = flat[:, 18 * NT * NE:18 * NT * NE + 2 * NT * (NL + 1)].rearrange("p (i t) -> p i t", i=2 * NT)
        ov_le = flat[:, 22 * NT * NE:22 * NT * NE + NOV * NE].rearrange("p (t e) -> p t e", t=NOV)
        place_row, at = area(at, P)
        place_1h = work[:, 2 * D:2 * D + 2 * NT * P].rearrange("p (i s) -> p i s", i=2 * NT)
        rowof = work[:, 5 * D + 3 * F:5 * D + 3 * F + 2 * NT * NL].rearrange("p (i t) -> p i t", i=2 * NT)
        logitT = work[0:NE, D:D + T]
        assert 2 * NT * P <= 3 * F and 2 * NT * NL <= 3 * F
        htok = [ys[0], ys[1]]
        yl = [[work[:, (2 * j + k) * D:(2 * j + k + 1) * D] for k in range(2)] for j in range(NT)]
        ysum_c = [work[:, (2 * NT + b) * D:(2 * NT + b + 1) * D] for b in range(2)]
        ysum = [ys[0], ys[1]]
        assert at <= WORK
        at = 0
        e2, at = area(at, DC * T)
        xb = e2[:, 0:DC * (CH + S)].rearrange("p (c t) -> p c t", c=DC)
        e2 = e2.rearrange("p (c t) -> p c t", c=DC)
        xcT, at = area(at, DC * T)
        ybT, at = area(at, DC * T)
        xcT, ybT = [x.rearrange("p (c t) -> p c t", c=DC) for x in (xcT, ybT)]
        xbs, at = area(at, DC * NB * (CH + SS))
        xbs = xbs.rearrange("p (c b t) -> p c b t", c=DC, b=NB)
        NBLK, BW = lru_w_a.shape[1], lru_w_a.shape[2]
        BC = BW // P
        wai, at = area(at, 2 * NBLK * BC * BW)
        wai = wai.rearrange("p (w g k n) -> p w g k n", w=2, g=NBLK, k=BC)
        tanh_i = []
        for b in range(2):
            v, at = area(at, T)
            tanh_i.append(v)
        assert at <= WORK, at
        def xcT_rows(n):
            return xcT.rearrange("p c t -> p (c t)")[:, n * D:(n + 1) * D]

        aT = hT

        h_rows = [nc.dram_tensor(f"h_rows{l}", [T, D], F32).ap() for l in range(DEPTH)]
        y_rows = [nc.dram_tensor(f"y_rows{l}", [2 * T, D], F32).ap() for l in range(DEPTH)]

        slot_loaded = [sem(f"slot_loaded{i}") for i in range(RING)]
        gate_sem = sem("stage_gate")
        vec_step = sem("vec_step")
        act_step = sem("act_step")
        pool_step = sem("pool_step")
        in_loaded = sem("in_loaded")
        state_loaded = sem("state_loaded")
        small_loaded = sem("small_loaded")
        blocks_loaded = sem("blocks_loaded")
        poolw_loaded = sem("poolw_loaded")
        stored = sem("stored")
        copied = sem("copied")
        turned = sem("turned")
        turned_out = sem("turned_out")
        mod_used = sem("mod_used")
        mod_done = sem("mod_done")
        silu_c = sem("silu_c")
        mrow_copied = sem("mrow_copied")
        mod_evicted = sem("mod_evicted")
        sq_ready = sem("sq_ready")
        sq_summed = sem("sq_summed")
        mean_ready = sem("mean_ready")
        normed = sem("normed")
        pooled_ready = sem("pooled_ready")
        mixed = sem("mixed")
        mixed_added = sem("mixed_added")
        tail_turned = sem("tail_turned")
        x_done = sem("x_done")
        x_out = sem("x_out")
        lru_used = sem("lru_used")
        conv_done = sem("conv_done")
        gates_done = sem("gates_done")
        a_ready = sem("a_ready")
        gates_read = sem("gates_read")
        mult_done = sem("mult_done")
        waits_seen = sem("waits_seen")
        std_ready = sem("std_ready")
        power_ready = sem("power_ready")
        root_ready = sem("root_ready")
        lam_exp = sem("lam_exp")
        z_ready = sem("z_ready")
        o_done = sem("o_done")
        o_out = sem("o_out")
        o_added = sem("o_added")
        tails_ready = sem("tails_ready")
        yt_done = sem("yt_done")
        yt_out = sem("yt_out")
        y_loaded = [sem(f"y_loaded{j}") for j in range(NT)]
        yt_stored = [sem(f"yt_stored{b}") for b in range(2)]

        ROUTE = ["logits_done", "logits_out", "logits", "lmax", "ex", "count_in", "counts", "turn", "turn_out",
                 "rows_stored0", "rows_stored1", "places", "list_in", "list_out", "list_ready", "y_scaled",
                 "y_summed", "y_turned", "y_added"]
        TILE = ["toks_ready", "yrows_ready", "gathered0", "gathered1", "tx_done", "xe_copied", "g_done", "u_done", "silu_done",
                "hid_done", "th_done", "ht_copied", "y_done", "ys_copied", "scattered0", "scattered1"]
        rt = [{n: sem(f"r{l}_{n}") for n in ROUTE} for l in range(DEPTH)]
        ts = {n: sem(f"t_{n}") for n in TILE}
        ov = [{n: sem(f"o{l}_{n}") for n in TILE + ["loaded"]} for l in range(DEPTH)]

        block = ctx.enter_context(nc.Block())

        passed = {"pe": 0, "act": 0, "dve": 0, "pool": 0}

        def stage_end(eng, name):
            passed[name] += 1
            eng.drain().then_inc(gate_sem, 1)
            eng.wait_ge(gate_sem, 4 * passed[name])

        SMALL = ((b_mod.rearrange("l (r p) -> (l r) p", p=P), 0, 0), (norm_g.rearrange("l n (r p) -> (l n r) p", p=P), 1, 0),
                 (pool_scale, 1, 32), (final_g.rearrange("(o d) -> o d", o=1), 1, 40), (lru_b_x, 1, 48), (lru_b_y, 1, 56),
                 (conv_w[0], 1, 64), (conv_b, 2, 0), (lru_b_a, 2, 8), (lru_b_i, 2, 16), (lru_lambda, 2, 24),
                 (lru_b_out, 2, 32), (c_prompt, 3, 0), (c_sample, 3, DC))
        N_SMALL = len(SMALL) + 2

        def param_groups():
            return [[(rows[0:DEPTH * NM, 0, :], 0)], [(rows[0:96, 1, :], 0)], [(rows[0:40, 2, :], 0)],
                    [(rows[0:NQ * DC, 3, :], 0)]]

        def state_groups():
            def cut(n, h, c):
                return st_rows[0:h, n, c * P:(c + 1) * P]
            return [[(cut(0, NB * PB, c), (c % 4) * NB * PB) for c in range(4 * g, 4 * g + 4)] for g in range(2)] + [
                [(cut(1, NB * CH, c), c * NB * CH) for c in range(DC)], [(cut(2, NB, c), c * NB) for c in range(DC)]]

        def x_groups():
            return [[(xtok[:, j, c * P:(c + 1) * P], j * P) for j in range(NPT)] for c in range(DC)] + [
                [(xtok_s[0:NS, c * P:(c + 1) * P], c * NS) for c in range(DC)]]

        @block.sync
        def _(sp):
            rot = 0

            def wait_free(prev, s):
                if prev is None:
                    return
                kind, l = prev
                if kind == "mod":
                    sp.wait_ge(mod_used, RING * (MOD_ROT * (l + 1) - 1) + s + 1)
                elif kind == "moe":
                    b, part = s // 3, s % 3
                    name, n = (("g_done", 1), ("u_done", 1), ("y_done", 2))[part]
                    sp.wait_ge(ts[name], n * (NE * l + NE - 2 + b + 1))
                else:
                    sp.wait_ge(lru_used, s + 1)

            def load_mod(l, prev):
                src = w_mod[l].rearrange("(k p) n -> p k n", p=P)
                for r in range(MOD_ROT):
                    for s in range(RING):
                        if r == 0:
                            wait_free(prev, s)
                        else:
                            sp.wait_ge(mod_used, RING * (MOD_ROT * l + r - 1) + s + 1)
                        at = (r * RING + s) * HALF
                        sp.dma_start(ring[s][:, :].rearrange("p (k n) -> p k n", k=DC),
                                     src[:, :, at:at + HALF]).then_inc(slot_loaded[s], 16)

            def load_expert(l, e, b, loaded, wait):
                for part, w in enumerate((moe_w_gate, moe_w_up, moe_w_down)):
                    s = 3 * b + part
                    wait(s)
                    one = w[l][bass.ds(e, 1)]
                    src = one.rearrange("o (k p) n -> p (o k) n", p=P)
                    sp.dma_start(ring[s][:, :].rearrange("p (k n) -> p k n", k=src.shape[1]),
                                 src).then_inc(loaded(s), 16)

            def load_moe(l, prev):
                for b in range(2):
                    load_expert(l, b, b, lambda s: slot_loaded[s], lambda s: wait_free(prev, s))
                with sp.Fori(1, NE // 2) as it:
                    for b in range(2):
                        def used(s, b=b):
                            name, n = (("g_done", 1), ("u_done", 1), ("y_done", 2))[s % 3]
                            sp.wait_ge(ts[name], it * (2 * n) + n * (NE * l + b - 1))
                        load_expert(l, it * 2 + b, b, lambda s: slot_loaded[s], used)

            def load_overflow(l):
                sp.wait_ge(rt[l]["list_ready"], 2)
                n_ov = sp.value_load(ovinfo[0:1, NOV:NOV + 1], min_val=0, max_val=NOV)
                with sp.If(n_ov > 0):
                    sp.wait_ge(ts["y_done"], 2 * NE * (l + 1))
                    with sp.Fori(0, n_ov) as i:
                        e = sp.value_load(ovinfo[0:1, bass.ds(i, 1)], min_val=0, max_val=NE - 1)
                        load_expert(l, e, 0, lambda s: ov[l]["loaded"], lambda s: None)
                        sp.wait_ge(ov[l]["y_done"], (i + 1) * 2)
                        sp.sem_inc(waits_seen, 1)

            def load_lru(prev):
                s = 0
                for w in (lru_w_x, lru_w_y, lru_w_out):
                    for half in range(2):
                        if s == 4:
                            for j in range(NT):
                                sp.wait_ge(y_loaded[j], 32)
                        wait_free(prev, s)
                        sp.dma_start(ring[s][:, :].rearrange("p (k n) -> p k n", k=DC),
                                     w[0].rearrange("(k p) n -> p k n", p=P)[:, :, half * HALF:(half + 1) * HALF]
                                     ).then_inc(slot_loaded[s], 16)
                        s += 1

            sp.wait_ge(small_loaded, 16 * N_SMALL)
            load_mod(0, None)
            sp.dma_start(new_pool_sample[0][:, 0:PB - SS, :], state_pool_buf[0][:, SS:PB, :]).then_inc(copied, 16)
            load_mod(1, ("mod", 0))
            load_moe(0, ("mod", 1))
            load_overflow(0)
            load_lru(("moe", 0))
            load_moe(1, ("lru", 0))
            load_overflow(1)
            sp.wait_ge(copied, 16)

        MOE0_ROT = 2 * MOD_ROT
        LRU_ROT = MOE0_ROT + NE // 2
        MOE_ROT = [MOE0_ROT, LRU_ROT + 1]

        @block.tensor
        def _(pe):
            def turn_rows(groups, n):
                for parts in groups:
                    if n >= 4:
                        pe.wait_ge(turned_out, n - 3)
                    for src, col in parts:
                        w = src.shape[0]
                        last = pe.transpose(bank[n % 4][:, col:col + w], src, ident[0:w, 0:w])
                    last.then_inc(turned, 1)
                    n += 1
                return n

            def mod(l, r, ss=range(RING)):
                def turn(u):
                    pe.wait_ge(mrow_copied, u + 1)
                    for m in range(4):
                        at = ((u % RING) * 4 + m) * NQ
                        last = pe.transpose(bank[7][:, at:at + NQ], mrow[u % 2][:, m * P:(m + 1) * P], ident[0:NQ, 0:NQ])
                    return last

                for s in ss:
                    u = (l * MOD_ROT + r) * RING + s
                    pe.wait_ge(slot_loaded[s], 16 * (l * MOD_ROT + r + 1))
                    if u >= 2:
                        pe.wait_ge(mrow_copied, u - 1)
                    w = ring[s][:, :].rearrange("p (k n) -> p k n", k=DC)
                    for k in range(DC):
                        last = pe.matmul(bank[5 + u % 2][0:NQ, :], scT[:, k, :], w[:, k, :],
                                         start=(k == 0), stop=(k == DC - 1))
                    last.then_inc(mod_used, 1)
                    if s == 1 and u >= RING:
                        pe.wait_ge(mod_evicted, u // RING)
                    if s >= 1:
                        turn(u - 1)
                if s == RING - 1:
                    turn(u).then_inc(mod_done, 1)

            pe.wait_ge(pool_step, 3)
            pe.wait_ge(small_loaded, 16 * N_SMALL)
            n = turn_rows(param_groups(), 0)
            pe.wait_ge(silu_c, 1)
            mod(0, 0)
            pe.wait_ge(state_loaded, 16 * 3)
            n = turn_rows(state_groups(), n)
            pe.wait_ge(in_loaded, 16 * 2)
            n = turn_rows(x_groups(), n)
            mod(0, 1)
            stage_end(pe, "pe")

            def mean(n):
                pe.wait_ge(sq_summed, n + 1)
                for h in range(2):
                    pe.matmul(bank[h][:, 0:H2], mean_w[:, :], hT[:, 0, h * H2:(h + 1) * H2]).then_inc(mean_ready, 1)

            def tail(bk, srcs):
                for c in range(DC):
                    src = srcs(c)
                    w = src.shape[-1]
                    last = pe.transpose(bank[bk + c // 4][0:w, (c % 4) * P:(c % 4 + 1) * P], src, ident[:, :])
                last.then_inc(tail_turned, 1)

            def pool_mix():
                tail(3, lambda c: hT[:, c, S - PB:S])
                tail(0, lambda c: hT[:, c, S:T])
                mod(1, 0)
                pe.wait_ge(poolw_loaded, 16)
                for g in range(NG):
                    pe.wait_ge(pooled_ready, g + 1)
                    for m in range(2):
                        i = 2 * g + m
                        if i >= 2:
                            pe.wait_ge(mixed_added, i - 1)
                        for k in range(2):
                            pe.matmul(bank[i % 2][:, :], pw[:, g, k, m * P:(m + 1) * P], pooledT[:, 2 * g + k, 0:S],
                                      start=(k == 0), stop=(k == 1))
                        for k in range(2):
                            last = pe.matmul(bank[2][:, i * NS:(i + 1) * NS], pw[:, g, k, m * P:(m + 1) * P],
                                             pooledT[:, 2 * g + k, S:T], start=(k == 0), stop=(k == 1))
                        last.then_inc(mixed, 1)
                stage_end(pe, "pe")

            def tx(q, b, n, first, got):
                got(b)
                if not first:
                    pe.wait_ge(q["xe_copied"], n * 2)
                for c in range(DC):
                    last = pe.transpose(bank[4 + c // 4][:, (c % 4) * P:(c % 4 + 1) * P],
                                        xg[b][:, c * P:(c + 1) * P], ident[:, :])
                last.then_inc(q["tx_done"], 1)

            def widen(q, part, b, n, first, loaded, ks):
                if ks[0] == 0:
                    if part == 0:
                        pe.wait_ge(q["xe_copied"], n * 2 + 2)
                    loaded(3 * b + part)
                    if not first:
                        pe.wait_ge(q[("silu_done", "hid_done")[part]], n)
                w = ring[3 * b + part][:, :].rearrange("p (k n) -> p k n", k=DC)
                for k in ks:
                    last = pe.matmul(bank[part][:, :], xe[b][:, k, :], w[:, k, :], start=(k == 0), stop=(k == DC - 1))
                if ks[-1] == DC - 1:
                    last.then_inc(q[("g_done", "u_done")[part]], 1)

            def turn_hidden(q, b, n, first):
                pe.wait_ge(q["hid_done"], n + 1)
                if not first:
                    pe.wait_ge(q["ht_copied"], n * 2)
                for c in range(FC):
                    last = pe.transpose(bank[6 + c // 2][:, (c % 2) * P:(c % 2 + 1) * P], hid[b][:, c * P:(c + 1) * P],
                                        ident[:, :])
                last.then_inc(q["th_done"], 1)

            def down(q, b, n, first, loaded):
                pe.wait_ge(q["ht_copied"], n * 2 + 2)
                loaded(3 * b + 2)
                if not first:
                    pe.wait_ge(q["ys_copied"], n * 2)
                w = ring[3 * b + 2][:, :].rearrange("p (k n) -> p k n", k=FC)
                for half in range(2):
                    for k in range(FC):
                        last = pe.matmul(bank[2 + half][:, :], hidT[b][:, k, :], w[:, k, half * HALF:(half + 1) * HALF],
                                         start=(k == 0), stop=(k == FC - 1))
                    last.then_inc(q["y_done"], 1)

            def moe(l):
                r, q = rt[l], ts
                for c in range(DC):
                    for h in range(2):
                        last = pe.matmul(bank[2 + h][0:NE, 0:H2], rw[:, c, :], hT[:, c, h * H2:(h + 1) * H2],
                                         start=(c == 0), stop=(c == DC - 1))
                last.then_inc(r["logits_done"], 1)
                for j in range(NT):
                    w = TW[j]
                    for half in range(2):
                        i = 2 * j + half
                        if i >= 2:
                            pe.wait_ge(r["turn_out"], i - 1)
                        for c in range(4):
                            last = pe.transpose(bank[half][0:w, c * P:(c + 1) * P],
                                                hT[:, 4 * half + c, j * P:j * P + w], ident[:, :])
                        last.then_inc(r["turn"], 1)
                    if j == 0:
                        pe.wait_ge(r["logits_out"], 1)
                        for i in range(NT):
                            last = pe.transpose(bank[4][0:TW[i], i * NE:(i + 1) * NE], logitT[:, i * P:i * P + TW[i]],
                                                ident[0:NE, 0:NE])
                        last.then_inc(r["logits"], 1)
                if l == 0:
                    mod(1, 1, range(0, 1))
                pe.wait_ge(r["count_in"], 1)
                for j in range(NT):
                    for i in range(j):
                        pe.matmul(bank[3][:, j * NE:(j + 1) * NE], ones_b[:, :], picks[:, i, :], start=(i == 0), stop=False)
                    pe.matmul(bank[3][:, j * NE:(j + 1) * NE], before_b[:, :], picks[:, j, :], start=(j == 0), stop=True)
                for i in range(NT):
                    last = pe.matmul(bank[3][:, NT * NE:(NT + 1) * NE], ones_b[:, :], picks[:, i, :],
                                     start=(i == 0), stop=(i == NT - 1))
                last.then_inc(r["counts"], 1)
                if l == 0:
                    mod(1, 1, range(1, 2))
                pe.wait_ge(r["list_in"], 1)
                for i in range(2 * NT):
                    w = TW[i % NT]
                    last = pe.matmul(bank[2][:, 0:NL], place_1h[0:w, i, :], rowof[0:w, i, :],
                                     start=(i == 0), stop=(i == 2 * NT - 1))
                last.then_inc(r["list_out"], 1)
                if l == 0:
                    mod(1, 1, range(2, RING))
                stage_end(pe, "pe")

                rot0 = MOE_ROT[l]

                def step(it, b, first=False, last=False):
                    t = it * 2 + (b + NE * l)
                    nb, nit = 1 - b, it + b

                    def loaded(s):
                        pe.wait_ge(slot_loaded[s], (it + (rot0 + 1)) * 16)

                    def loaded_next(s):
                        pe.wait_ge(slot_loaded[s], (nit + (rot0 + 1)) * 16)

                    if not last:
                        tx(q, nb, t + 1, False,
                           lambda _: pe.wait_ge(q[f"gathered{nb}"], (nit + (l * (NE // 2) + 1)) * 16))
                    widen(q, 1, b, t, first, loaded, range(DC))
                    if not last:
                        widen(q, 0, nb, t + 1, False, loaded_next, range(DC // 2))
                    turn_hidden(q, b, t, first)
                    if not last:
                        widen(q, 0, nb, t + 1, False, loaded_next, range(DC // 2, DC))
                    down(q, b, t, first, loaded)

                tx(q, 0, l * NE, True, lambda _: pe.wait_ge(q["gathered0"], (l * (NE // 2) + 1) * 16))
                widen(q, 0, 0, l * NE, True, lambda s: pe.wait_ge(slot_loaded[s], (rot0 + 1) * 16), range(DC))
                step(0, 0, first=True)
                step(0, 1)
                with pe.Fori(1, NE // 2 - 1) as it:
                    step(it, 0)
                    step(it, 1)
                step(NE // 2 - 1, 0)
                step(NE // 2 - 1, 1, last=True)
                o = ov[l]
                n_ov = pe.value_load(ovinfo[0:1, NOV:NOV + 1], min_val=0, max_val=NOV)
                with pe.If(n_ov > 0):
                    with pe.Fori(0, n_ov) as i:
                        tx(o, 0, i, True, lambda _: pe.wait_ge(o["gathered0"], (i + 1) * 16))
                        for part in range(2):
                            widen(o, part, 0, i, True, lambda s: pe.wait_ge(o["loaded"], (i + 1) * 48), range(DC))
                        turn_hidden(o, 0, i, True)
                        down(o, 0, i, True, lambda s: None)
                stage_end(pe, "pe")
                for j in range(NT):
                    w = TW[j]
                    pe.wait_ge(r["y_summed"], j + 1)
                    if j >= 2:
                        pe.wait_ge(r["y_added"], j - 1)
                    for c in range(DC):
                        bk = 2 * (j % 2) + c // 4
                        last = pe.transpose(bank[bk][:, (c % 4) * P:(c % 4) * P + w],
                                            ysum_c[j % 2][0:w, c * P:(c + 1) * P], ident[0:w, 0:w])
                    last.then_inc(r["y_turned"], 1)
                stage_end(pe, "pe")

            def lru():
                for br in range(2):
                    for m in range(DC):
                        i = br * DC + m
                        s = 2 * br + m // 4
                        if m % 4 == 0:
                            pe.wait_ge(slot_loaded[s], 16 * (LRU_ROT + 1))
                        if i >= 2:
                            pe.wait_ge(x_out, i - 1)
                        w = ring[s][:, :].rearrange("p (k n) -> p k n", k=DC)[:, :, (m % 4) * P:(m % 4 + 1) * P]
                        for h in range(2):
                            for k in range(DC):
                                last = pe.matmul(bank[2 * (i % 2) + h][:, 0:H2], w[:, k, :], hT[:, k, h * H2:(h + 1) * H2],
                                                 start=(k == 0), stop=(k == DC - 1))
                        last.then_inc(x_done, 1)
                        if m % 4 == 3:
                            pe.drain().then_inc(lru_used, 1)
                pe.wait_ge(blocks_loaded, 32)
                pe.wait_ge(x_out, 2 * DC)
                pe.wait_ge(conv_done, 1)
                for g in range(NBLK):
                    for m in range(BC):
                        i = g * BC + m
                        if i >= 2:
                            pe.wait_ge(gates_read, i - 1)
                        for which in range(2):
                            for h in range(2):
                                for k in range(BC):
                                    last = pe.matmul(bank[4 * (i % 2) + 2 * which + h][:, 0:H2],
                                                     wai[:, which, g, k, m * P:(m + 1) * P],
                                                     xcT[:, BC * g + k, h * H2:(h + 1) * H2],
                                                     start=(k == 0), stop=(k == BC - 1))
                        last.then_inc(gates_done, 1)
                for s in (4, 5):
                    pe.wait_ge(slot_loaded[s], 16 * (LRU_ROT + 1))
                pe.wait_ge(z_ready, DC + 1)
                for m in range(DC):
                    s = 4 + m // 4
                    if m >= 2:
                        pe.wait_ge(o_out, m - 1)
                    w = ring[s][:, :].rearrange("p (k n) -> p k n", k=DC)[:, :, (m % 4) * P:(m % 4 + 1) * P]
                    for h in range(2):
                        for k in range(DC):
                            last = pe.matmul(bank[2 * (m % 2) + h][:, 0:H2], w[:, k, :], ybT[:, k, h * H2:(h + 1) * H2],
                                             start=(k == 0), stop=(k == DC - 1))
                    last.then_inc(o_done, 1)
                    if m % 4 == 3:
                        pe.drain().then_inc(lru_used, 1)
                pe.wait_ge(tails_ready, 1)
                tail(6, lambda c: conv_tail[:, c, :])
                tail(4, lambda c: h_tail[:, c, :])
                stage_end(pe, "pe")

            mean(0)
            stage_end(pe, "pe")
            pool_mix()
            mean(1)
            stage_end(pe, "pe")
            moe(0)
            mean(2)
            stage_end(pe, "pe")
            lru()
            mean(3)
            stage_end(pe, "pe")
            moe(1)
            mean(4)
            stage_end(pe, "pe")
            for j in range(NT):
                w = TW[j]
                for half in range(2):
                    i = 2 * j + half
                    if i >= 4:
                        pe.wait_ge(yt_out, i - 3)
                    for c in range(4):
                        last = pe.transpose(bank[i % 4][0:w, c * P:(c + 1) * P],
                                            hT[:, 4 * half + c, j * P:j * P + w], ident[:, :])
                    last.then_inc(yt_done, 1)

        @block.scalar
        def _(act):
            n_own = [0]
            n_stored = [0]

            def own(ins):
                n_own[0] += 1
                ins.then_inc(act_step, 1)
                act.wait_ge(act_step, n_own[0])

            def store(dst, src):
                n_stored[0] += 16
                act.dma_start(dst, src).then_inc(stored, 16)

            for src, n, r in SMALL:
                if len(src.shape) == 2 and src.shape[1] != P:
                    src = src.rearrange("n (r p) -> (n r) p", p=P)
                act.dma_start(rows[r:r + src.shape[0], n, :], src).then_inc(small_loaded, 16)
            act.dma_start(rw[:, :, :], router_w.rearrange("(k p) e -> p k e", p=P)).then_inc(small_loaded, 16)
            act.dma_start(rb[:, :], router_b.partition_broadcast(P)).then_inc(small_loaded, 16)
            act.dma_start(xtok, x_prompt[0].rearrange("(j p) d -> p j d", p=P)).then_inc(in_loaded, 16)
            act.dma_start(xtok_s[0:NS, :], x_sample.rearrange("b s d -> (b s) d")).then_inc(in_loaded, 16)
            act.dma_start(st_rows[0:NB * PB, 0, :], state_pool_buf[0].rearrange("b r d -> (b r) d")).then_inc(state_loaded, 16)
            act.dma_start(st_rows[0:NB * CH, 1, :], state_conv_buf[0].rearrange("b r d -> (b r) d")).then_inc(state_loaded, 16)
            act.dma_start(st_rows[0:NB, 2, :], state_lru_h[0]).then_inc(state_loaded, 16)
            act.wait_ge(lam_exp, 1)
            act.activation(small2[:, DC:2 * DC], small2[:, 0:DC], ACT.Exp).then_inc(lam_exp, 1)
            act.wait_ge(turned_out, 4)
            act.activation(scT[:, :, :].rearrange("p c n -> p n c"), craw.rearrange("p (n c) -> p n c", n=NQ),
                           ACT.Silu).then_inc(silu_c, 1)

            def mod_rows(l, r):
                for u in range((l * MOD_ROT + r) * RING, (l * MOD_ROT + r + 1) * RING):
                    act.wait_ge(mod_used, u + 1)
                    act.copy(mrow[u % 2], bank[5 + u % 2][0:NQ, :]).then_inc(mrow_copied, 1)

            mod_rows(0, 0)
            mod_rows(0, 1)
            stage_end(act, "act")
            act.dma_start(pw, pool_w[0].rearrange("g (k p) n -> p g k n", p=P)).then_inc(poolw_loaded, 16)

            def norm(n, layer, which, last=False):
                for c in range(DC):
                    act.activation(hT[:, c, :], xT[:, c, :], ACT.Square).then_inc(sq_ready, 1)
                for h in range(2):
                    act.wait_ge(mean_ready, 2 * n + h + 1)
                    act.activation(rstd[:, h * H2:(h + 1) * H2], bank[h][:, 0:H2], ACT.Sqrt, bias=consts[:, 0:1]
                                   ).then_inc(std_ready, 1)
                for c in range(DC):
                    act.wait_ge(normed, n * DC + c + 1)
                    if last:
                        act.activation(hT[:, c, :], hT[:, c, :], ACT.Copy, scale=vec("final_g", c))
                    else:
                        act.activation(hT[:, c, 0:S], hT[:, c, 0:S], ACT.Identity,
                                       scale=gainT[:, layer, which, c, 0:1], bias=shiftT[:, layer, which, c, 0:1])
                stage_end(act, "act")

            def tail_rows_out(w0, stores, n, bk=4):
                act.wait_ge(tail_turned, n)
                for half in range(2):
                    ins = act.copy(w0[:, half * HALF:(half + 1) * HALF], bank[bk + half][0:w0.shape[0], :])
                own(ins)
                for dst, lo, hi in stores:
                    store(dst, w0[lo:hi, :])

            def pool_mix():
                tail_rows_out(tail_rows[0:PB, 0, :], [(new_pool_prompt[0, 0], 0, PB)], 1, 3)
                tail_rows_out(tail_rows[0:NS, 1, :],
                              [(new_pool_sample[0, b, PB - SS:PB, :], b * SS, (b + 1) * SS) for b in range(NB)], 2, 0)
                mod_rows(1, 0)
                act.wait_ge(stored, n_stored[0])
                stage_end(act, "act")
            def moe(l):
                r, q = rt[l], ts
                act.wait_ge(r["logits_done"], 1)
                act.copy(logitT[:, 0:H2], bank[2][0:NE, 0:H2])
                act.copy(logitT[:, H2:T], bank[3][0:NE, 0:H2]).then_inc(r["logits_out"], 1)
                for j in range(NT):
                    if j == 1:
                        act.wait_ge(r["lmax"], 1)
                        act.activation(ex, lg, ACT.Exp).then_inc(r["ex"], 1)
                    w = TW[j]
                    if j >= 2:
                        act.wait_ge(r[f"rows_stored{j % 2}"], 16 * (j // 2))
                    for half in range(2):
                        act.wait_ge(r["turn"], 2 * j + half + 1)
                        ins = act.copy(htok[j % 2][0:w, half * HALF:(half + 1) * HALF], bank[half][0:w, :])
                        ins.then_inc(r["turn_out"], 1)
                    act.wait_ge(r["turn_out"], 2 * j + 2)
                    act.dma_start(h_rows[l][j * P:j * P + w, :], htok[j % 2][0:w, :]).then_inc(r[f"rows_stored{j % 2}"], 16)
                if l == 0:
                    mod_rows(1, 1)
                stage_end(act, "act")

                def xe_copy(q, b, n, used):
                    act.wait_ge(q["tx_done"], n + 1)
                    used()
                    act.copy(xe[b][:, 0:4, :], bank[4][:, :].rearrange("p (c t) -> p c t", c=4)).then_inc(q["xe_copied"], 1)

                def tile(q, b, n, first, x_next, ys_free):
                    act.wait_ge(q["g_done"], n + 1)
                    if not first:
                        act.wait_ge(q["hid_done"], n - 1)
                    act.activation(sg[b], bank[0][:, :], ACT.Silu).then_inc(q["silu_done"], 1)
                    x_next()
                    act.wait_ge(q["th_done"], n + 1)
                    if not first:
                        act.wait_ge(q["y_done"], n * 2 - 2)
                    act.copy(hidT[b][:, 0:2, :], bank[6][:, 0:2 * P].rearrange("p (c t) -> p c t", c=2)
                             ).then_inc(q["ht_copied"], 1)
                    act.wait_ge(q["y_done"], n * 2 + 1)
                    ys_free()
                    act.copy(ys[b][:, 0:HALF], bank[2][:, :]).then_inc(q["ys_copied"], 1)

                def step(it, b, first=False, last=False):
                    t = it * 2 + (b + NE * l)
                    nb = 1 - b

                    def x_next():
                        if not last:
                            xe_copy(q, nb, t + 1, lambda: None if first and b == 0 else act.wait_ge(q["u_done"], t))

                    tile(q, b, t, first, x_next,
                         lambda: None if first else act.wait_ge(q[f"scattered{b}"], it * 16 + l * (NE * 8)))

                xe_copy(q, 0, NE * l, lambda: None)
                step(0, 0, first=True)
                step(0, 1, first=True)
                with act.Fori(1, NE // 2 - 1) as it:
                    step(it, 0)
                    step(it, 1)
                step(NE // 2 - 1, 0)
                step(NE // 2 - 1, 1, last=True)
                o = ov[l]
                n_ov = act.value_load(ovinfo[0:1, NOV:NOV + 1], min_val=0, max_val=NOV)
                with act.If(n_ov > 0):
                    with act.Fori(0, n_ov) as i:
                        xe_copy(o, 0, i, lambda: None)
                        tile(o, 0, i, True, lambda: None, lambda: None)
                stage_end(act, "act")
                for j in range(NT):
                    w = TW[j]
                    for k in range(2):
                        act.dma_start(yl[j][k][0:w, :], y_rows[l][k * T + j * P:k * T + j * P + w, :]
                                      ).then_inc(y_loaded[j], 16)
                for j in range(NT):
                    w = TW[j]
                    act.wait_ge(y_loaded[j], 32 * (l + 1))
                    if j >= 2:
                        act.wait_ge(r["y_turned"], j - 1)
                    act.activation(ysum_c[j % 2][0:w, :], yl[j][0][0:w, :], ACT.Copy,
                                   scale=wts[0:w, 0, j:j + 1]).then_inc(r["y_scaled"], 1)
                stage_end(act, "act")

            def lru():
                for br in range(2):
                    for m in range(DC):
                        i = br * DC + m
                        act.wait_ge(x_done, i + 1)
                        b0, b1 = bank[2 * (i % 2)], bank[2 * (i % 2) + 1]
                        if br == 0:
                            b_x = vec("b_x", m)
                            act.activation(xb[:, m, CH:CH + H2], b0[:, 0:H2], ACT.Identity, bias=b_x)
                            act.activation(xb[:, m, CH + H2:CH + S], b1[:, 0:HP], ACT.Identity, bias=b_x)
                            act.activation(xbs[:, m, :, CH:CH + SS], b1[:, HP:H2].rearrange("p (b s) -> p b s", b=NB),
                                           ACT.Identity, bias=b_x).then_inc(x_out, 1)
                        else:
                            act.activation(ybT[:, m, 0:H2], b0[:, 0:H2], GELU, bias=vec("b_y", m))
                            act.activation(ybT[:, m, H2:T], b1[:, 0:H2], GELU, bias=vec("b_y", m)).then_inc(x_out, 1)
                for i in range(DC):
                    act.wait_ge(gates_done, i + 1)
                    if i >= 2:
                        act.wait_ge(mult_done, i - 1)
                    a = aT[:, i, :]
                    for h in range(2):
                        at = slice(h * H2, (h + 1) * H2)
                        act.activation(a[:, at], bank[4 * (i % 2) + h][:, 0:H2], ACT.Tanh, scale=0.5,
                                       bias=half_b[:, 0, i:i + 1])
                        ins = act.activation(tanh_i[i % 2][:, at], bank[4 * (i % 2) + 2 + h][:, 0:H2], ACT.Tanh, scale=0.5,
                                             bias=half_b[:, 1, i:i + 1])
                    ins.then_inc(gates_read, 1)
                    act.wait_ge(gates_read, i + 1)
                    act.activation(e2[:, i, :], a, ACT.Exp, scale=kdec[:, 1, i:i + 1], bias=kdec[:, 1, i:i + 1])
                    act.activation(a, a, ACT.Exp, scale=kdec[:, 0, i:i + 1], bias=kdec[:, 0, i:i + 1]).then_inc(a_ready, 1)
                for i in range(DC):
                    act.wait_ge(power_ready, i + 1)
                    act.activation(e2[:, i, :], e2[:, i, :], ACT.Sqrt, bias=consts[:, 1:2]).then_inc(root_ready, 1)
                for m in range(DC):
                    act.wait_ge(o_done, m + 1)
                    if m >= 2:
                        act.wait_ge(o_added, m - 1)
                    b0, b1 = bank[2 * (m % 2)], bank[2 * (m % 2) + 1]
                    gate, gb = gateT[:, 1, 0, m, 0:1], gbT[:, m, 0:1]
                    act.activation(tanh_i[m % 2][:, 0:H2], b0[:, 0:H2], ACT.Identity, scale=gate, bias=gb)
                    act.activation(tanh_i[m % 2][:, H2:S], b1[:, 0:HP], ACT.Identity, scale=gate, bias=gb)
                    act.copy(small2[:, m * NS:(m + 1) * NS], b1[:, HP:H2]).then_inc(o_out, 1)
                tail_rows_out(xcT_rows(0)[0:CH * NQ, :],
                              [(new_conv_prompt[0, 0], 0, CH),
                               (new_conv_sample[0].rearrange("b r d -> (b r) d"), CH, CH * NQ)], 3, 6)
                tail_rows_out(xcT_rows(1)[0:NQ, :], [(new_h_prompt[0], 0, 1), (new_h_sample[0], 1, NQ)], 4, 4)
                act.wait_ge(stored, n_stored[0])
                stage_end(act, "act")

            norm(0, 0, 0)
            pool_mix()
            norm(1, 0, 1)
            moe(0)
            act.dma_start(wai[:, 0], lru_w_a[0].rearrange("g (k p) n -> p g k n", p=P)).then_inc(blocks_loaded, 16)
            act.dma_start(wai[:, 1], lru_w_i[0].rearrange("g (k p) n -> p g k n", p=P)).then_inc(blocks_loaded, 16)
            norm(2, 1, 0)
            lru()
            norm(3, 1, 1)
            moe(1)
            norm(4, None, None, last=True)
            for j in range(NT):
                w = TW[j]
                if j >= 2:
                    act.wait_ge(yt_stored[j % 2], 16 * (j // 2))
                for half in range(2):
                    i = 2 * j + half
                    act.wait_ge(yt_done, i + 1)
                    act.copy(ysum[j % 2][0:w, half * HALF:(half + 1) * HALF], bank[i % 4][0:w, :]).then_inc(yt_out, 1)
                act.wait_ge(yt_out, 2 * j + 2)
                dst = y_prompt[0, j * P:(j + 1) * P, :] if w == P else y_sample.rearrange("b s d -> (b s) d")
                act.dma_start(dst, ysum[j % 2][0:w, :]).then_inc(yt_stored[j % 2], 16)
            for b in range(2):
                act.wait_ge(yt_stored[b], 16 * ((NT + 1 - b) // 2))

        @block.vector
        def _(dve):
            n_own = [0]

            def own(ins):
                n_own[0] += 1
                ins.then_inc(vec_step, 1)
                dve.wait_ge(vec_step, n_own[0])

            def tt(out, a, b, op):
                own(dve.tensor_tensor(out, a, b, op))

            def spread(a, n):
                return a.unsqueeze(len(a.shape)).to_broadcast(list(a.shape) + [n])

            dve.memset(mean_w[:, :], 1.0 / D)
            dve.memset(ones_b[:, :], 1.0)
            dve.memset(consts[:, 0:1], EPS)
            dve.memset(consts[:, 1:2], 0.25)
            own(dve.memset(valid[:, :], 1.0))
            n = 0

            def out_copy(dst, src):
                dve.tensor_copy(dst, src).then_inc(turned_out, 1)

            dve.wait_ge(turned, 1)
            out_copy(bmodT[:, :], bank[0][:, 0:DEPTH * NM])
            dve.wait_ge(turned, 2)
            out_copy(vecT[:, 0:96], bank[1][:, 0:96])
            dve.wait_ge(turned, 3)
            out_copy(vecT[:, 96:136], bank[2][:, 0:40])
            dve.wait_ge(turned, 4)
            out_copy(craw, bank[3][:, 0:NQ * DC])
            dve.wait_ge(turned_out, 4)
            lam = vec("lam")
            k0, k1 = kdec[:, 0, :], kdec[:, 1, :]
            z, z2 = small[:, 0:DC], small[:, DC:2 * DC]
            own(dve.tensor_scalar(z, lam, -1.0, None, ALU.mult))
            tt(z, z, lam, ALU.min)
            dve.tensor_copy(small2[:, 0:DC], z).then_inc(lam_exp, 1)
            dve.wait_ge(lam_exp, 2)
            own(dve.tensor_scalar(z2, small2[:, DC:2 * DC], 2.0, None, ALU.add))
            own(dve.reciprocal(z2, z2))
            tt(z, small2[:, DC:2 * DC], z2, ALU.mult)
            tt(z2, z, z, ALU.mult)
            own(dve.tensor_scalar(k0, z2, 1.0 / 19, 1.0 / 17, ALU.mult, ALU.add))
            for d in (15, 13, 11, 9, 7, 5, 3, 1):
                tt(k0, k0, z2, ALU.mult)
                own(dve.tensor_scalar(k0, k0, 1.0 / d, None, ALU.add))
            tt(k0, k0, z, ALU.mult)
            own(dve.tensor_scalar(z2, lam, -1.0, 0.0, ALU.mult, ALU.max))
            own(dve.scalar_tensor_tensor(k0, k0, 2.0, z2, ALU.mult, ALU.add))
            own(dve.tensor_scalar(k0, k0, -LRU_C / 2, None, ALU.mult))
            dve.tensor_scalar(k1, k0, 2.0, None, ALU.mult)
            dve.tensor_scalar(half_b[:, 0, :], vec("b_a"), 0.5, None, ALU.mult)
            dve.tensor_scalar(half_b[:, 1, :], vec("b_i"), 0.5, None, ALU.mult)
            dve.wait_ge(pool_step, 5)
            own(dve.tensor_copy(invcnt[:, :], iota_e[:, 0:16]))
            own(dve.tensor_scalar(invcnt[:, :], invcnt[:, :], 1.0, None, ALU.add))
            own(dve.reciprocal(invcnt[:, :], invcnt[:, :]))

            def mod_out(l, r):
                n = l * MOD_ROT + r
                m0, m1 = r * RING * 4, (r + 1) * RING * 4
                dve.wait_ge(mod_done, n + 1)
                dve.tensor_tensor(modT[:, m0:m1, :], bank[7][:, 0:RING * 4 * NQ].rearrange("p (m n) -> p m n", n=NQ),
                                  spread(bmodT[:, l * NM + m0:l * NM + m1], NQ), ALU.add).then_inc(mod_evicted, 1)
                dve.wait_ge(mod_evicted, n + 1)

            def adaln(l):
                for which in range(2):
                    m0 = 3 * DC * which
                    g = spread(vecT[:, (2 * l + which) * DC:(2 * l + which + 1) * DC], NQ)
                    own(dve.scalar_tensor_tensor(gainT[:, l, which], modT[:, m0 + DC:m0 + 2 * DC, :], 1.0, g,
                                                 ALU.add, ALU.mult))
                    own(dve.tensor_copy(shiftT[:, l, which], modT[:, m0:m0 + DC, :]))
                    own(dve.tensor_copy(gateT[:, l, which], modT[:, m0 + 2 * DC:m0 + 3 * DC, :]))
                if l == 0:
                    tt(gateT[:, 0, 0], gateT[:, 0, 0], spread(vec("pool_scale"), NQ), ALU.mult)
                else:
                    tt(gbT[:, :, :], gateT[:, 1, 0], spread(vec("b_out"), NQ), ALU.mult)

            mod_out(0, 0)
            for g in range(2):
                dve.wait_ge(turned, 5 + g)
                out_copy(poolT[:, 4 * g:4 * g + 4, :], bank[g][:, 0:4 * NB * PB].rearrange("p (c r) -> p c r", c=4))
            dve.wait_ge(turned, 7)
            out_copy(convT[:, :, :], bank[2][:, 0:DC * NB * CH].rearrange("p (c r) -> p c r", c=DC))
            dve.wait_ge(turned, 8)
            out_copy(h0T[:, :, :], bank[3][:, 0:DC * NB].rearrange("p (c r) -> p c r", c=DC))
            for c in range(DC):
                dve.wait_ge(turned, 9 + c)
                out_copy(xT[:, c, 0:S], bank[c % 4][:, :])
            dve.wait_ge(turned, 9 + DC)
            out_copy(xT[:, :, S:T], bank[0][:, 0:DC * NS].rearrange("p (c t) -> p c t", c=DC))
            mod_out(0, 1)
            adaln(0)
            stage_end(dve, "dve")

            def seqs(a):
                return a.rearrange("p c (b s) -> p c b s", b=NB)

            def norm(n, layer, which, last=False):
                for c in range(1, DC):
                    dve.wait_ge(sq_ready, n * DC + c + 1)
                    if c < DC - 1:
                        tt(hT[:, 0, :], hT[:, 0, :], hT[:, c, :], ALU.add)
                    else:
                        dve.tensor_tensor(hT[:, 0, :], hT[:, 0, :], hT[:, c, :], ALU.add).then_inc(sq_summed, 1)
                for h in range(2):
                    dve.wait_ge(std_ready, 2 * n + h + 1)
                    own(dve.reciprocal(rstd[:, h * H2:(h + 1) * H2], rstd[:, h * H2:(h + 1) * H2]))
                for c in range(DC):
                    dve.tensor_tensor(hT[:, c, :], xT[:, c, :], rstd, ALU.mult).then_inc(normed, 1)
                if not last:
                    dve.wait_ge(normed, (n + 1) * DC)
                    h = seqs(hT[:, :, S:T])
                    tt(h, h, spread(gainT[:, layer, which, :, 1:NQ], SS), ALU.mult)
                    tt(h, h, spread(shiftT[:, layer, which, :, 1:NQ], SS), ALU.add)
                stage_end(dve, "dve")

            def add_samples(src, layer, which):
                t = small[:, :].rearrange("p (c t) -> p c t", c=DC)
                tt(seqs(t), seqs(src), spread(gateT[:, layer, which, :, 1:NQ], SS), ALU.mult)
                tt(xT[:, :, S:T], xT[:, :, S:T], t, ALU.add)

            def pool_mix():
                for g, w in enumerate(POOL_WINDOWS):
                    h = hT[:, 2 * g:2 * g + 2, 0:S]
                    src, dst, d = h, psum_a, 1
                    s_src, s_dst = spool_a, spool_b
                    dve.tensor_copy(spool_a[:, :, :, 0:PB],
                                    poolT[:, 2 * g:2 * g + 2, :].rearrange("p c (b r) -> p c b r", b=NB))
                    own(dve.tensor_copy(spool_a[:, :, :, PB:PB + SS], seqs(hT[:, 2 * g:2 * g + 2, S:T])))
                    while d < w:
                        dve.tensor_copy(dst[:, :, 0:d], src[:, :, 0:d])
                        dve.tensor_tensor(dst[:, :, d:S], src[:, :, d:S], src[:, :, 0:S - d], ALU.add)
                        tt(s_dst[:, :, :, 2 * d - 1:PB + SS], s_src[:, :, :, 2 * d - 1:PB + SS],
                           s_src[:, :, :, d - 1:PB + SS - d], ALU.add)
                        src, dst = dst, (psum_b if dst is psum_a else psum_a)
                        s_src, s_dst = s_dst, s_src
                        d *= 2
                    out = pooledT[:, 2 * g:2 * g + 2, :]
                    cnt = invcnt[:, 0:w - 1].unsqueeze(1).to_broadcast([P, 2, w - 1])
                    tt(dst[:, :, 0:w - 1], src[:, :, 0:w - 1], cnt, ALU.mult)
                    dve.tensor_tensor(out[:, :, 0:w - 1], dst[:, :, 0:w - 1], h[:, :, 0:w - 1], ALU.subtract)
                    dve.scalar_tensor_tensor(out[:, :, w - 1:S], src[:, :, w - 1:S], 1.0 / w, h[:, :, w - 1:S],
                                             ALU.mult, ALU.subtract)
                    own(dve.tensor_scalar(s_dst[:, :, :, PB:PB + SS], s_src[:, :, :, PB:PB + SS], 1.0 / w, None, ALU.mult))
                    dve.tensor_tensor(seqs(out[:, :, S:T]), s_dst[:, :, :, PB:PB + SS],
                                      seqs(hT[:, 2 * g:2 * g + 2, S:T]), ALU.subtract).then_inc(pooled_ready, 1)
                    dve.wait_ge(pooled_ready, g + 1)
                mod_out(1, 0)
                for i in range(DC):
                    dve.wait_ge(mixed, i + 1)
                    dve.scalar_tensor_tensor(xT[:, i, 0:S], bank[i % 2][:, :], gateT[:, 0, 0, i, 0:1], xT[:, i, 0:S],
                                             ALU.mult, ALU.add).then_inc(mixed_added, 1)
                add_samples(bank[2][:, 0:DC * NS].rearrange("p (c t) -> p c t", c=DC), 0, 0)
                stage_end(dve, "dve")

            def first_max(out, vals, n, shape):
                rows_n = shape
                top = tmp_b[:, 0:rows_n]
                own(dve.tensor_reduce(top, vals, AX, ALU.max))
                tt(out, vals, spread(top, n), ALU.is_ge)
                it = iota_e[:, 0:n].unsqueeze(1).to_broadcast([P, rows_n, n])
                own(dve.scalar_tensor_tensor(out, out, -64.0, it, ALU.mult, ALU.add))
                own(dve.tensor_reduce(top, out, AX, ALU.min))
                tt(out, out, spread(top, n), ALU.is_equal)

            def moe(l):
                r, q = rt[l], ts
                own(dve.memset(lg, 0.0))
                dve.wait_ge(r["logits"], 1)
                own(dve.tensor_copy(lg[:, 0:NPT, :], bank[4][:, 0:NPT * NE].rearrange("p (j e) -> p j e", j=NPT)))
                own(dve.tensor_copy(lg[0:TW[-1], NPT, :], bank[4][0:TW[-1], NPT * NE:NT * NE]))
                own(dve.tensor_reduce(tmp_b[:, 0:NT], lg, AX, ALU.max))
                dve.tensor_tensor(lg, lg, spread(tmp_b[:, 0:NT], NE), ALU.subtract).then_inc(r["lmax"], 1)
                dve.wait_ge(r["ex"], 1)
                own(dve.tensor_reduce(tmp_b[:, 0:NT], ex, AX, ALU.add))
                own(dve.reciprocal(tmp_b[:, 0:NT], tmp_b[:, 0:NT]))
                tt(ex, ex, spread(tmp_b[:, 0:NT], NE), ALU.mult)
                tt(sel, ex, rb[:, :].unsqueeze(1).to_broadcast([P, NT, NE]), ALU.add)
                s4 = sel.rearrange("p j (g e) -> p (j g) e", g=NG)
                hi, lo = [x.rearrange("p j (g e) -> p (j g) e", g=NG) for x in (val_a, val_b)]
                tt(hi[:, :, 0:2], s4[:, :, 0:2], s4[:, :, 2:4], ALU.max)
                tt(lo[:, :, 0:2], s4[:, :, 0:2], s4[:, :, 2:4], ALU.min)
                tt(hi[:, :, 2:3], hi[:, :, 0:1], hi[:, :, 1:2], ALU.max)
                tt(hi[:, :, 3:4], hi[:, :, 0:1], hi[:, :, 1:2], ALU.min)
                tt(lo[:, :, 2:3], lo[:, :, 0:1], lo[:, :, 1:2], ALU.max)
                tt(lo[:, :, 3:4], lo[:, :, 2:3], hi[:, :, 3:4], ALU.max)
                gs = gsc.rearrange("p j g -> p (j g)")
                tt(gs.unsqueeze(2), lo[:, :, 3:4], hi[:, :, 2:3], ALU.add)
                first_max(gbest, gsc, NG, NT)
                own(dve.tensor_scalar(gbest, gbest, BIG, -BIG, ALU.mult, ALU.add))
                tt(s4, s4, spread(gbest.rearrange("p j g -> p (j g)"), EG), ALU.add)
                first_max(one, sel, NE, NT)
                own(dve.scalar_tensor_tensor(sel, one, -3 * BIG, sel, ALU.mult, ALU.add))
                first_max(two, sel, NE, NT)
                picked, vals, in_places = (route[:, n:n + 2].rearrange("p n j e -> p n (j e)") for n in (3, 5, 1))
                both = lambda a: a.rearrange("p n (j e) -> p (n j) e", e=NE)
                twice = lambda a: a.rearrange("p j e -> p (j e)").unsqueeze(1).to_broadcast([P, 2, NT * NE])
                tt(vals, picked, twice(ex), ALU.mult)
                own(dve.tensor_reduce(wts[:, :, :].rearrange("p n j -> p (n j)"), both(vals), AX, ALU.add))
                tt(tmp_b[:, 0:NT], wts[:, 0, :], wts[:, 1, :], ALU.add)
                own(dve.reciprocal(tmp_b[:, 0:NT], tmp_b[:, 0:NT]))
                for k in range(2):
                    tt(wts[:, k, :], wts[:, k, :], tmp_b[:, 0:NT], ALU.mult)
                tt(val_a, one, two, ALU.add)
                dve.tensor_tensor(picks[:, :, :], val_a, spread(valid[:, :], NE), ALU.mult).then_inc(r["count_in"], 1)
                dve.wait_ge(r["counts"], 1)
                own(dve.tensor_copy(sel, bank[3][:, 0:NT * NE].rearrange("p (j e) -> p j e", j=NT)))
                own(dve.tensor_copy(cnt_e, bank[3][:, NT * NE:(NT + 1) * NE]))
                own(dve.tensor_scalar(ov_e, cnt_e, float(P), None, ALU.is_gt))
                for k in range(2, (T + P - 1) // P):
                    own(dve.tensor_scalar(cum_e, cnt_e, float(k * P), None, ALU.is_gt))
                    tt(ov_e, ov_e, cum_e, ALU.add)
                own(dve.tensor_scalar(cnt_e, cnt_e, 0.0, 1.0, ALU.mult, ALU.add))
                own(dve.tensor_tensor_scan(cum_e, cnt_e, ov_e, 0.0, ALU.mult, ALU.add))
                tt(end_e, cum_e, ov_e, ALU.subtract)
                tt(end_e, end_e, iota_e[:, :], ALU.subtract)
                own(dve.tensor_scalar(end_e, end_e, float(NE - 1), float(P), ALU.add, ALU.mult))
                own(dve.tensor_scalar(val_a, sel, float(P), None, ALU.is_ge))
                tt(val_a, val_a, end_e.unsqueeze(1).to_broadcast([P, NT, NE]), ALU.mult)
                tt(val_a, val_a, sel, ALU.add)
                own(dve.tensor_scalar(end_e, iota_e[:, :], float(P), None, ALU.mult))
                tt(val_a, val_a, end_e.unsqueeze(1).to_broadcast([P, NT, NE]), ALU.add)
                tt(in_places, picked, twice(val_a), ALU.mult)
                own(dve.tensor_reduce(slot_f, both(in_places), AX, ALU.add))
                tt(reached, spread(slot_f, NL + 1), tile_at[:, :].unsqueeze(1).to_broadcast([P, 2 * NT, NL + 1]), ALU.is_ge)
                own(dve.tensor_reduce(tile_of, reached[:, :, 0:NL], AX, ALU.add))
                own(dve.scalar_tensor_tensor(place_of, tile_of, -float(P), slot_f, ALU.mult, ALU.add))
                dve.wait_ge(r["places"], 1)
                dve.tensor_tensor(place_1h, spread(place_of, P), place_row.unsqueeze(1).to_broadcast([P, 2 * NT, P]),
                                  ALU.is_equal)
                tt(rowof, reached[:, :, 0:NL], reached[:, :, 1:NL + 1], ALU.subtract)
                tt(rowof, rowof, spread(row_number[:, :], NL), ALU.mult)
                dve.drain().then_inc(r["list_in"], 1)
                dve.wait_ge(r["list_out"], 1)
                own(dve.tensor_scalar(lt_g, bank[2][:, 0:NL], 0.0, float(NOWHERE + 1), ALU.is_le, ALU.mult))
                own(dve.scalar_tensor_tensor(lt_f, bank[2][:, 0:NL], -1.0, lt_g, ALU.add, ALU.add))
                own(dve.tensor_copy(yrow[:, :], lt_f))
                own(dve.tensor_scalar(lt_g, lt_f, float(T), float(-T), ALU.is_ge, ALU.mult))
                tt(lt_f, lt_f, lt_g, ALU.add)
                own(dve.tensor_copy(tokl[:, :], lt_f))
                dve.drain().then_inc(r["list_ready"], 1)
                tt(ov_le, cum_e.unsqueeze(1).to_broadcast([P, NOV, NE]), spread(iota_e[:, 0:NOV], NE), ALU.is_le)
                own(dve.tensor_reduce(ov_f[:, 0:NOV], ov_le, AX, ALU.add))
                own(dve.tensor_copy(ov_f[:, NOV:NOV + 1], cum_e[:, NE - 1:NE]))
                own(dve.tensor_copy(ovinfo[:, :], ov_f[0:1, :]))
                dve.drain().then_inc(r["list_ready"], 1)
                if l == 0:
                    mod_out(1, 1)
                    adaln(1)
                stage_end(dve, "dve")

                def xe_copy(q, b, n, used):
                    dve.wait_ge(q["tx_done"], n + 1)
                    used()
                    dve.tensor_copy(xe[b][:, 4:8, :], bank[5][:, :].rearrange("p (c t) -> p c t", c=4)
                                    ).then_inc(q["xe_copied"], 1)

                def tile(q, b, n, first, x_next, ys_free):
                    x_next()
                    dve.wait_ge(q["silu_done"], n + 1)
                    dve.wait_ge(q["u_done"], n + 1)
                    if not first:
                        dve.wait_ge(q["th_done"], n - 1)
                    dve.tensor_tensor(hid[b], sg[b], bank[1][:, :], ALU.mult).then_inc(q["hid_done"], 1)
                    dve.wait_ge(q["th_done"], n + 1)
                    if not first:
                        dve.wait_ge(q["y_done"], n * 2 - 2)
                    dve.tensor_copy(hidT[b][:, 2:4, :], bank[7][:, 0:2 * P].rearrange("p (c t) -> p c t", c=2)
                                    ).then_inc(q["ht_copied"], 1)
                    dve.wait_ge(q["y_done"], n * 2 + 2)
                    ys_free()
                    dve.tensor_copy(ys[b][:, HALF:D], bank[3][:, :]).then_inc(q["ys_copied"], 1)

                def step(it, b, first=False, last=False):
                    t = it * 2 + (b + NE * l)
                    nb = 1 - b

                    def x_next():
                        if not last:
                            xe_copy(q, nb, t + 1, lambda: None if first and b == 0 else dve.wait_ge(q["u_done"], t))

                    tile(q, b, t, first, x_next,
                         lambda: None if first else dve.wait_ge(q[f"scattered{b}"], it * 16 + l * (NE * 8)))

                xe_copy(q, 0, NE * l, lambda: None)
                step(0, 0, first=True)
                step(0, 1, first=True)
                with dve.Fori(1, NE // 2 - 1) as it:
                    step(it, 0)
                    step(it, 1)
                step(NE // 2 - 1, 0)
                step(NE // 2 - 1, 1, last=True)
                o = ov[l]
                n_ov = dve.value_load(ovinfo[0:1, NOV:NOV + 1], min_val=0, max_val=NOV)
                with dve.If(n_ov > 0):
                    with dve.Fori(0, n_ov) as i:
                        xe_copy(o, 0, i, lambda: None)
                        tile(o, 0, i, True, lambda: None, lambda: None)
                stage_end(dve, "dve")
                def add_tile(j):
                    w = TW[j]
                    dve.wait_ge(r["y_turned"], j + 1)
                    bks = [bank[2 * (j % 2) + h][:, :].rearrange("p (c t) -> p c t", c=4) for h in range(2)]
                    if w == P:
                        for c in range(DC):
                            ins = dve.scalar_tensor_tensor(xT[:, c, j * P:(j + 1) * P], bks[c // 4][:, c % 4, :],
                                                           gateT[:, l, 1, c, 0:1], xT[:, c, j * P:(j + 1) * P],
                                                           ALU.mult, ALU.add)
                        ins.then_inc(r["y_added"], 1)
                    else:
                        s2 = small2[:, :].rearrange("p (c t) -> p c t", c=DC)
                        for h in range(2):
                            own(dve.tensor_copy(s2[:, 4 * h:4 * h + 4, :], bks[h][:, :, 0:w]))
                        add_samples(s2, l, 1)

                for j in range(NT):
                    w = TW[j]
                    dve.wait_ge(r["y_scaled"], j + 1)
                    dve.scalar_tensor_tensor(ysum_c[j % 2][0:w, :], yl[j][1][0:w, :], wts[0:w, 1, j:j + 1],
                                             ysum_c[j % 2][0:w, :], ALU.mult, ALU.add).then_inc(r["y_summed"], 1)
                    if j >= 1:
                        add_tile(j - 1)
                add_tile(NT - 1)
                stage_end(dve, "dve")

            def lru():
                xs = [small[:, :].rearrange("p (c t) -> p c t", c=DC), small2[:, :].rearrange("p (c t) -> p c t", c=DC)]
                dve.memset(xb[:, :, 0:CH], 0.0)
                own(dve.tensor_copy(xbs[:, :, :, 0:CH], convT[:, :, :].rearrange("p c (b r) -> p c b r", b=NB)))
                for m in range(DC):
                    dve.wait_ge(x_out, m + 1)
                    own(dve.tensor_scalar(xcT[:, m, 0:S], xb[:, m, 0:S], vec("cw0", m), vec("conv_b", m), ALU.mult, ALU.add))
                    for k in range(1, CW):
                        ins = dve.scalar_tensor_tensor(xcT[:, m, 0:S], xb[:, m, k:k + S], vec(f"cw{k}", m),
                                                       xcT[:, m, 0:S], ALU.mult, ALU.add)
                        own(ins)
                xc_s = seqs(xcT[:, :, S:T])
                t_s = seqs(xs[0])
                tt(xc_s, xbs[:, :, :, 0:SS], spread(spread(vec("cw0"), NB), SS), ALU.mult)
                for k in range(1, CW):
                    tt(t_s, xbs[:, :, :, k:k + SS], spread(spread(vec(f"cw{k}"), NB), SS), ALU.mult)
                    tt(xc_s, xc_s, t_s, ALU.add)
                tt(xcT[:, :, S:T], xcT[:, :, S:T], spread(vec("conv_b"), NS), ALU.add)
                own(dve.tensor_copy(conv_tail[:, :, 0:CH], xb[:, :, S:S + CH]))
                own(dve.tensor_copy(conv_tail[:, :, CH:CH * NQ].rearrange("p c (b r) -> p c b r", b=NB),
                                    xbs[:, :, :, SS:SS + CH]))
                dve.drain().then_inc(conv_done, 1)
                for i in range(DC):
                    g = i // BC
                    dve.wait_ge(gates_done, BC * (g + 1))
                    dve.wait_ge(gates_read, i + 1)
                    dve.scalar_tensor_tensor(xcT[:, i, :], tanh_i[i % 2], 1.0, xcT[:, i, :], ALU.add, ALU.mult
                                             ).then_inc(mult_done, 1)
                    dve.wait_ge(a_ready, i + 1)
                    dve.tensor_scalar(e2[:, i, :], e2[:, i, :], 1.0, -0.25, ALU.min, ALU.mult).then_inc(power_ready, 1)
                dve.wait_ge(mult_done, DC)
                for i in range(DC):
                    dve.wait_ge(root_ready, i + 1)
                    own(dve.memset(e2[:, i, 0:1], 0.5))
                    tt(xcT[:, i, :], xcT[:, i, :], e2[:, i, :], ALU.mult)
                    own(dve.tensor_tensor_scan(e2[:, i, 0:S], aT[:, i, 0:S], xcT[:, i, 0:S], 0.0, ALU.mult, ALU.add))
                    own(dve.tensor_copy(h_tail[:, i, 0:1], e2[:, i, S - 1:S]))
                    dve.wait_ge(x_out, DC + i + 1)
                    dve.tensor_tensor(ybT[:, i, 0:S], e2[:, i, 0:S], ybT[:, i, 0:S], ALU.mult).then_inc(z_ready, 1)
                a_s, b_s = seqs(aT[:, :, S:T]), seqs(xcT[:, :, S:T])
                prev = h0T[:, :, :]
                for s in range(SS):
                    cur = seqs(xs[1])[:, :, :, s]
                    tt(cur, a_s[:, :, :, s], prev, ALU.mult)
                    tt(cur, cur, b_s[:, :, :, s], ALU.add)
                    prev = cur
                own(dve.tensor_copy(h_tail[:, :, 1:NQ], prev))
                dve.tensor_tensor(ybT[:, :, S:T], xs[1], ybT[:, :, S:T], ALU.mult).then_inc(z_ready, 1)
                dve.drain().then_inc(tails_ready, 1)
                for m in range(DC):
                    dve.wait_ge(o_out, m + 1)
                    dve.tensor_tensor(xT[:, m, 0:S], xT[:, m, 0:S], tanh_i[m % 2][:, 0:S], ALU.add).then_inc(o_added, 1)
                add_samples(xs[1], 1, 0)
                tt(seqs(xT[:, :, S:T]), seqs(xT[:, :, S:T]), spread(gbT[:, :, 1:NQ], SS), ALU.add)
                stage_end(dve, "dve")

            norm(0, 0, 0)
            pool_mix()
            norm(1, 0, 1)
            moe(0)
            norm(2, 1, 0)
            lru()
            norm(3, 1, 1)
            moe(1)
            norm(4, None, None, last=True)

        @block.gpsimd
        def _(pool):
            def own(ins, sem_=pool_step):
                own.n += 1
                ins.then_inc(pool_step, 1)
                pool.wait_ge(pool_step, own.n)
            own.n = 0
            own(pool.memset(ident[:, :], 0.0))
            own(pool.affine_select(ident[:, :], ident[:, :], [[-1, P]], ALU.not_equal, 1.0, base=0, channel_multiplier=1))
            own(pool.memset(before_b[:, :], 1.0))
            own(pool.affine_select(before_b[:, :], before_b[:, :], [[1, P]], ALU.is_gt, 0.0, base=0, channel_multiplier=-1))
            own(pool.iota(iota_e[:, :], [[1, NE]], base=0, channel_multiplier=0, allow_small_or_imprecise_dtypes=True))
            own(pool.iota(row_number[:, 0:NT], [[P, NT]], base=1, channel_multiplier=1, allow_small_or_imprecise_dtypes=True))
            own(pool.iota(row_number[:, NT:2 * NT], [[P, NT]], base=T + 1, channel_multiplier=1,
                          allow_small_or_imprecise_dtypes=True))
            own(pool.iota(tile_at[:, :], [[P, NL + 1]], base=0, channel_multiplier=0, allow_small_or_imprecise_dtypes=True))
            pool.wait_ge(vec_step, 1)
            own(pool.affine_select(valid[:, :], valid[:, :], [[-P, NT]], ALU.is_gt, 0.0, base=T, channel_multiplier=-1))
            stage_end(pool, "pool")

            def moe(l):
                r, q = rt[l], ts
                pool.iota(place_row, [[1, P]], base=-P, channel_multiplier=0,
                          allow_small_or_imprecise_dtypes=True).then_inc(r["places"], 1)
                for b in range(2):
                    own(pool.memset(xg[b], 0.0))
                pool.wait_ge(r["list_ready"], 1)
                for b in range(2):
                    pool.wait_ge(r[f"rows_stored{b}"], 16 * ((NT + 1 - b) // 2))

                def gather(q, b, n, t):
                    pool.tensor_copy(toks[b][:, :], tokl[:, bass.ds(t, 1)]).then_inc(q["toks_ready"], 1)
                    pool.wait_ge(q["toks_ready"], n + 1)
                    pool.sem_inc(waits_seen, 1)
                    pool.indirect_dma_start(xg[b], None, h_rows[l], bass.IndirectOffsetOnAxis(toks[b][:, :], 0),
                                            bounds_check=T - 1, oob_is_err=False).then_inc(q[f"gathered{b}"], 16)

                def scatter(q, b, n, t):
                    pool.tensor_copy(yrows[b][:, :], yrow[:, bass.ds(t, 1)]).then_inc(q["yrows_ready"], 1)
                    pool.wait_ge(q["yrows_ready"], n + 1)
                    pool.wait_ge(q["ys_copied"], n * 2 + 2)
                    pool.sem_inc(waits_seen, 1)
                    pool.indirect_dma_start(y_rows[l], bass.IndirectOffsetOnAxis(yrows[b][:, :], 0), ys[b], None,
                                            bounds_check=2 * T - 1, oob_is_err=False).then_inc(q[f"scattered{b}"], 16)

                def step(it, b, first=False, last=False):
                    t = it * 2 + b
                    n = it * 2 + (b + NE * l)
                    if not last:
                        pool.wait_ge(q["tx_done"], n + 1)
                        gather(q, b, n + 2, t + 2)
                    if not first:
                        pool.wait_ge(q[f"scattered{b}"], it * 16 + l * (NE * 8))
                    scatter(q, b, n, t)

                gather(q, 0, NE * l, 0)
                gather(q, 1, NE * l + 1, 1)
                stage_end(pool, "pool")
                step(0, 0, first=True)
                step(0, 1, first=True)
                with pool.Fori(1, NE // 2 - 1) as it:
                    step(it, 0)
                    step(it, 1)
                step(NE // 2 - 1, 0, last=True)
                step(NE // 2 - 1, 1, last=True)
                for b in range(2):
                    pool.wait_ge(q[f"scattered{b}"], (l + 1) * (NE * 8))
                o = ov[l]
                n_ov = pool.value_load(ovinfo[0:1, NOV:NOV + 1], min_val=0, max_val=NOV)
                with pool.If(n_ov > 0):
                    with pool.Fori(0, n_ov) as i:
                        gather(o, 0, i, i + NE)
                        scatter(o, 0, i, i + NE)
                        pool.wait_ge(o["scattered0"], (i + 1) * 16)
                stage_end(pool, "pool")
                stage_end(pool, "pool")

            stage_end(pool, "pool")
            stage_end(pool, "pool")
            stage_end(pool, "pool")
            moe(0)
            stage_end(pool, "pool")
            stage_end(pool, "pool")
            stage_end(pool, "pool")
            moe(1)
            stage_end(pool, "pool")


_INS = ['x_prompt', 'x_sample', 'c_prompt', 'c_sample', 'state_pool_buf', 'state_conv_buf', 'state_lru_h',
        'w_mod', 'b_mod', 'norm_g', 'pool_w', 'pool_scale', 'lru_w_x', 'lru_b_x', 'lru_w_y', 'lru_b_y',
        'conv_w', 'conv_b', 'lru_w_a', 'lru_b_a', 'lru_w_i', 'lru_b_i', 'lru_lambda', 'lru_w_out', 'lru_b_out',
        'router_w', 'router_b', 'moe_w_gate', 'moe_w_up', 'moe_w_down', 'final_g']
_OUTS = [(1, 512, 1024), (8, 4, 1024), (1, 1, 15, 1024), (1, 8, 15, 1024), (1, 1, 3, 1024), (1, 8, 3, 1024),
         (1, 1, 1024), (1, 8, 1024)]


def kernel(**inputs):
    import numpy as _np
    import concourse.bacc as _bacc
    from concourse import mybir as _mybir
    from concourse.bass_utils import run_bass_kernel_spmd as _run

    nc = _bacc.Bacc("TRN2", target_bir_lowering=False, num_devices=1, dynamic_dma_scratch_size=8192)
    arrays, args = {}, []
    for name in _INS:
        a = _np.ascontiguousarray(inputs[name])
        arrays[f"in_{name}_dram"] = a
        args.append(nc.dram_tensor(f"in_{name}_dram", a.shape, _mybir.dt.from_np(a.dtype), kind="ExternalInput").ap())
    for i, shape in enumerate(_OUTS):
        args.append(nc.dram_tensor(f"out_{i}_dram", shape, _mybir.dt.float32, kind="ExternalOutput").ap())
    hybrid_trunk_kernel(nc, *args)
    r = _run(nc, [arrays], core_ids=[0])
    return tuple(r.results[0][f"out_{i}_dram"] for i in range(len(_OUTS)))
```

```python
from contextlib import ExitStack

import concourse.bass as bass
from concourse import mybir

P = 128
ALU = mybir.AluOpType
ACT = mybir.ActivationFunctionType
F32 = mybir.dt.float32
BF16 = mybir.dt.bfloat16
I32 = mybir.dt.int32
AX = mybir.AxisListType.X

POOL_WINDOWS = (2, 4, 8, 16)
LRU_C = 8.0
EPS = 1e-6
BIG = 1e30
GELU = ACT.Gelu_apprx_tanh


def hybrid_trunk_kernel(nc, x_prompt, x_sample, c_prompt, c_sample, state_pool_buf, state_conv_buf, state_lru_h,
                        w_mod, b_mod, norm_g, pool_w, pool_scale, lru_w_x, lru_b_x, lru_w_y, lru_b_y,
                        conv_w, conv_b, lru_w_a, lru_b_a, lru_w_i, lru_b_i, lru_lambda, lru_w_out, lru_b_out,
                        router_w, router_b, moe_w_gate, moe_w_up, moe_w_down, final_g,
                        y_prompt, y_sample, new_pool_prompt, new_pool_sample, new_conv_prompt, new_conv_sample,
                        new_h_prompt, new_h_sample):
    _, S, D = x_prompt.shape
    NB, SS, _ = x_sample.shape
    NS = NB * SS
    T = S + NS
    DC = D // P
    NQ = 1 + NB
    DEPTH = w_mod.shape[0]
    NM = 6 * DC
    PB = state_pool_buf.shape[2]
    CW = conv_w.shape[1]
    CH = CW - 1
    NE, F = moe_w_gate.shape[1], moe_w_gate.shape[3]
    FC = F // P
    NG = 4
    EG = NE // NG
    HALF = 512
    H2 = T // 2
    HP = S - H2
    NT = (T + P - 1) // P
    TW = [min(P, T - j * P) for j in range(NT)]
    NPT = S // P
    NOV = (2 * T - NE) // P
    NL = NE + NOV
    RING = 6
    UNIT = DC * HALF
    assert UNIT == FC * D and D == 2 * HALF and S == HALF and F == HALF
    MOD_ROT = w_mod.shape[2] // HALF // RING
    NOWHERE = 4000

    with ExitStack() as ctx:
        def sb(name, shape, dt=F32):
            return ctx.enter_context(nc.sbuf_tensor(name, shape, dt))

        def sem(name):
            return ctx.enter_context(nc.semaphore(name))

        WORK = 18688
        ring = [sb(f"ring{i}", [P, UNIT]) for i in range(RING)]
        xT = sb("xT", [P, DC, T])
        hT = sb("hT", [P, DC, T])
        work = sb("work", [P, WORK])
        modT = sb("modT", [P, NM, NQ])
        gainT = sb("gainT", [P, DEPTH, 2, DC, NQ])
        shiftT = sb("shiftT", [P, DEPTH, 2, DC, NQ])
        gateT = sb("gateT", [P, DEPTH, 2, DC, NQ])
        gbT = sb("gbT", [P, DC, NQ])
        bmodT = sb("bmodT", [P, DEPTH * NM])
        VEC = ["norm_g0", "norm_g1", "norm_g2", "norm_g3", "pool_scale", "final_g", "b_x", "b_y",
               "cw0", "cw1", "cw2", "cw3", "conv_b", "b_a", "b_i"]
        vecT = sb("vecT", [P, (len(VEC) + 2) * DC])
        rw = sb("rw", [P, DC, NE])
        rb = sb("rb", [P, NE])
        ident = sb("ident", [P, P])
        mean_w = sb("mean_w", [P, P])
        ones_b = sb("ones_b", [P, P], BF16)
        before_b = sb("before_b", [P, P], BF16)
        iota_e = sb("iota_e", [P, NE])
        row_number = sb("row_number", [P, 2 * NT])
        tile_at = sb("tile_at", [P, NL + 1])
        valid = sb("valid", [P, NT])
        invcnt = sb("invcnt", [P, 16])
        scT = sb("scT", [P, DC, NQ])
        poolT = work[:, 13312:13312 + DC * NB * PB].rearrange("p (c r) -> p c r", c=DC)
        rstd = work[:, WORK - T:WORK]
        convT = sb("convT", [P, DC, NB * CH])
        h0T = sb("h0T", [P, DC, NB])
        kdec = sb("kdec", [P, 2, DC])
        half_b = sb("half_b", [P, 2, DC])
        mrow = [work[0:NQ, 14336 + b * HALF:14336 + (b + 1) * HALF] for b in range(2)]
        mrow_last = [work[0:NQ, 12288 + b * HALF:12288 + (b + 1) * HALF] for b in range(2)]
        small = sb("small", [P, DC * NS])
        small2 = sb("small2", [P, DC * NS])
        wts = sb("wts", [P, 2, NT])
        tokl = sb("tokl", [P, NL], I32)
        yrow = sb("yrow", [P, NL], I32)
        toks = [sb(f"toks{b}", [P, 1], I32) for b in range(2)]
        yrows = [sb(f"yrows{b}", [P, 1], I32) for b in range(2)]
        consts = sb("consts", [P, 2])
        spent = modT[:, :, :].rearrange("p m n -> p (m n)")
        conv_tail = spent[:, 0:DC * CH * NQ].rearrange("p (c n) -> p c n", c=DC)
        h_tail = spent[:, DC * CH * NQ:DC * (CH + 1) * NQ].rearrange("p (c n) -> p c n", c=DC)
        gate_cols = spent[:, 0:DC * (NS + 1)].rearrange("p (c n) -> p c n", c=DC)
        picks = sb("picks", [P, NT, NE], BF16)
        ovinfo = sb("ovinfo", [1, NOV + 1], I32)

        bank = [ctx.enter_context(nc.psum_tensor(f"bank{i}", [P, HALF], F32)) for i in range(8)]

        def vec(name, c=None):
            n = VEC.index(name) if name in VEC else {"lam": len(VEC), "b_out": len(VEC) + 1}[name]
            return vecT[:, n * DC:(n + 1) * DC] if c is None else vecT[:, n * DC + c:n * DC + c + 1]

        def mrow_of(u):
            return (mrow_last if u >= (DEPTH * MOD_ROT - 1) * RING else mrow)[u % 2]

        def area(at, n):
            return work[:, at:at + n], at + n

        xtok, at = area(0, NPT * D)
        xtok = xtok.rearrange("p (j d) -> p j d", j=NPT)
        xtok_s, at = area(at, D)
        rows, at = area(at, 5 * P)
        rows = rows.rearrange("p (n d) -> p n d", n=5)
        st_rows, at = area(at, 3 * D)
        st_rows = st_rows.rearrange("p (n d) -> p n d", n=3)
        craw, at = area(at, NQ * DC)
        pooledT, at = area(0, DC * T)
        pooledT = pooledT.rearrange("p (c t) -> p c t", c=DC)
        pw, at = area(at, 2 * NG * 256)
        pw = pw.rearrange("p (g k n) -> p g k n", g=NG, k=2)
        psum_a, at = area(at, 2 * S)
        psum_b, at = area(at, 2 * S)
        psum_a, psum_b = [x.rearrange("p (c t) -> p c t", c=2) for x in (psum_a, psum_b)]
        sbuf_n = 2 * NB * (PB + SS)
        spool_a, at = area(at, sbuf_n)
        spool_b, at = area(at, sbuf_n)
        spool_a, spool_b = [x.rearrange("p (c b t) -> p c b t", c=2, b=NB) for x in (spool_a, spool_b)]
        tail_rows, at = area(at, 2 * D)
        tail_rows = tail_rows.rearrange("p (n d) -> p n d", n=2)
        assert at <= 13312
        at = 0
        xg, xe, sg, hid, hidT, ys = [], [], [], [], [], []
        for b in range(2):
            for lst, n in ((xg, D), (xe, D), (sg, F), (hid, F), (hidT, F), (ys, D)):
                v, at = area(at, n)
                lst.append(v)
        xe = [x.rearrange("p (c t) -> p c t", c=DC) for x in xe]
        hidT = [x.rearrange("p (c t) -> p c t", c=FC) for x in hidT]
        route, at = area(at, 24 * NT * NE)
        route = route.rearrange("p (n j e) -> p n j e", n=24, e=NE)
        lg, ex, sel, one, two, val_a, val_b = (route[:, n] for n in range(7))
        flat = route.rearrange("p n j e -> p (n j e)")
        gsc, gbest = (flat[:, n * NT * NE:n * NT * NE + NT * NG].rearrange("p (j g) -> p j g", g=NG) for n in (7, 8))
        tmp_b = flat[:, 9 * NT * NE:9 * NT * NE + 32]
        cnt_e, ov_e, cum_e = (flat[:, (10 + n) * NT * NE:(10 + n) * NT * NE + NE] for n in range(3))
        end_e = flat[:, 17 * NT * NE:17 * NT * NE + NE]
        ov_f = flat[:, 13 * NT * NE:13 * NT * NE + NOV + 1]
        slot_f, tile_of, place_of = (flat[:, 14 * NT * NE + n * 16:14 * NT * NE + n * 16 + 2 * NT] for n in range(3))
        lt_f, lt_g = (flat[:, (15 + n) * NT * NE:(15 + n) * NT * NE + NL] for n in range(2))
        reached = flat[:, 18 * NT * NE:18 * NT * NE + 2 * NT * (NL + 1)].rearrange("p (i t) -> p i t", i=2 * NT)
        ov_le = flat[:, 22 * NT * NE:22 * NT * NE + NOV * NE].rearrange("p (t e) -> p t e", t=NOV)
        place_row, at = area(at, P)
        place_1h = work[:, 2 * D:2 * D + 2 * NT * P].rearrange("p (i s) -> p i s", i=2 * NT)
        rowof = work[:, 5 * D + 3 * F:5 * D + 3 * F + 2 * NT * NL].rearrange("p (i t) -> p i t", i=2 * NT)
        logitT = work[0:NE, D:D + T]
        assert 2 * NT * P <= 3 * F and 2 * NT * NL <= 3 * F
        htok = [ys[0], ys[1]]
        yl = [[work[:, (2 * j + k) * D:(2 * j + k + 1) * D] for k in range(2)] for j in range(NT)]
        ysum_c = [work[:, (2 * NT + b) * D:(2 * NT + b + 1) * D] for b in range(2)]
        x_row = [work[:, D:2 * D], work[:, 4 * D + 3 * F:5 * D + 3 * F]]
        gate_row = work[0:NS + 1, 5 * D + 4 * F:6 * D + 4 * F]
        x_last = [ring[3][:, j * D:(j + 1) * D] for j in range(NPT)] + [ring[4][:, 0:D]]
        gate_last = [ring[4][:, D:2 * D]] * NPT + [ring[4][:, 2 * D:3 * D]]
        final_row = ring[4][:, 3 * D:4 * D]
        assert at <= WORK
        at = 0
        e2, at = area(at, DC * T)
        xb = e2[:, 0:DC * (CH + S)].rearrange("p (c t) -> p c t", c=DC)
        e2 = e2.rearrange("p (c t) -> p c t", c=DC)
        xcT, at = area(at, DC * T)
        ybT, at = area(at, DC * T)
        xcT, ybT = [x.rearrange("p (c t) -> p c t", c=DC) for x in (xcT, ybT)]
        xbs, at = area(at, DC * NB * (CH + SS))
        xbs = xbs.rearrange("p (c b t) -> p c b t", c=DC, b=NB)
        NBLK, BW = lru_w_a.shape[1], lru_w_a.shape[2]
        BC = BW // P
        wai, at = area(at, 2 * NBLK * BC * BW)
        wai = wai.rearrange("p (w g k n) -> p w g k n", w=2, g=NBLK, k=BC)
        tanh_i = []
        for b in range(2):
            v, at = area(at, T)
            tanh_i.append(v)
        assert at <= WORK, at
        def xcT_rows(n):
            return xcT.rearrange("p c t -> p (c t)")[:, n * D:(n + 1) * D]

        aT = hT

        h_rows = [nc.dram_tensor(f"h_rows{l}", [T, D], F32).ap() for l in range(DEPTH)]
        y_rows = [nc.dram_tensor(f"y_rows{l}", [2 * T, D], F32).ap() for l in range(DEPTH)]

        x_rows = nc.dram_tensor("x_rows", [T, D], F32).ap()
        gate_rows = nc.dram_tensor("gate_rows", [NS + 1, D], F32).ap()

        slot_loaded = [sem(f"slot_loaded{i}") for i in range(RING)]
        gate_sem = sem("stage_gate")
        vec_step = sem("vec_step")
        act_step = sem("act_step")
        pool_step = sem("pool_step")
        in_loaded = sem("in_loaded")
        state_loaded = sem("state_loaded")
        small_loaded = sem("small_loaded")
        blocks_loaded = sem("blocks_loaded")
        poolw_loaded = sem("poolw_loaded")
        stored = sem("stored")
        copied = sem("copied")
        turned = sem("turned")
        turned_out = sem("turned_out")
        mod_used = sem("mod_used")
        mod_done = sem("mod_done")
        silu_c = sem("silu_c")
        mrow_copied = sem("mrow_copied")
        mod_evicted = sem("mod_evicted")
        sq_ready = sem("sq_ready")
        sq_summed = sem("sq_summed")
        mean_ready = sem("mean_ready")
        normed = sem("normed")
        chunk_ready = sem("chunk_ready")
        pooled_ready = sem("pooled_ready")
        mixed = sem("mixed")
        mixed_added = sem("mixed_added")
        tail_turned = sem("tail_turned")
        x_done = sem("x_done")
        x_out = sem("x_out")
        lru_used = sem("lru_used")
        conv_done = sem("conv_done")
        gates_done = sem("gates_done")
        a_ready = sem("a_ready")
        gates_read = sem("gates_read")
        mult_done = sem("mult_done")
        waits_seen = sem("waits_seen")
        std_ready = sem("std_ready")
        power_ready = sem("power_ready")
        root_ready = sem("root_ready")
        lam_exp = sem("lam_exp")
        z_ready = sem("z_ready")
        o_done = sem("o_done")
        o_out = sem("o_out")
        o_added = sem("o_added")
        tails_ready = sem("tails_ready")
        gate_cols_ready = sem("gate_cols_ready")
        gate_row_stored = sem("gate_row_stored")
        x_rows_stored = [sem(f"x_rows_stored{b}") for b in range(2)]
        last_loaded = sem("last_loaded")
        last_gated = sem("last_gated")
        last_x = sem("last_x")
        last_squares = sem("last_squares")
        last_std = sem("last_std")
        y_ready = sem("y_ready")
        y_loaded = [sem(f"y_loaded{j}") for j in range(NT)]
        y_stored = sem("y_stored")

        ROUTE = ["logits_done", "logits_out", "logits", "lmax", "ex", "count_in", "counts", "turn", "turn_out",
                 "rows_stored0", "rows_stored1", "places", "list_in", "list_out", "list_ready", "y_scaled",
                 "y_summed", "y_turned", "y_added"]
        TILE = ["toks_ready", "yrows_ready", "gathered0", "gathered1", "tx_done", "xe_copied", "g_done", "u_done", "silu_done",
                "hid_done", "th_done", "ht_copied", "y_done", "ys_copied", "scattered0", "scattered1"]
        rt = [{n: sem(f"r{l}_{n}") for n in ROUTE} for l in range(DEPTH)]
        ts = {n: sem(f"t_{n}") for n in TILE}
        ov = [{n: sem(f"o{l}_{n}") for n in TILE + ["loaded"]} for l in range(DEPTH)]

        block = ctx.enter_context(nc.Block())

        passed = {"pe": 0, "act": 0, "dve": 0, "pool": 0}

        def stage_end(eng, name):
            passed[name] += 1
            eng.drain().then_inc(gate_sem, 1)
            eng.wait_ge(gate_sem, 4 * passed[name])

        SMALL = ((b_mod.rearrange("l (r p) -> (l r) p", p=P), 0, 0), (norm_g.rearrange("l n (r p) -> (l n r) p", p=P), 1, 0),
                 (pool_scale, 1, 32), (final_g.rearrange("(o d) -> o d", o=1), 1, 40), (lru_b_x, 1, 48), (lru_b_y, 1, 56),
                 (conv_w[0], 1, 64), (conv_b, 2, 0), (lru_b_a, 2, 8), (lru_b_i, 2, 16), (lru_lambda, 2, 24),
                 (lru_b_out, 2, 32), (c_prompt, 3, 0), (c_sample, 3, DC))
        N_SMALL = len(SMALL) + 2

        def param_groups():
            return [[(rows[0:DEPTH * NM, 0, :], 0)], [(rows[0:96, 1, :], 0)], [(rows[0:40, 2, :], 0)],
                    [(rows[0:NQ * DC, 3, :], 0)]]

        def state_groups():
            def cut(n, h, c):
                return st_rows[0:h, n, c * P:(c + 1) * P]
            return [[(cut(0, NB * PB, c), (c % 4) * NB * PB) for c in range(4 * g, 4 * g + 4)] for g in range(2)] + [
                [(cut(1, NB * CH, c), c * NB * CH) for c in range(DC)], [(cut(2, NB, c), c * NB) for c in range(DC)]]

        def x_groups():
            return [[(xtok[:, j, c * P:(c + 1) * P], j * P) for j in range(NPT)] for c in range(DC)] + [
                [(xtok_s[0:NS, c * P:(c + 1) * P], c * NS) for c in range(DC)]]

        @block.sync
        def _(sp):
            def wait_free(prev, s):
                if prev is None:
                    return
                kind, l = prev
                if kind == "mod":
                    sp.wait_ge(mod_used, RING * l + s + 1)
                elif kind == "moe":
                    b, part = s // 3, s % 3
                    name, n = (("g_done", 1), ("u_done", 1), ("y_done", 2))[part]
                    sp.wait_ge(ts[name], n * (NE * l + NE - 2 + b + 1))
                else:
                    sp.wait_ge(lru_used, s + 1)

            def load_mod(l, r, prev):
                src = w_mod[l].rearrange("(k p) n -> p k n", p=P)
                for s in range(RING):
                    wait_free(prev, s)
                    at = (r * RING + s) * HALF
                    sp.dma_start(ring[s][:, :].rearrange("p (k n) -> p k n", k=DC),
                                 src[:, :, at:at + HALF]).then_inc(slot_loaded[s], 16)

            def load_expert(l, e, b, loaded, wait):
                for part, w in enumerate((moe_w_gate, moe_w_up, moe_w_down)):
                    s = 3 * b + part
                    wait(s)
                    one = w[l][bass.ds(e, 1)]
                    src = one.rearrange("o (k p) n -> p (o k) n", p=P)
                    sp.dma_start(ring[s][:, :].rearrange("p (k n) -> p k n", k=src.shape[1]),
                                 src).then_inc(loaded(s), 16)

            def load_moe(l, prev):
                for b in range(2):
                    load_expert(l, b, b, lambda s: slot_loaded[s], lambda s: wait_free(prev, s))
                with sp.Fori(1, NE // 2) as it:
                    for b in range(2):
                        def used(s, b=b):
                            name, n = (("g_done", 1), ("u_done", 1), ("y_done", 2))[s % 3]
                            sp.wait_ge(ts[name], it * (2 * n) + n * (NE * l + b - 1))
                        load_expert(l, it * 2 + b, b, lambda s: slot_loaded[s], used)

            def load_overflow(l):
                sp.wait_ge(rt[l]["list_ready"], 2)
                n_ov = sp.value_load(ovinfo[0:1, NOV:NOV + 1], min_val=0, max_val=NOV)
                with sp.If(n_ov > 0):
                    sp.wait_ge(ts["y_done"], 2 * NE * (l + 1))
                    with sp.Fori(0, n_ov) as i:
                        e = sp.value_load(ovinfo[0:1, bass.ds(i, 1)], min_val=0, max_val=NE - 1)
                        load_expert(l, e, 0, lambda s: ov[l]["loaded"], lambda s: None)
                        sp.wait_ge(ov[l]["y_done"], (i + 1) * 2)
                        sp.sem_inc(waits_seen, 1)

            def load_lru(prev):
                for j in range(NT):
                    sp.wait_ge(y_loaded[j], 32)
                s = 0
                for w in (lru_w_x, lru_w_y, lru_w_out):
                    for half in range(2):
                        wait_free(prev, s)
                        sp.dma_start(ring[s][:, :].rearrange("p (k n) -> p k n", k=DC),
                                     w[0].rearrange("(k p) n -> p k n", p=P)[:, :, half * HALF:(half + 1) * HALF]
                                     ).then_inc(slot_loaded[s], 16)
                        s += 1

            sp.wait_ge(small_loaded, 16 * N_SMALL)
            load_mod(0, 0, None)
            load_mod(0, 1, ("mod", 0))
            sp.dma_start(new_pool_sample[0][:, 0:PB - SS, :], state_pool_buf[0][:, SS:PB, :]).then_inc(copied, 16)
            load_mod(1, 0, ("mod", 1))
            load_moe(0, ("mod", 2))
            load_overflow(0)
            load_mod(1, 1, ("moe", 0))
            load_lru(("mod", 3))
            load_moe(1, ("lru", 0))
            load_overflow(1)
            for b in range(2):
                sp.wait_ge(x_rows_stored[b], 16 * ((NT + 1 - b) // 2))
            sp.wait_ge(gate_row_stored, 16)
            sp.wait_ge(ts["g_done"], DEPTH * NE)
            sp.dma_start(ring[3][:, :].rearrange("p (j d) -> p j d", j=NPT),
                         x_rows[0:S, :].rearrange("(j p) d -> p j d", p=P)).then_inc(last_loaded, 16)
            sp.wait_ge(ts["u_done"], DEPTH * NE)
            sp.dma_start(x_last[NPT][0:NS, :], x_rows[S:T, :]).then_inc(last_loaded, 16)
            sp.dma_start(gate_last[0], gate_rows[0].partition_broadcast(P)).then_inc(last_loaded, 16)
            sp.dma_start(gate_last[NPT][0:NS, :], gate_rows[1:NS + 1, :]).then_inc(last_loaded, 16)
            sp.dma_start(final_row, final_g.partition_broadcast(P)).then_inc(last_loaded, 16)
            for j in range(NT):
                w = TW[j]
                sp.wait_ge(y_ready, j + 1)
                dst = y_prompt[0, j * P:(j + 1) * P, :] if w == P else y_sample.rearrange("b s d -> (b s) d")
                sp.dma_start(dst, yl[j][0][0:w, :]).then_inc(y_stored, 16)
            sp.wait_ge(y_stored, 16 * NT)
            sp.wait_ge(copied, 16)

        NORM_UNITS = [([(0, 1, 0)], [(0, 1, 1)]), ([(1, 0, 1)], [(1, 0, 2)]),
                      ([(1, 1, 3)], [(1, 1, 4), (1, 1, 5)]), ([], [])]
        assert MOD_ROT == 2 and 3 * DC * P == RING * HALF
        MOE0_ROT = 3
        MOD_ROTS = [[0, 1], [2, MOE0_ROT + NE // 2]]
        LRU_ROT = MOD_ROTS[1][1] + 1
        MOE_ROT = [MOE0_ROT, LRU_ROT + 1]

        @block.tensor
        def _(pe):
            def turn_rows(groups, n):
                for parts in groups:
                    if n >= 4:
                        pe.wait_ge(turned_out, n - 3)
                    for src, col in parts:
                        w = src.shape[0]
                        last = pe.transpose(bank[n % 4][:, col:col + w], src, ident[0:w, 0:w])
                    last.then_inc(turned, 1)
                    n += 1
                return n

            def mod(l, r, ss=range(RING)):
                def turn(u):
                    pe.wait_ge(mrow_copied, u + 1)
                    for m in range(4):
                        at = ((u % RING) * 4 + m) * NQ
                        last = pe.transpose(bank[7][:, at:at + NQ], mrow_of(u)[:, m * P:(m + 1) * P], ident[0:NQ, 0:NQ])
                    return last

                for s in ss:
                    u = (l * MOD_ROT + r) * RING + s
                    pe.wait_ge(slot_loaded[s], 16 * (MOD_ROTS[l][r] + 1))
                    if u >= 2:
                        pe.wait_ge(mrow_copied, u - 1)
                    w = ring[s][:, :].rearrange("p (k n) -> p k n", k=DC)
                    for k in range(DC):
                        last = pe.matmul(bank[5 + u % 2][0:NQ, :], scT[:, k, :], w[:, k, :],
                                         start=(k == 0), stop=(k == DC - 1))
                    last.then_inc(mod_used, 1)
                    if s == 1 and u >= RING:
                        pe.wait_ge(mod_evicted, u // RING)
                    if s >= 1:
                        turn(u - 1)
                if s == RING - 1:
                    turn(u).then_inc(mod_done, 1)

            pe.wait_ge(pool_step, 3)
            pe.wait_ge(small_loaded, 16 * N_SMALL)
            n = turn_rows(param_groups(), 0)
            pe.wait_ge(silu_c, 1)
            mod(0, 0)
            pe.wait_ge(state_loaded, 16 * 3)
            n = turn_rows(state_groups(), n)
            pe.wait_ge(in_loaded, 16 * 2)
            n = turn_rows(x_groups(), n)
            stage_end(pe, "pe")

            def mean(n):
                for l, r, s in NORM_UNITS[n][0]:
                    mod(l, r, [s])
                pe.wait_ge(sq_summed, n + 1)
                for h in range(2):
                    pe.matmul(bank[h][:, 0:H2], mean_w[:, :], hT[:, 0, h * H2:(h + 1) * H2]).then_inc(mean_ready, 1)
                for l, r, s in NORM_UNITS[n][1]:
                    mod(l, r, [s])

            def tail(bk, srcs):
                for c in range(DC):
                    src = srcs(c)
                    w = src.shape[-1]
                    last = pe.transpose(bank[bk + c // 4][0:w, (c % 4) * P:(c % 4 + 1) * P], src, ident[:, :])
                last.then_inc(tail_turned, 1)

            def pool_mix():
                tail(3, lambda c: hT[:, c, S - PB:S])
                tail(0, lambda c: hT[:, c, S:T])
                mod(0, 1, range(2, RING))
                mod(1, 0, [0])
                pe.wait_ge(poolw_loaded, 16)
                for g in range(NG):
                    pe.wait_ge(pooled_ready, g + 1)
                    for m in range(2):
                        i = 2 * g + m
                        if i >= 2:
                            pe.wait_ge(mixed_added, i - 1)
                        for k in range(2):
                            pe.matmul(bank[i % 2][:, :], pw[:, g, k, m * P:(m + 1) * P], pooledT[:, 2 * g + k, 0:S],
                                      start=(k == 0), stop=(k == 1))
                        for k in range(2):
                            last = pe.matmul(bank[2][:, i * NS:(i + 1) * NS], pw[:, g, k, m * P:(m + 1) * P],
                                             pooledT[:, 2 * g + k, S:T], start=(k == 0), stop=(k == 1))
                        last.then_inc(mixed, 1)
                stage_end(pe, "pe")

            def tx(q, b, n, first, got):
                got(b)
                if not first:
                    pe.wait_ge(q["xe_copied"], n * 2)
                for c in range(DC):
                    last = pe.transpose(bank[4 + c // 4][:, (c % 4) * P:(c % 4 + 1) * P],
                                        xg[b][:, c * P:(c + 1) * P], ident[:, :])
                last.then_inc(q["tx_done"], 1)

            def widen(q, part, b, n, first, loaded, ks):
                if ks[0] == 0:
                    if part == 0:
                        pe.wait_ge(q["xe_copied"], n * 2 + 2)
                    loaded(3 * b + part)
                    if not first:
                        pe.wait_ge(q[("silu_done", "hid_done")[part]], n)
                w = ring[3 * b + part][:, :].rearrange("p (k n) -> p k n", k=DC)
                for k in ks:
                    last = pe.matmul(bank[part][:, :], xe[b][:, k, :], w[:, k, :], start=(k == 0), stop=(k == DC - 1))
                if ks[-1] == DC - 1:
                    last.then_inc(q[("g_done", "u_done")[part]], 1)

            def turn_hidden(q, b, n, first):
                pe.wait_ge(q["hid_done"], n + 1)
                if not first:
                    pe.wait_ge(q["ht_copied"], n * 2)
                for c in range(FC):
                    last = pe.transpose(bank[6 + c // 2][:, (c % 2) * P:(c % 2 + 1) * P], hid[b][:, c * P:(c + 1) * P],
                                        ident[:, :])
                last.then_inc(q["th_done"], 1)

            def down(q, b, n, first, loaded):
                pe.wait_ge(q["ht_copied"], n * 2 + 2)
                loaded(3 * b + 2)
                if not first:
                    pe.wait_ge(q["ys_copied"], n * 2)
                w = ring[3 * b + 2][:, :].rearrange("p (k n) -> p k n", k=FC)
                for half in range(2):
                    for k in range(FC):
                        last = pe.matmul(bank[2 + half][:, :], hidT[b][:, k, :], w[:, k, half * HALF:(half + 1) * HALF],
                                         start=(k == 0), stop=(k == FC - 1))
                    last.then_inc(q["y_done"], 1)

            def logits(l, h):
                for c in range(DC):
                    if h == 0:
                        pe.wait_ge(chunk_ready, l * DC + c + 1)
                    last = pe.matmul(bank[2 + h][0:NE, 0:H2], rw[:, c, :], hT[:, c, h * H2:(h + 1) * H2],
                                     start=(c == 0), stop=(c == DC - 1))
                if h == 1:
                    last.then_inc(rt[l]["logits_done"], 1)

            def moe(l):
                r, q = rt[l], ts
                logits(l, 1)
                for j in range(NT):
                    w = TW[j]
                    for half in range(2):
                        i = 2 * j + half
                        if i >= 2:
                            pe.wait_ge(r["turn_out"], i - 1)
                        for c in range(4):
                            last = pe.transpose(bank[half][0:w, c * P:(c + 1) * P],
                                                hT[:, 4 * half + c, j * P:j * P + w], ident[:, :])
                        last.then_inc(r["turn"], 1)
                    if j == 0:
                        pe.wait_ge(r["logits_out"], 1)
                        for i in range(NT):
                            last = pe.transpose(bank[4][0:TW[i], i * NE:(i + 1) * NE], logitT[:, i * P:i * P + TW[i]],
                                                ident[0:NE, 0:NE])
                        last.then_inc(r["logits"], 1)

                def turn_x(js):
                    for j in js:
                        w = TW[j]
                        for half in range(2):
                            i = 2 * NT + 2 * j + half
                            pe.wait_ge(r["turn_out"], i - 1)
                            for c in range(4):
                                last = pe.transpose(bank[half][0:w, c * P:(c + 1) * P],
                                                    xT[:, 4 * half + c, j * P:j * P + w], ident[:, :])
                            last.then_inc(r["turn"], 1)

                if l == 0:
                    mod(1, 0, [3])
                else:
                    pe.wait_ge(gate_cols_ready, 1)
                    tail(5, lambda c: gate_cols[:, c, :])
                    turn_x(range(0, 1))
                pe.wait_ge(r["count_in"], 1)
                for j in range(NT):
                    for i in range(j):
                        pe.matmul(bank[3][:, j * NE:(j + 1) * NE], ones_b[:, :], picks[:, i, :], start=(i == 0), stop=False)
                    pe.matmul(bank[3][:, j * NE:(j + 1) * NE], before_b[:, :], picks[:, j, :], start=(j == 0), stop=True)
                for i in range(NT):
                    last = pe.matmul(bank[3][:, NT * NE:(NT + 1) * NE], ones_b[:, :], picks[:, i, :],
                                     start=(i == 0), stop=(i == NT - 1))
                last.then_inc(r["counts"], 1)
                if l == 0:
                    mod(1, 0, [4])
                else:
                    turn_x(range(1, NT))
                pe.wait_ge(r["list_in"], 1)
                for i in range(2 * NT):
                    w = TW[i % NT]
                    last = pe.matmul(bank[2][:, 0:NL], place_1h[0:w, i, :], rowof[0:w, i, :],
                                     start=(i == 0), stop=(i == 2 * NT - 1))
                last.then_inc(r["list_out"], 1)
                if l == 0:
                    mod(1, 0, [5])
                stage_end(pe, "pe")

                rot0 = MOE_ROT[l]

                def step(it, b, first=False, last=False):
                    t = it * 2 + (b + NE * l)
                    nb, nit = 1 - b, it + b

                    def loaded(s):
                        pe.wait_ge(slot_loaded[s], (it + (rot0 + 1)) * 16)

                    def loaded_next(s):
                        pe.wait_ge(slot_loaded[s], (nit + (rot0 + 1)) * 16)

                    if not last:
                        tx(q, nb, t + 1, False,
                           lambda _: pe.wait_ge(q[f"gathered{nb}"], (nit + (l * (NE // 2) + 1)) * 16))
                    widen(q, 1, b, t, first, loaded, range(DC))
                    if not last:
                        widen(q, 0, nb, t + 1, False, loaded_next, range(DC // 2))
                    turn_hidden(q, b, t, first)
                    if not last:
                        widen(q, 0, nb, t + 1, False, loaded_next, range(DC // 2, DC))
                    down(q, b, t, first, loaded)

                tx(q, 0, l * NE, True, lambda _: pe.wait_ge(q["gathered0"], (l * (NE // 2) + 1) * 16))
                widen(q, 0, 0, l * NE, True, lambda s: pe.wait_ge(slot_loaded[s], (rot0 + 1) * 16), range(DC))
                step(0, 0, first=True)
                step(0, 1)
                with pe.Fori(1, NE // 2 - 1) as it:
                    step(it, 0)
                    step(it, 1)
                step(NE // 2 - 1, 0)
                step(NE // 2 - 1, 1, last=True)
                o = ov[l]
                n_ov = pe.value_load(ovinfo[0:1, NOV:NOV + 1], min_val=0, max_val=NOV)
                with pe.If(n_ov > 0):
                    with pe.Fori(0, n_ov) as i:
                        tx(o, 0, i, True, lambda _: pe.wait_ge(o["gathered0"], (i + 1) * 16))
                        for part in range(2):
                            widen(o, part, 0, i, True, lambda s: pe.wait_ge(o["loaded"], (i + 1) * 48), range(DC))
                        turn_hidden(o, 0, i, True)
                        down(o, 0, i, True, lambda s: None)
                if l == 0:
                    mod(1, 1, [0, 1])
                stage_end(pe, "pe")
                if l == 1:
                    return
                mod(1, 1, [2])
                for j in range(NT):
                    w = TW[j]
                    pe.wait_ge(r["y_summed"], j + 1)
                    if j >= 2:
                        pe.wait_ge(r["y_added"], j - 1)
                    for c in range(DC):
                        bk = 2 * (j % 2) + c // 4
                        last = pe.transpose(bank[bk][:, (c % 4) * P:(c % 4) * P + w],
                                            ysum_c[j % 2][0:w, c * P:(c + 1) * P], ident[0:w, 0:w])
                    last.then_inc(r["y_turned"], 1)
                stage_end(pe, "pe")

            def lru():
                for br in range(2):
                    for m in range(DC):
                        i = br * DC + m
                        s = 2 * br + m // 4
                        if m % 4 == 0:
                            pe.wait_ge(slot_loaded[s], 16 * (LRU_ROT + 1))
                        if i >= 2:
                            pe.wait_ge(x_out, i - 1)
                        w = ring[s][:, :].rearrange("p (k n) -> p k n", k=DC)[:, :, (m % 4) * P:(m % 4 + 1) * P]
                        for h in range(2):
                            for k in range(DC):
                                last = pe.matmul(bank[2 * (i % 2) + h][:, 0:H2], w[:, k, :], hT[:, k, h * H2:(h + 1) * H2],
                                                 start=(k == 0), stop=(k == DC - 1))
                        last.then_inc(x_done, 1)
                        if m % 4 == 3:
                            pe.drain().then_inc(lru_used, 1)
                pe.wait_ge(blocks_loaded, 32)
                pe.wait_ge(x_out, 2 * DC)
                pe.wait_ge(conv_done, 1)
                for g in range(NBLK):
                    for m in range(BC):
                        i = g * BC + m
                        if i >= 2:
                            pe.wait_ge(gates_read, i - 1)
                        for which in range(2):
                            for h in range(2):
                                for k in range(BC):
                                    last = pe.matmul(bank[4 * (i % 2) + 2 * which + h][:, 0:H2],
                                                     wai[:, which, g, k, m * P:(m + 1) * P],
                                                     xcT[:, BC * g + k, h * H2:(h + 1) * H2],
                                                     start=(k == 0), stop=(k == BC - 1))
                        last.then_inc(gates_done, 1)
                for s in (4, 5):
                    pe.wait_ge(slot_loaded[s], 16 * (LRU_ROT + 1))
                pe.wait_ge(gates_read, DC)

                def w_out(k, m):
                    return ring[4 + m // 4][:, :].rearrange("p (k n) -> p k n", k=DC)[:, k, (m % 4) * P:(m % 4 + 1) * P]

                for k in range(DC):
                    pe.wait_ge(z_ready, k + 1)
                    for m in range(DC):
                        ins = pe.matmul(bank[m][:, 0:H2], w_out(k, m), ybT[:, k, 0:H2], start=(k == 0), stop=(k == DC - 1))
                        if k == DC - 1:
                            ins.then_inc(o_done, 1)
                pe.wait_ge(z_ready, DC + 1)
                for m in range(DC):
                    pe.wait_ge(o_out, m + 1 if m < 4 else DC + m - 3)
                    for k in range(DC):
                        last = pe.matmul(bank[m % 4][:, 0:H2], w_out(k, m), ybT[:, k, H2:T], start=(k == 0), stop=(k == DC - 1))
                    last.then_inc(o_done, 1)
                    if m % 4 == 3:
                        pe.drain().then_inc(lru_used, 1)
                    if m == 5:
                        pe.wait_ge(tails_ready, 1)
                        tail(6, lambda c: conv_tail[:, c, :])
                        tail(4, lambda c: h_tail[:, c, :])
                stage_end(pe, "pe")

            mean(0)
            stage_end(pe, "pe")
            pool_mix()
            mean(1)
            logits(0, 0)
            stage_end(pe, "pe")
            moe(0)
            mean(2)
            stage_end(pe, "pe")
            lru()
            mean(3)
            logits(1, 0)
            stage_end(pe, "pe")
            moe(1)

        @block.scalar
        def _(act):
            n_own = [0]
            n_stored = [0]

            def own(ins):
                n_own[0] += 1
                ins.then_inc(act_step, 1)
                act.wait_ge(act_step, n_own[0])

            def store(dst, src):
                n_stored[0] += 16
                act.dma_start(dst, src).then_inc(stored, 16)

            for src, n, r in SMALL:
                if len(src.shape) == 2 and src.shape[1] != P:
                    src = src.rearrange("n (r p) -> (n r) p", p=P)
                act.dma_start(rows[r:r + src.shape[0], n, :], src).then_inc(small_loaded, 16)
            act.dma_start(rw[:, :, :], router_w.rearrange("(k p) e -> p k e", p=P)).then_inc(small_loaded, 16)
            act.dma_start(rb[:, :], router_b.partition_broadcast(P)).then_inc(small_loaded, 16)
            act.wait_ge(lam_exp, 1)
            act.activation(small2[:, DC:2 * DC], small2[:, 0:DC], ACT.Exp).then_inc(lam_exp, 1)
            act.wait_ge(turned_out, 4)
            act.activation(scT[:, :, :].rearrange("p c n -> p n c"), craw.rearrange("p (n c) -> p n c", n=NQ),
                           ACT.Silu).then_inc(silu_c, 1)
            act.dma_start(xtok, x_prompt[0].rearrange("(j p) d -> p j d", p=P)).then_inc(in_loaded, 16)
            act.dma_start(xtok_s[0:NS, :], x_sample.rearrange("b s d -> (b s) d")).then_inc(in_loaded, 16)
            act.dma_start(st_rows[0:NB * PB, 0, :], state_pool_buf[0].rearrange("b r d -> (b r) d")).then_inc(state_loaded, 16)
            act.dma_start(st_rows[0:NB * CH, 1, :], state_conv_buf[0].rearrange("b r d -> (b r) d")).then_inc(state_loaded, 16)
            act.dma_start(st_rows[0:NB, 2, :], state_lru_h[0]).then_inc(state_loaded, 16)

            def mod_rows(l, r, ss=range(RING)):
                for s in ss:
                    u = (l * MOD_ROT + r) * RING + s
                    act.wait_ge(mod_used, u + 1)
                    act.copy(mrow_of(u), bank[5 + u % 2][0:NQ, :]).then_inc(mrow_copied, 1)

            mod_rows(0, 0)
            stage_end(act, "act")
            act.dma_start(pw, pool_w[0].rearrange("g (k p) n -> p g k n", p=P)).then_inc(poolw_loaded, 16)

            def norm(n, layer, which):
                for c in range(DC):
                    act.activation(hT[:, c, :], xT[:, c, :], ACT.Square).then_inc(sq_ready, 1)
                for l, r, s in NORM_UNITS[n][0]:
                    mod_rows(l, r, [s])
                for h in range(2):
                    act.wait_ge(mean_ready, 2 * n + h + 1)
                    act.activation(rstd[:, h * H2:(h + 1) * H2], bank[h][:, 0:H2], ACT.Sqrt, bias=consts[:, 0:1]
                                   ).then_inc(std_ready, 1)
                for c in range(DC):
                    act.wait_ge(normed, n * DC + c + 1)
                    ins = act.activation(hT[:, c, 0:S], hT[:, c, 0:S], ACT.Identity,
                                         scale=gainT[:, layer, which, c, 0:1], bias=shiftT[:, layer, which, c, 0:1])
                    if which == 1:
                        ins.then_inc(chunk_ready, 1)
                for l, r, s in NORM_UNITS[n][1]:
                    mod_rows(l, r, [s])
                act.wait_ge(stored, n_stored[0])
                stage_end(act, "act")

            def tail_rows_out(w0, stores, n, bk=4):
                act.wait_ge(tail_turned, n)
                for half in range(2):
                    ins = act.copy(w0[:, half * HALF:(half + 1) * HALF], bank[bk + half][0:w0.shape[0], :])
                own(ins)
                for dst, lo, hi in stores:
                    store(dst, w0[lo:hi, :])

            def pool_mix():
                tail_rows_out(tail_rows[0:PB, 0, :], [(new_pool_prompt[0, 0], 0, PB)], 1, 3)
                tail_rows_out(tail_rows[0:NS, 1, :],
                              [(new_pool_sample[0, b, PB - SS:PB, :], b * SS, (b + 1) * SS) for b in range(NB)], 2, 0)
                mod_rows(0, 1, range(2, RING))
                mod_rows(1, 0, [0])
                stage_end(act, "act")
            def last_rows(r):
                for j in range(NT + 2):
                    if j < NT:
                        w = TW[j]
                        act.wait_ge(y_loaded[j], 32 * DEPTH)
                        act.activation(yl[j][0][0:w, :], yl[j][0][0:w, :], ACT.Copy,
                                       scale=wts[0:w, 0, j:j + 1]).then_inc(r["y_scaled"], 1)
                    if j >= 2:
                        i, w = j - 2, TW[j - 2]
                        act.wait_ge(last_x, i + 1)
                        act.activation(yl[i][1][0:w, :], yl[i][0][0:w, :], ACT.Square,
                                       accum_out=small[0:w, i:i + 1]).then_inc(last_squares, 1)
                        act.wait_ge(last_squares, i + 1)
                        act.activation(small2[0:w, i:i + 1], small[0:w, i:i + 1], ACT.Sqrt, scale=1.0 / D,
                                       bias=consts[0:w, 0:1]).then_inc(last_std, 1)

            def moe(l):
                r, q = rt[l], ts
                act.wait_ge(r["logits_done"], 1)
                act.copy(logitT[:, 0:H2], bank[2][0:NE, 0:H2])
                act.copy(logitT[:, H2:T], bank[3][0:NE, 0:H2]).then_inc(r["logits_out"], 1)
                for j in range(NT):
                    if j == 1:
                        act.wait_ge(r["lmax"], 1)
                        act.activation(ex, lg, ACT.Exp).then_inc(r["ex"], 1)
                    w = TW[j]
                    if j >= 2:
                        act.wait_ge(r[f"rows_stored{j % 2}"], 16 * (j // 2))
                    for half in range(2):
                        act.wait_ge(r["turn"], 2 * j + half + 1)
                        ins = act.copy(htok[j % 2][0:w, half * HALF:(half + 1) * HALF], bank[half][0:w, :])
                        ins.then_inc(r["turn_out"], 1)
                    act.wait_ge(r["turn_out"], 2 * j + 2)
                    act.dma_start(h_rows[l][j * P:j * P + w, :], htok[j % 2][0:w, :]).then_inc(r[f"rows_stored{j % 2}"], 16)
                if l == 0:
                    mod_rows(1, 0, range(3, RING))
                else:
                    act.wait_ge(tail_turned, 5)
                    for half in range(2):
                        ins = act.copy(gate_row[:, half * HALF:(half + 1) * HALF], bank[5 + half][0:NS + 1, :])
                    own(ins)
                    act.dma_start(gate_rows, gate_row).then_inc(gate_row_stored, 16)
                    for j in range(NT):
                        w = TW[j]
                        if j >= 2:
                            act.wait_ge(x_rows_stored[j % 2], 16 * (j // 2))
                        for half in range(2):
                            act.wait_ge(r["turn"], 2 * NT + 2 * j + half + 1)
                            act.copy(x_row[j % 2][0:w, half * HALF:(half + 1) * HALF], bank[half][0:w, :]
                                     ).then_inc(r["turn_out"], 1)
                        act.wait_ge(r["turn_out"], 2 * NT + 2 * j + 2)
                        act.dma_start(x_rows[j * P:j * P + w, :], x_row[j % 2][0:w, :]).then_inc(x_rows_stored[j % 2], 16)
                    act.wait_ge(gate_row_stored, 16)
                    for b in range(2):
                        act.wait_ge(x_rows_stored[b], 16 * ((NT + 1 - b) // 2))
                stage_end(act, "act")

                def xe_copy(q, b, n, used):
                    act.wait_ge(q["tx_done"], n + 1)
                    used()
                    act.copy(xe[b][:, 0:4, :], bank[4][:, :].rearrange("p (c t) -> p c t", c=4)).then_inc(q["xe_copied"], 1)

                def tile(q, b, n, first, x_next, ys_free):
                    act.wait_ge(q["g_done"], n + 1)
                    if not first:
                        act.wait_ge(q["hid_done"], n - 1)
                    act.activation(sg[b], bank[0][:, :], ACT.Silu).then_inc(q["silu_done"], 1)
                    x_next()
                    act.wait_ge(q["th_done"], n + 1)
                    if not first:
                        act.wait_ge(q["y_done"], n * 2 - 2)
                    act.copy(hidT[b][:, 0:2, :], bank[6][:, 0:2 * P].rearrange("p (c t) -> p c t", c=2)
                             ).then_inc(q["ht_copied"], 1)
                    act.wait_ge(q["y_done"], n * 2 + 1)
                    ys_free()
                    act.copy(ys[b][:, 0:HALF], bank[2][:, :]).then_inc(q["ys_copied"], 1)

                def step(it, b, first=False, last=False):
                    t = it * 2 + (b + NE * l)
                    nb = 1 - b

                    def x_next():
                        if not last:
                            xe_copy(q, nb, t + 1, lambda: None if first and b == 0 else act.wait_ge(q["u_done"], t))

                    tile(q, b, t, first, x_next,
                         lambda: None if first else act.wait_ge(q[f"scattered{b}"], it * 16 + l * (NE * 8)))

                xe_copy(q, 0, NE * l, lambda: None)
                step(0, 0, first=True)
                step(0, 1, first=True)
                with act.Fori(1, NE // 2 - 1) as it:
                    step(it, 0)
                    step(it, 1)
                step(NE // 2 - 1, 0)
                step(NE // 2 - 1, 1, last=True)
                o = ov[l]
                n_ov = act.value_load(ovinfo[0:1, NOV:NOV + 1], min_val=0, max_val=NOV)
                with act.If(n_ov > 0):
                    with act.Fori(0, n_ov) as i:
                        xe_copy(o, 0, i, lambda: None)
                        tile(o, 0, i, True, lambda: None, lambda: None)
                if l == 0:
                    mod_rows(1, 1, [0, 1])
                stage_end(act, "act")
                for j in range(NT):
                    w = TW[j]
                    for k in range(2):
                        act.dma_start(yl[j][k][0:w, :], y_rows[l][k * T + j * P:k * T + j * P + w, :]
                                      ).then_inc(y_loaded[j], 16)
                if l == 1:
                    last_rows(r)
                    return
                mod_rows(1, 1, [2])
                for j in range(NT):
                    w = TW[j]
                    act.wait_ge(y_loaded[j], 32 * (l + 1))
                    if j >= 2:
                        act.wait_ge(r["y_turned"], j - 1)
                    act.activation(ysum_c[j % 2][0:w, :], yl[j][0][0:w, :], ACT.Copy,
                                   scale=wts[0:w, 0, j:j + 1]).then_inc(r["y_scaled"], 1)
                stage_end(act, "act")

            def lru():
                for br in range(2):
                    for m in range(DC):
                        i = br * DC + m
                        act.wait_ge(x_done, i + 1)
                        b0, b1 = bank[2 * (i % 2)], bank[2 * (i % 2) + 1]
                        if br == 0:
                            b_x = vec("b_x", m)
                            act.activation(xb[:, m, CH:CH + H2], b0[:, 0:H2], ACT.Identity, bias=b_x)
                            act.activation(xb[:, m, CH + H2:CH + S], b1[:, 0:HP], ACT.Identity, bias=b_x)
                            act.activation(xbs[:, m, :, CH:CH + SS], b1[:, HP:H2].rearrange("p (b s) -> p b s", b=NB),
                                           ACT.Identity, bias=b_x).then_inc(x_out, 1)
                        else:
                            act.activation(ybT[:, m, 0:H2], b0[:, 0:H2], GELU, bias=vec("b_y", m))
                            act.activation(ybT[:, m, H2:T], b1[:, 0:H2], GELU, bias=vec("b_y", m)).then_inc(x_out, 1)
                for i in range(DC):
                    act.wait_ge(gates_done, i + 1)
                    if i >= 2:
                        act.wait_ge(mult_done, i - 1)
                    a = aT[:, i, :]
                    for h in range(2):
                        at = slice(h * H2, (h + 1) * H2)
                        act.activation(a[:, at], bank[4 * (i % 2) + h][:, 0:H2], ACT.Tanh, scale=0.5,
                                       bias=half_b[:, 0, i:i + 1])
                        ins = act.activation(tanh_i[i % 2][:, at], bank[4 * (i % 2) + 2 + h][:, 0:H2], ACT.Tanh, scale=0.5,
                                             bias=half_b[:, 1, i:i + 1])
                    ins.then_inc(gates_read, 1)
                    act.wait_ge(gates_read, i + 1)
                    act.activation(e2[:, i, :], a, ACT.Exp, scale=kdec[:, 1, i:i + 1], bias=kdec[:, 1, i:i + 1])
                    act.activation(a, a, ACT.Exp, scale=kdec[:, 0, i:i + 1], bias=kdec[:, 0, i:i + 1]).then_inc(a_ready, 1)
                for i in range(DC):
                    act.wait_ge(power_ready, i + 1)
                    act.activation(e2[:, i, :], e2[:, i, :], ACT.Sqrt, bias=consts[:, 1:2]).then_inc(root_ready, 1)
                for i in range(2 * DC):
                    h, m = i // DC, i % DC
                    act.wait_ge(o_done, i + 1)
                    if i >= 2:
                        act.wait_ge(o_added, i - 1)
                    src = bank[m] if h == 0 else bank[m % 4]
                    n = (H2, HP)[h]
                    ins = act.activation(tanh_i[i % 2][:, 0:n], src[:, 0:n], ACT.Identity, scale=gateT[:, 1, 0, m, 0:1],
                                         bias=gbT[:, m, 0:1])
                    if h == 1:
                        ins = act.copy(small2[:, m * NS:(m + 1) * NS], src[:, HP:H2])
                    ins.then_inc(o_out, 1)
                    if i == DC + 5:
                        tail_rows_out(xcT_rows(0)[0:CH * NQ, :],
                                      [(new_conv_prompt[0, 0], 0, CH),
                                       (new_conv_sample[0].rearrange("b r d -> (b r) d"), CH, CH * NQ)], 3, 6)
                        tail_rows_out(xcT_rows(1)[0:NQ, :], [(new_h_prompt[0], 0, 1), (new_h_sample[0], 1, NQ)], 4, 4)
                stage_end(act, "act")

            norm(0, 0, 0)
            pool_mix()
            norm(1, 0, 1)
            moe(0)
            act.dma_start(wai[:, 0], lru_w_a[0].rearrange("g (k p) n -> p g k n", p=P)).then_inc(blocks_loaded, 16)
            act.dma_start(wai[:, 1], lru_w_i[0].rearrange("g (k p) n -> p g k n", p=P)).then_inc(blocks_loaded, 16)
            norm(2, 1, 0)
            lru()
            norm(3, 1, 1)
            moe(1)

        @block.vector
        def _(dve):
            n_own = [0]

            def own(ins):
                n_own[0] += 1
                ins.then_inc(vec_step, 1)
                dve.wait_ge(vec_step, n_own[0])

            def tt(out, a, b, op):
                own(dve.tensor_tensor(out, a, b, op))

            def spread(a, n):
                return a.unsqueeze(len(a.shape)).to_broadcast(list(a.shape) + [n])

            dve.memset(mean_w[:, :], 1.0 / D)
            dve.memset(ones_b[:, :], 1.0)
            dve.memset(consts[:, 0:1], EPS)
            dve.memset(consts[:, 1:2], 0.25)
            own(dve.memset(valid[:, :], 1.0))
            n = 0

            def out_copy(dst, src):
                dve.tensor_copy(dst, src).then_inc(turned_out, 1)

            dve.wait_ge(turned, 1)
            out_copy(bmodT[:, :], bank[0][:, 0:DEPTH * NM])
            dve.wait_ge(turned, 2)
            out_copy(vecT[:, 0:96], bank[1][:, 0:96])
            dve.wait_ge(turned, 3)
            out_copy(vecT[:, 96:136], bank[2][:, 0:40])
            dve.wait_ge(turned, 4)
            out_copy(craw, bank[3][:, 0:NQ * DC])
            dve.wait_ge(turned_out, 4)
            lam = vec("lam")
            k0, k1 = kdec[:, 0, :], kdec[:, 1, :]
            z, z2 = small[:, 0:DC], small[:, DC:2 * DC]
            own(dve.tensor_scalar(z, lam, -1.0, None, ALU.mult))
            tt(z, z, lam, ALU.min)
            dve.tensor_copy(small2[:, 0:DC], z).then_inc(lam_exp, 1)
            dve.wait_ge(lam_exp, 2)
            own(dve.tensor_scalar(z2, small2[:, DC:2 * DC], 2.0, None, ALU.add))
            own(dve.reciprocal(z2, z2))
            tt(z, small2[:, DC:2 * DC], z2, ALU.mult)
            tt(z2, z, z, ALU.mult)
            own(dve.tensor_scalar(k0, z2, 1.0 / 19, 1.0 / 17, ALU.mult, ALU.add))
            for d in (15, 13, 11, 9, 7, 5, 3, 1):
                tt(k0, k0, z2, ALU.mult)
                own(dve.tensor_scalar(k0, k0, 1.0 / d, None, ALU.add))
            tt(k0, k0, z, ALU.mult)
            own(dve.tensor_scalar(z2, lam, -1.0, 0.0, ALU.mult, ALU.max))
            own(dve.scalar_tensor_tensor(k0, k0, 2.0, z2, ALU.mult, ALU.add))
            own(dve.tensor_scalar(k0, k0, -LRU_C / 2, None, ALU.mult))
            dve.tensor_scalar(k1, k0, 2.0, None, ALU.mult)
            dve.tensor_scalar(half_b[:, 0, :], vec("b_a"), 0.5, None, ALU.mult)
            dve.tensor_scalar(half_b[:, 1, :], vec("b_i"), 0.5, None, ALU.mult)
            dve.wait_ge(pool_step, 5)
            own(dve.tensor_copy(invcnt[:, :], iota_e[:, 0:16]))
            own(dve.tensor_scalar(invcnt[:, :], invcnt[:, :], 1.0, None, ALU.add))
            own(dve.reciprocal(invcnt[:, :], invcnt[:, :]))

            def mod_out(l, r):
                n = l * MOD_ROT + r
                m0, m1 = r * RING * 4, (r + 1) * RING * 4
                dve.wait_ge(mod_done, n + 1)
                dve.tensor_tensor(modT[:, m0:m1, :], bank[7][:, 0:RING * 4 * NQ].rearrange("p (m n) -> p m n", n=NQ),
                                  spread(bmodT[:, l * NM + m0:l * NM + m1], NQ), ALU.add).then_inc(mod_evicted, 1)
                dve.wait_ge(mod_evicted, n + 1)

            def adaln(l, which):
                m0 = 3 * DC * which
                g = spread(vecT[:, (2 * l + which) * DC:(2 * l + which + 1) * DC], NQ)
                own(dve.scalar_tensor_tensor(gainT[:, l, which], modT[:, m0 + DC:m0 + 2 * DC, :], 1.0, g,
                                             ALU.add, ALU.mult))
                own(dve.tensor_copy(shiftT[:, l, which], modT[:, m0:m0 + DC, :]))
                own(dve.tensor_copy(gateT[:, l, which], modT[:, m0 + 2 * DC:m0 + 3 * DC, :]))
                if l == 0 and which == 0:
                    tt(gateT[:, 0, 0], gateT[:, 0, 0], spread(vec("pool_scale"), NQ), ALU.mult)
                if l == 1 and which == 0:
                    tt(gbT[:, :, :], gateT[:, 1, 0], spread(vec("b_out"), NQ), ALU.mult)

            mod_out(0, 0)
            for g in range(2):
                dve.wait_ge(turned, 5 + g)
                out_copy(poolT[:, 4 * g:4 * g + 4, :], bank[g][:, 0:4 * NB * PB].rearrange("p (c r) -> p c r", c=4))
            dve.wait_ge(turned, 7)
            out_copy(convT[:, :, :], bank[2][:, 0:DC * NB * CH].rearrange("p (c r) -> p c r", c=DC))
            dve.wait_ge(turned, 8)
            out_copy(h0T[:, :, :], bank[3][:, 0:DC * NB].rearrange("p (c r) -> p c r", c=DC))
            for c in range(DC):
                dve.wait_ge(turned, 9 + c)
                out_copy(xT[:, c, 0:S], bank[c % 4][:, :])
            dve.wait_ge(turned, 9 + DC)
            out_copy(xT[:, :, S:T], bank[0][:, 0:DC * NS].rearrange("p (c t) -> p c t", c=DC))
            adaln(0, 0)
            stage_end(dve, "dve")

            def seqs(a):
                return a.rearrange("p c (b s) -> p c b s", b=NB)

            def norm(n, layer, which):
                for c in range(1, DC):
                    dve.wait_ge(sq_ready, n * DC + c + 1)
                    if c < DC - 1:
                        tt(hT[:, 0, :], hT[:, 0, :], hT[:, c, :], ALU.add)
                    else:
                        dve.tensor_tensor(hT[:, 0, :], hT[:, 0, :], hT[:, c, :], ALU.add).then_inc(sq_summed, 1)
                for h in range(2):
                    dve.wait_ge(std_ready, 2 * n + h + 1)
                    own(dve.reciprocal(rstd[:, h * H2:(h + 1) * H2], rstd[:, h * H2:(h + 1) * H2]))
                for c in range(DC):
                    dve.tensor_tensor(hT[:, c, :], xT[:, c, :], rstd, ALU.mult).then_inc(normed, 1)
                dve.wait_ge(normed, (n + 1) * DC)
                h = seqs(hT[:, :, S:T])
                tt(h, h, spread(gainT[:, layer, which, :, 1:NQ], SS), ALU.mult)
                tt(h, h, spread(shiftT[:, layer, which, :, 1:NQ], SS), ALU.add)
                if n == 2:
                    mod_out(1, 1)
                    adaln(1, 1)
                stage_end(dve, "dve")

            def add_samples(src, layer, which):
                t = small[:, :].rearrange("p (c t) -> p c t", c=DC)
                tt(seqs(t), seqs(src), spread(gateT[:, layer, which, :, 1:NQ], SS), ALU.mult)
                tt(xT[:, :, S:T], xT[:, :, S:T], t, ALU.add)

            def pool_mix():
                for g, w in enumerate(POOL_WINDOWS):
                    h = hT[:, 2 * g:2 * g + 2, 0:S]
                    src, dst, d = h, psum_a, 1
                    s_src, s_dst = spool_a, spool_b
                    dve.tensor_copy(spool_a[:, :, :, 0:PB],
                                    poolT[:, 2 * g:2 * g + 2, :].rearrange("p c (b r) -> p c b r", b=NB))
                    own(dve.tensor_copy(spool_a[:, :, :, PB:PB + SS], seqs(hT[:, 2 * g:2 * g + 2, S:T])))
                    while d < w:
                        dve.tensor_copy(dst[:, :, 0:d], src[:, :, 0:d])
                        dve.tensor_tensor(dst[:, :, d:S], src[:, :, d:S], src[:, :, 0:S - d], ALU.add)
                        tt(s_dst[:, :, :, 2 * d - 1:PB + SS], s_src[:, :, :, 2 * d - 1:PB + SS],
                           s_src[:, :, :, d - 1:PB + SS - d], ALU.add)
                        src, dst = dst, (psum_b if dst is psum_a else psum_a)
                        s_src, s_dst = s_dst, s_src
                        d *= 2
                    out = pooledT[:, 2 * g:2 * g + 2, :]
                    cnt = invcnt[:, 0:w - 1].unsqueeze(1).to_broadcast([P, 2, w - 1])
                    tt(dst[:, :, 0:w - 1], src[:, :, 0:w - 1], cnt, ALU.mult)
                    dve.tensor_tensor(out[:, :, 0:w - 1], dst[:, :, 0:w - 1], h[:, :, 0:w - 1], ALU.subtract)
                    dve.scalar_tensor_tensor(out[:, :, w - 1:S], src[:, :, w - 1:S], 1.0 / w, h[:, :, w - 1:S],
                                             ALU.mult, ALU.subtract)
                    own(dve.tensor_scalar(s_dst[:, :, :, PB:PB + SS], s_src[:, :, :, PB:PB + SS], 1.0 / w, None, ALU.mult))
                    dve.tensor_tensor(seqs(out[:, :, S:T]), s_dst[:, :, :, PB:PB + SS],
                                      seqs(hT[:, 2 * g:2 * g + 2, S:T]), ALU.subtract).then_inc(pooled_ready, 1)
                    dve.wait_ge(pooled_ready, g + 1)
                mod_out(0, 1)
                adaln(0, 1)
                for i in range(DC):
                    dve.wait_ge(mixed, i + 1)
                    dve.scalar_tensor_tensor(xT[:, i, 0:S], bank[i % 2][:, :], gateT[:, 0, 0, i, 0:1], xT[:, i, 0:S],
                                             ALU.mult, ALU.add).then_inc(mixed_added, 1)
                add_samples(bank[2][:, 0:DC * NS].rearrange("p (c t) -> p c t", c=DC), 0, 0)
                stage_end(dve, "dve")

            def first_max(out, vals, n, shape):
                rows_n = shape
                top = tmp_b[:, 0:rows_n]
                own(dve.tensor_reduce(top, vals, AX, ALU.max))
                tt(out, vals, spread(top, n), ALU.is_ge)
                it = iota_e[:, 0:n].unsqueeze(1).to_broadcast([P, rows_n, n])
                own(dve.scalar_tensor_tensor(out, out, -64.0, it, ALU.mult, ALU.add))
                own(dve.tensor_reduce(top, out, AX, ALU.min))
                tt(out, out, spread(top, n), ALU.is_equal)

            def last_rows(r):
                for j in range(NT + 2):
                    if j < NT:
                        w = TW[j]
                        dve.wait_ge(r["y_scaled"], j + 1)
                        dve.scalar_tensor_tensor(yl[j][0][0:w, :], yl[j][1][0:w, :], wts[0:w, 1, j:j + 1],
                                                 yl[j][0][0:w, :], ALU.mult, ALU.add).then_inc(r["y_summed"], 1)
                    if 1 <= j < NT + 1:
                        i, w = j - 1, TW[j - 1]
                        dve.wait_ge(last_gated, i + 1)
                        dve.tensor_tensor(yl[i][0][0:w, :], yl[i][0][0:w, :], x_last[i][0:w, :], ALU.add).then_inc(last_x, 1)
                    if j >= 2:
                        i, w = j - 2, TW[j - 2]
                        dve.wait_ge(last_std, i + 1)
                        own(dve.reciprocal(small2[0:w, i:i + 1], small2[0:w, i:i + 1]))
                        dve.scalar_tensor_tensor(yl[i][0][0:w, :], yl[i][0][0:w, :], small2[0:w, i:i + 1],
                                                 final_row[0:w, :], ALU.mult, ALU.mult).then_inc(y_ready, 1)

            def moe(l):
                r, q = rt[l], ts
                if l == 1:
                    dve.tensor_copy(gate_cols[:, :, 0:1], gateT[:, 1, 1, :, 0:1])
                    own(dve.tensor_copy(seqs(gate_cols[:, :, 1:NS + 1]), spread(gateT[:, 1, 1, :, 1:NQ], SS)))
                    dve.drain().then_inc(gate_cols_ready, 1)
                own(dve.memset(lg, 0.0))
                dve.wait_ge(r["logits"], 1)
                own(dve.tensor_copy(lg[:, 0:NPT, :], bank[4][:, 0:NPT * NE].rearrange("p (j e) -> p j e", j=NPT)))
                own(dve.tensor_copy(lg[0:TW[-1], NPT, :], bank[4][0:TW[-1], NPT * NE:NT * NE]))
                own(dve.tensor_reduce(tmp_b[:, 0:NT], lg, AX, ALU.max))
                dve.tensor_tensor(lg, lg, spread(tmp_b[:, 0:NT], NE), ALU.subtract).then_inc(r["lmax"], 1)
                dve.wait_ge(r["ex"], 1)
                own(dve.tensor_reduce(tmp_b[:, 0:NT], ex, AX, ALU.add))
                own(dve.reciprocal(tmp_b[:, 0:NT], tmp_b[:, 0:NT]))
                tt(ex, ex, spread(tmp_b[:, 0:NT], NE), ALU.mult)
                tt(sel, ex, rb[:, :].unsqueeze(1).to_broadcast([P, NT, NE]), ALU.add)
                s4 = sel.rearrange("p j (g e) -> p (j g) e", g=NG)
                hi, lo = [x.rearrange("p j (g e) -> p (j g) e", g=NG) for x in (val_a, val_b)]
                tt(hi[:, :, 0:2], s4[:, :, 0:2], s4[:, :, 2:4], ALU.max)
                tt(lo[:, :, 0:2], s4[:, :, 0:2], s4[:, :, 2:4], ALU.min)
                tt(hi[:, :, 2:3], hi[:, :, 0:1], hi[:, :, 1:2], ALU.max)
                tt(hi[:, :, 3:4], hi[:, :, 0:1], hi[:, :, 1:2], ALU.min)
                tt(lo[:, :, 2:3], lo[:, :, 0:1], lo[:, :, 1:2], ALU.max)
                tt(lo[:, :, 3:4], lo[:, :, 2:3], hi[:, :, 3:4], ALU.max)
                gs = gsc.rearrange("p j g -> p (j g)")
                tt(gs.unsqueeze(2), lo[:, :, 3:4], hi[:, :, 2:3], ALU.add)
                first_max(gbest, gsc, NG, NT)
                own(dve.tensor_scalar(gbest, gbest, BIG, -BIG, ALU.mult, ALU.add))
                tt(s4, s4, spread(gbest.rearrange("p j g -> p (j g)"), EG), ALU.add)
                first_max(one, sel, NE, NT)
                own(dve.scalar_tensor_tensor(sel, one, -3 * BIG, sel, ALU.mult, ALU.add))
                first_max(two, sel, NE, NT)
                picked, vals, in_places = (route[:, n:n + 2].rearrange("p n j e -> p n (j e)") for n in (3, 5, 1))
                both = lambda a: a.rearrange("p n (j e) -> p (n j) e", e=NE)
                twice = lambda a: a.rearrange("p j e -> p (j e)").unsqueeze(1).to_broadcast([P, 2, NT * NE])
                tt(vals, picked, twice(ex), ALU.mult)
                own(dve.tensor_reduce(wts[:, :, :].rearrange("p n j -> p (n j)"), both(vals), AX, ALU.add))
                tt(tmp_b[:, 0:NT], wts[:, 0, :], wts[:, 1, :], ALU.add)
                own(dve.reciprocal(tmp_b[:, 0:NT], tmp_b[:, 0:NT]))
                for k in range(2):
                    tt(wts[:, k, :], wts[:, k, :], tmp_b[:, 0:NT], ALU.mult)
                tt(val_a, one, two, ALU.add)
                dve.tensor_tensor(picks[:, :, :], val_a, spread(valid[:, :], NE), ALU.mult).then_inc(r["count_in"], 1)
                dve.wait_ge(r["counts"], 1)
                own(dve.tensor_copy(sel, bank[3][:, 0:NT * NE].rearrange("p (j e) -> p j e", j=NT)))
                own(dve.tensor_copy(cnt_e, bank[3][:, NT * NE:(NT + 1) * NE]))
                own(dve.tensor_scalar(ov_e, cnt_e, float(P), None, ALU.is_gt))
                for k in range(2, (T + P - 1) // P):
                    own(dve.tensor_scalar(cum_e, cnt_e, float(k * P), None, ALU.is_gt))
                    tt(ov_e, ov_e, cum_e, ALU.add)
                own(dve.tensor_scalar(cnt_e, cnt_e, 0.0, 1.0, ALU.mult, ALU.add))
                own(dve.tensor_tensor_scan(cum_e, cnt_e, ov_e, 0.0, ALU.mult, ALU.add))
                tt(end_e, cum_e, ov_e, ALU.subtract)
                tt(end_e, end_e, iota_e[:, :], ALU.subtract)
                own(dve.tensor_scalar(end_e, end_e, float(NE - 1), float(P), ALU.add, ALU.mult))
                own(dve.tensor_scalar(val_a, sel, float(P), None, ALU.is_ge))
                tt(val_a, val_a, end_e.unsqueeze(1).to_broadcast([P, NT, NE]), ALU.mult)
                tt(val_a, val_a, sel, ALU.add)
                own(dve.tensor_scalar(end_e, iota_e[:, :], float(P), None, ALU.mult))
                tt(val_a, val_a, end_e.unsqueeze(1).to_broadcast([P, NT, NE]), ALU.add)
                tt(in_places, picked, twice(val_a), ALU.mult)
                own(dve.tensor_reduce(slot_f, both(in_places), AX, ALU.add))
                tt(reached, spread(slot_f, NL + 1), tile_at[:, :].unsqueeze(1).to_broadcast([P, 2 * NT, NL + 1]), ALU.is_ge)
                own(dve.tensor_reduce(tile_of, reached[:, :, 0:NL], AX, ALU.add))
                own(dve.scalar_tensor_tensor(place_of, tile_of, -float(P), slot_f, ALU.mult, ALU.add))
                dve.wait_ge(r["places"], 1)
                dve.tensor_tensor(place_1h, spread(place_of, P), place_row.unsqueeze(1).to_broadcast([P, 2 * NT, P]),
                                  ALU.is_equal)
                tt(rowof, reached[:, :, 0:NL], reached[:, :, 1:NL + 1], ALU.subtract)
                tt(rowof, rowof, spread(row_number[:, :], NL), ALU.mult)
                dve.drain().then_inc(r["list_in"], 1)
                dve.wait_ge(r["list_out"], 1)
                own(dve.tensor_scalar(lt_g, bank[2][:, 0:NL], 0.0, float(NOWHERE + 1), ALU.is_le, ALU.mult))
                own(dve.scalar_tensor_tensor(lt_f, bank[2][:, 0:NL], -1.0, lt_g, ALU.add, ALU.add))
                own(dve.tensor_copy(yrow[:, :], lt_f))
                own(dve.tensor_scalar(lt_g, lt_f, float(T), float(-T), ALU.is_ge, ALU.mult))
                tt(lt_f, lt_f, lt_g, ALU.add)
                own(dve.tensor_copy(tokl[:, :], lt_f))
                dve.drain().then_inc(r["list_ready"], 1)
                tt(ov_le, cum_e.unsqueeze(1).to_broadcast([P, NOV, NE]), spread(iota_e[:, 0:NOV], NE), ALU.is_le)
                own(dve.tensor_reduce(ov_f[:, 0:NOV], ov_le, AX, ALU.add))
                own(dve.tensor_copy(ov_f[:, NOV:NOV + 1], cum_e[:, NE - 1:NE]))
                own(dve.tensor_copy(ovinfo[:, :], ov_f[0:1, :]))
                dve.drain().then_inc(r["list_ready"], 1)
                if l == 0:
                    mod_out(1, 0)
                    adaln(1, 0)
                stage_end(dve, "dve")

                def xe_copy(q, b, n, used):
                    dve.wait_ge(q["tx_done"], n + 1)
                    used()
                    dve.tensor_copy(xe[b][:, 4:8, :], bank[5][:, :].rearrange("p (c t) -> p c t", c=4)
                                    ).then_inc(q["xe_copied"], 1)

                def tile(q, b, n, first, x_next, ys_free):
                    x_next()
                    dve.wait_ge(q["silu_done"], n + 1)
                    dve.wait_ge(q["u_done"], n + 1)
                    if not first:
                        dve.wait_ge(q["th_done"], n - 1)
                    dve.tensor_tensor(hid[b], sg[b], bank[1][:, :], ALU.mult).then_inc(q["hid_done"], 1)
                    dve.wait_ge(q["th_done"], n + 1)
                    if not first:
                        dve.wait_ge(q["y_done"], n * 2 - 2)
                    dve.tensor_copy(hidT[b][:, 2:4, :], bank[7][:, 0:2 * P].rearrange("p (c t) -> p c t", c=2)
                                    ).then_inc(q["ht_copied"], 1)
                    dve.wait_ge(q["y_done"], n * 2 + 2)
                    ys_free()
                    dve.tensor_copy(ys[b][:, HALF:D], bank[3][:, :]).then_inc(q["ys_copied"], 1)

                def step(it, b, first=False, last=False):
                    t = it * 2 + (b + NE * l)
                    nb = 1 - b

                    def x_next():
                        if not last:
                            xe_copy(q, nb, t + 1, lambda: None if first and b == 0 else dve.wait_ge(q["u_done"], t))

                    tile(q, b, t, first, x_next,
                         lambda: None if first else dve.wait_ge(q[f"scattered{b}"], it * 16 + l * (NE * 8)))

                xe_copy(q, 0, NE * l, lambda: None)
                step(0, 0, first=True)
                step(0, 1, first=True)
                with dve.Fori(1, NE // 2 - 1) as it:
                    step(it, 0)
                    step(it, 1)
                step(NE // 2 - 1, 0)
                step(NE // 2 - 1, 1, last=True)
                o = ov[l]
                n_ov = dve.value_load(ovinfo[0:1, NOV:NOV + 1], min_val=0, max_val=NOV)
                with dve.If(n_ov > 0):
                    with dve.Fori(0, n_ov) as i:
                        xe_copy(o, 0, i, lambda: None)
                        tile(o, 0, i, True, lambda: None, lambda: None)
                stage_end(dve, "dve")
                if l == 1:
                    last_rows(r)
                    return
                def add_tile(j):
                    w = TW[j]
                    dve.wait_ge(r["y_turned"], j + 1)
                    bks = [bank[2 * (j % 2) + h][:, :].rearrange("p (c t) -> p c t", c=4) for h in range(2)]
                    if w == P:
                        for c in range(DC):
                            ins = dve.scalar_tensor_tensor(xT[:, c, j * P:(j + 1) * P], bks[c // 4][:, c % 4, :],
                                                           gateT[:, l, 1, c, 0:1], xT[:, c, j * P:(j + 1) * P],
                                                           ALU.mult, ALU.add)
                        ins.then_inc(r["y_added"], 1)
                    else:
                        s2 = small2[:, :].rearrange("p (c t) -> p c t", c=DC)
                        for h in range(2):
                            own(dve.tensor_copy(s2[:, 4 * h:4 * h + 4, :], bks[h][:, :, 0:w]))
                        add_samples(s2, l, 1)

                for j in range(NT):
                    w = TW[j]
                    dve.wait_ge(r["y_scaled"], j + 1)
                    dve.scalar_tensor_tensor(ysum_c[j % 2][0:w, :], yl[j][1][0:w, :], wts[0:w, 1, j:j + 1],
                                             ysum_c[j % 2][0:w, :], ALU.mult, ALU.add).then_inc(r["y_summed"], 1)
                    if j >= 1:
                        add_tile(j - 1)
                add_tile(NT - 1)
                stage_end(dve, "dve")

            def lru():
                xs = [small[:, :].rearrange("p (c t) -> p c t", c=DC), small2[:, :].rearrange("p (c t) -> p c t", c=DC)]
                dve.memset(xb[:, :, 0:CH], 0.0)
                own(dve.tensor_copy(xbs[:, :, :, 0:CH], convT[:, :, :].rearrange("p c (b r) -> p c b r", b=NB)))
                for m in range(DC):
                    dve.wait_ge(x_out, m + 1)
                    own(dve.tensor_scalar(xcT[:, m, 0:S], xb[:, m, 0:S], vec("cw0", m), vec("conv_b", m), ALU.mult, ALU.add))
                    for k in range(1, CW):
                        ins = dve.scalar_tensor_tensor(xcT[:, m, 0:S], xb[:, m, k:k + S], vec(f"cw{k}", m),
                                                       xcT[:, m, 0:S], ALU.mult, ALU.add)
                        own(ins)
                xc_s = seqs(xcT[:, :, S:T])
                t_s = seqs(xs[0])
                tt(xc_s, xbs[:, :, :, 0:SS], spread(spread(vec("cw0"), NB), SS), ALU.mult)
                for k in range(1, CW):
                    tt(t_s, xbs[:, :, :, k:k + SS], spread(spread(vec(f"cw{k}"), NB), SS), ALU.mult)
                    tt(xc_s, xc_s, t_s, ALU.add)
                tt(xcT[:, :, S:T], xcT[:, :, S:T], spread(vec("conv_b"), NS), ALU.add)
                own(dve.tensor_copy(conv_tail[:, :, 0:CH], xb[:, :, S:S + CH]))
                own(dve.tensor_copy(conv_tail[:, :, CH:CH * NQ].rearrange("p c (b r) -> p c b r", b=NB),
                                    xbs[:, :, :, SS:SS + CH]))
                dve.drain().then_inc(conv_done, 1)
                for i in range(DC):
                    g = i // BC
                    dve.wait_ge(gates_done, BC * (g + 1))
                    dve.wait_ge(gates_read, i + 1)
                    dve.scalar_tensor_tensor(xcT[:, i, :], tanh_i[i % 2], 1.0, xcT[:, i, :], ALU.add, ALU.mult
                                             ).then_inc(mult_done, 1)
                    dve.wait_ge(a_ready, i + 1)
                    dve.tensor_scalar(e2[:, i, :], e2[:, i, :], 1.0, -0.25, ALU.min, ALU.mult).then_inc(power_ready, 1)
                dve.wait_ge(mult_done, DC)
                for i in range(DC):
                    dve.wait_ge(root_ready, i + 1)
                    own(dve.memset(e2[:, i, 0:1], 0.5))
                    tt(xcT[:, i, :], xcT[:, i, :], e2[:, i, :], ALU.mult)
                    own(dve.tensor_tensor_scan(e2[:, i, 0:S], aT[:, i, 0:S], xcT[:, i, 0:S], 0.0, ALU.mult, ALU.add))
                    own(dve.tensor_copy(h_tail[:, i, 0:1], e2[:, i, S - 1:S]))
                    dve.wait_ge(x_out, DC + i + 1)
                    dve.tensor_tensor(ybT[:, i, 0:S], e2[:, i, 0:S], ybT[:, i, 0:S], ALU.mult).then_inc(z_ready, 1)
                a_s, b_s = seqs(aT[:, :, S:T]), seqs(xcT[:, :, S:T])
                prev = h0T[:, :, :]
                for s in range(SS):
                    cur = seqs(xs[1])[:, :, :, s]
                    tt(cur, a_s[:, :, :, s], prev, ALU.mult)
                    tt(cur, cur, b_s[:, :, :, s], ALU.add)
                    prev = cur
                own(dve.tensor_copy(h_tail[:, :, 1:NQ], prev))
                dve.tensor_tensor(ybT[:, :, S:T], xs[1], ybT[:, :, S:T], ALU.mult).then_inc(z_ready, 1)
                dve.drain().then_inc(tails_ready, 1)
                for i in range(2 * DC):
                    h, m = i // DC, i % DC
                    at = slice(h * H2, min(S, (h + 1) * H2))
                    dve.wait_ge(o_out, i + 1)
                    dve.tensor_tensor(xT[:, m, at], xT[:, m, at], tanh_i[i % 2][:, 0:at.stop - at.start], ALU.add
                                      ).then_inc(o_added, 1)
                add_samples(xs[1], 1, 0)
                tt(seqs(xT[:, :, S:T]), seqs(xT[:, :, S:T]), spread(gbT[:, :, 1:NQ], SS), ALU.add)
                stage_end(dve, "dve")

            norm(0, 0, 0)
            pool_mix()
            norm(1, 0, 1)
            moe(0)
            norm(2, 1, 0)
            lru()
            norm(3, 1, 1)
            moe(1)

        @block.gpsimd
        def _(pool):
            def own(ins):
                own.n += 1
                ins.then_inc(pool_step, 1)
                pool.wait_ge(pool_step, own.n)
            own.n = 0
            own(pool.memset(ident[:, :], 0.0))
            own(pool.affine_select(ident[:, :], ident[:, :], [[-1, P]], ALU.not_equal, 1.0, base=0, channel_multiplier=1))
            own(pool.memset(before_b[:, :], 1.0))
            own(pool.affine_select(before_b[:, :], before_b[:, :], [[1, P]], ALU.is_gt, 0.0, base=0, channel_multiplier=-1))
            own(pool.iota(iota_e[:, :], [[1, NE]], base=0, channel_multiplier=0, allow_small_or_imprecise_dtypes=True))
            own(pool.iota(row_number[:, 0:NT], [[P, NT]], base=1, channel_multiplier=1, allow_small_or_imprecise_dtypes=True))
            own(pool.iota(row_number[:, NT:2 * NT], [[P, NT]], base=T + 1, channel_multiplier=1,
                          allow_small_or_imprecise_dtypes=True))
            own(pool.iota(tile_at[:, :], [[P, NL + 1]], base=0, channel_multiplier=0, allow_small_or_imprecise_dtypes=True))
            pool.wait_ge(vec_step, 1)
            own(pool.affine_select(valid[:, :], valid[:, :], [[-P, NT]], ALU.is_gt, 0.0, base=T, channel_multiplier=-1))
            stage_end(pool, "pool")

            def moe(l):
                r, q = rt[l], ts
                pool.iota(place_row, [[1, P]], base=-P, channel_multiplier=0,
                          allow_small_or_imprecise_dtypes=True).then_inc(r["places"], 1)
                for b in range(2):
                    own(pool.memset(xg[b], 0.0))
                pool.wait_ge(r["list_ready"], 1)
                for b in range(2):
                    pool.wait_ge(r[f"rows_stored{b}"], 16 * ((NT + 1 - b) // 2))

                def gather(q, b, n, t):
                    pool.tensor_copy(toks[b][:, :], tokl[:, bass.ds(t, 1)]).then_inc(q["toks_ready"], 1)
                    pool.wait_ge(q["toks_ready"], n + 1)
                    pool.sem_inc(waits_seen, 1)
                    pool.indirect_dma_start(xg[b], None, h_rows[l], bass.IndirectOffsetOnAxis(toks[b][:, :], 0),
                                            bounds_check=T - 1, oob_is_err=False).then_inc(q[f"gathered{b}"], 16)

                def scatter(q, b, n, t):
                    pool.tensor_copy(yrows[b][:, :], yrow[:, bass.ds(t, 1)]).then_inc(q["yrows_ready"], 1)
                    pool.wait_ge(q["yrows_ready"], n + 1)
                    pool.wait_ge(q["ys_copied"], n * 2 + 2)
                    pool.sem_inc(waits_seen, 1)
                    pool.indirect_dma_start(y_rows[l], bass.IndirectOffsetOnAxis(yrows[b][:, :], 0), ys[b], None,
                                            bounds_check=2 * T - 1, oob_is_err=False).then_inc(q[f"scattered{b}"], 16)

                def step(it, b, first=False, last=False):
                    t = it * 2 + b
                    n = it * 2 + (b + NE * l)
                    if not last:
                        pool.wait_ge(q["tx_done"], n + 1)
                        gather(q, b, n + 2, t + 2)
                    if not first:
                        pool.wait_ge(q[f"scattered{b}"], it * 16 + l * (NE * 8))
                    scatter(q, b, n, t)

                gather(q, 0, NE * l, 0)
                gather(q, 1, NE * l + 1, 1)
                stage_end(pool, "pool")
                step(0, 0, first=True)
                step(0, 1, first=True)
                with pool.Fori(1, NE // 2 - 1) as it:
                    step(it, 0)
                    step(it, 1)
                step(NE // 2 - 1, 0, last=True)
                step(NE // 2 - 1, 1, last=True)
                for b in range(2):
                    pool.wait_ge(q[f"scattered{b}"], (l + 1) * (NE * 8))
                o = ov[l]
                n_ov = pool.value_load(ovinfo[0:1, NOV:NOV + 1], min_val=0, max_val=NOV)
                with pool.If(n_ov > 0):
                    with pool.Fori(0, n_ov) as i:
                        gather(o, 0, i, i + NE)
                        scatter(o, 0, i, i + NE)
                        pool.wait_ge(o["scattered0"], (i + 1) * 16)
                stage_end(pool, "pool")
                if l == 0:
                    stage_end(pool, "pool")
                    return
                pool.wait_ge(last_loaded, 16 * 5)
                for j in range(NT):
                    w = TW[j]
                    pool.wait_ge(r["y_summed"], j + 1)
                    pool.tensor_tensor(yl[j][0][0:w, :], yl[j][0][0:w, :], gate_last[j][0:w, :], ALU.mult
                                       ).then_inc(last_gated, 1)

            stage_end(pool, "pool")
            stage_end(pool, "pool")
            stage_end(pool, "pool")
            moe(0)
            stage_end(pool, "pool")
            stage_end(pool, "pool")
            stage_end(pool, "pool")
            moe(1)


_INS = ['x_prompt', 'x_sample', 'c_prompt', 'c_sample', 'state_pool_buf', 'state_conv_buf', 'state_lru_h',
        'w_mod', 'b_mod', 'norm_g', 'pool_w', 'pool_scale', 'lru_w_x', 'lru_b_x', 'lru_w_y', 'lru_b_y',
        'conv_w', 'conv_b', 'lru_w_a', 'lru_b_a', 'lru_w_i', 'lru_b_i', 'lru_lambda', 'lru_w_out', 'lru_b_out',
        'router_w', 'router_b', 'moe_w_gate', 'moe_w_up', 'moe_w_down', 'final_g']
_OUTS = [(1, 512, 1024), (8, 4, 1024), (1, 1, 15, 1024), (1, 8, 15, 1024), (1, 1, 3, 1024), (1, 8, 3, 1024),
         (1, 1, 1024), (1, 8, 1024)]


def kernel(**inputs):
    import numpy as _np
    import concourse.bacc as _bacc
    from concourse import mybir as _mybir
    from concourse.bass_utils import run_bass_kernel_spmd as _run

    nc = _bacc.Bacc("TRN2", target_bir_lowering=False, num_devices=1, dynamic_dma_scratch_size=8192)
    arrays, args = {}, []
    for name in _INS:
        a = _np.ascontiguousarray(inputs[name])
        arrays[f"in_{name}_dram"] = a
        args.append(nc.dram_tensor(f"in_{name}_dram", a.shape, _mybir.dt.from_np(a.dtype), kind="ExternalInput").ap())
    for i, shape in enumerate(_OUTS):
        args.append(nc.dram_tensor(f"out_{i}_dram", shape, _mybir.dt.float32, kind="ExternalOutput").ap())
    hybrid_trunk_kernel(nc, *args)
    r = _run(nc, [arrays], core_ids=[0])
    return tuple(r.results[0][f"out_{i}_dram"] for i in range(len(_OUTS)))
```
